# Optimizing a Trainium2 kernel written in Bass

```python
import math
import jax, jax.numpy as jnp
from jax import lax
import numpy as np

D_MODEL = 1024
BATCH = 1
SEQ = 256
DEPTH = 2

HEAD_DIM = 64
MIX_WIDTH = D_MODEL
DIFF_WIDTH = MIX_WIDTH // 2
MOBA_WIDTH = MIX_WIDTH - DIFF_WIDTH
DIFF_HEADS = DIFF_WIDTH // (2 * HEAD_DIM)
DIFF_V_DIM = 2 * HEAD_DIM
MOBA_HEADS = MOBA_WIDTH // HEAD_DIM
PROJ_WIDTH = 3 * DIFF_WIDTH + 3 * MOBA_WIDTH
N_BIAS_HEADS = DIFF_HEADS + MOBA_HEADS
D_FF = ((8 * D_MODEL // 3 + 127) // 128) * 128
CONV_WIDTH = 3
DIFF_Q_BLOCK = 128
MOBA_BLOCK = 256
MOBA_TOPK = 3
MOBA_Q_CHUNK = 64
REL_BUCKETS = 32
REL_MAX_EXACT = REL_BUCKETS // 2
REL_MAX_DISTANCE = 1024
NORM_EPS = 1e-6


def rms_norm(x, g):
    xf = x.astype(jnp.float32)
    y = xf * lax.rsqrt(jnp.mean(xf * xf, axis=-1, keepdims=True) + NORM_EPS)
    return (y * g).astype(x.dtype)

def rel_bucket(dist):
    n = jnp.maximum(dist, 0)
    nf = jnp.maximum(n, REL_MAX_EXACT).astype(jnp.float32)
    large = REL_MAX_EXACT + (jnp.log(nf / REL_MAX_EXACT) / math.log(REL_MAX_DISTANCE / REL_MAX_EXACT)
                             * (REL_BUCKETS - REL_MAX_EXACT)).astype(jnp.int32)
    large = jnp.minimum(large, REL_BUCKETS - 1)
    return jnp.where(n < REL_MAX_EXACT, n, large)

def diff_attention(q, k, v, lam, lam_init, sub_g, bias_tab):
    B, S, H = q.shape[:3]
    nqb = S // DIFF_Q_BLOCK
    qb = q.reshape(B, nqb, DIFF_Q_BLOCK, H, 2, HEAD_DIM).transpose(1, 0, 2, 3, 4, 5)
    kpos = jnp.arange(S)
    scale = HEAD_DIM ** -0.5

    def block(args):
        qblk, i = args
        qpos = i * DIFF_Q_BLOCK + jnp.arange(DIFF_Q_BLOCK)
        dist = qpos[:, None] - kpos[None, :]
        bias = jnp.moveaxis(bias_tab[rel_bucket(dist)], -1, 0)
        logits = jnp.einsum('bqhmd,bkhmd->bmhqk', qblk, k).astype(jnp.float32) * scale + bias
        logits = jnp.where(dist >= 0, logits, -jnp.inf)
        p = jax.nn.softmax(logits, axis=-1)
        a = p[:, 0] - lam * p[:, 1]
        return jnp.einsum('bhqk,bkhe->bqhe', a.astype(v.dtype), v)

    out = lax.map(block, (qb, jnp.arange(nqb)))
    out = out.transpose(1, 0, 2, 3, 4).reshape(B, S, H, DIFF_V_DIM)
    out = rms_norm(out, sub_g) * (1.0 - lam_init)
    return out.reshape(B, S, H * DIFF_V_DIM)

def moba_attention(q, k, v, bias_tab):
    B, S, H, D = q.shape
    nb = -(-S // MOBA_BLOCK)
    pad = nb * MOBA_BLOCK - S
    padw = ((0, 0), (0, pad), (0, 0), (0, 0))
    kb = jnp.pad(k, padw).reshape(B, nb, MOBA_BLOCK, H, D).transpose(0, 3, 1, 2, 4)
    vb = jnp.pad(v, padw).reshape(B, nb, MOBA_BLOCK, H, D).transpose(0, 3, 1, 2, 4)
    kmean = jnp.mean(kb.astype(jnp.float32), axis=3)
    gate = jnp.einsum('bshd,bhnd->bhsn', q.astype(jnp.float32), kmean)
    past = jnp.arange(nb)[None, :] < (jnp.arange(S) // MOBA_BLOCK)[:, None]
    gate = jnp.where(past, gate, -jnp.inf)
    topk = min(MOBA_TOPK, nb)
    sel_score, sel_idx = lax.top_k(gate, topk)
    sel_valid = jnp.isfinite(sel_score)

    nc = S // MOBA_Q_CHUNK
    qc = q.reshape(B, nc, MOBA_Q_CHUNK, H, D).transpose(1, 0, 3, 2, 4)
    idx_c = sel_idx.reshape(B, H, nc, MOBA_Q_CHUNK, topk).transpose(2, 0, 1, 3, 4)
    val_c = sel_valid.reshape(B, H, nc, MOBA_Q_CHUNK, topk).transpose(2, 0, 1, 3, 4)
    bi = jnp.arange(B)[:, None, None, None]
    hi = jnp.arange(H)[None, :, None, None]
    hi5 = jnp.arange(H)[None, :, None, None, None]
    tab_h = bias_tab.T
    j = jnp.arange(MOBA_BLOCK)
    scale = D ** -0.5
    n_sel = topk * MOBA_BLOCK

    def chunk(args):
        qch, idx, valid, c = args
        qpos = c * MOBA_Q_CHUNK + jnp.arange(MOBA_Q_CHUNK)
        gk = kb[bi, hi, idx]
        gv = vb[bi, hi, idx]
        dist_p = qpos[None, None, :, None, None] - (idx[..., None] * MOBA_BLOCK + j)
        bias_p = tab_h[hi5, rel_bucket(dist_p)]
        lp = jnp.einsum('bhqd,bhqnjd->bhqnj', qch, gk).astype(jnp.float32) * scale + bias_p
        lp = jnp.where(valid[..., None], lp, -jnp.inf).reshape(B, H, MOBA_Q_CHUNK, n_sel)
        ob = (c * MOBA_Q_CHUNK) // MOBA_BLOCK
        ko = lax.dynamic_index_in_dim(kb, ob, axis=2, keepdims=False)
        vo = lax.dynamic_index_in_dim(vb, ob, axis=2, keepdims=False)
        dist_o = qpos[:, None] - (ob * MOBA_BLOCK + j)[None, :]
        bias_o = tab_h[:, rel_bucket(dist_o)]
        lo = jnp.einsum('bhqd,bhjd->bhqj', qch, ko).astype(jnp.float32) * scale + bias_o
        lo = jnp.where(dist_o >= 0, lo, -jnp.inf)
        p = jax.nn.softmax(jnp.concatenate([lp, lo], axis=-1), axis=-1).astype(v.dtype)
        pp = p[..., :n_sel].reshape(B, H, MOBA_Q_CHUNK, topk, MOBA_BLOCK)
        po = p[..., n_sel:]
        return (jnp.einsum('bhqnj,bhqnje->bhqe', pp, gv)
                + jnp.einsum('bhqj,bhje->bhqe', po, vo))

    out = lax.map(chunk, (qc, idx_c, val_c, jnp.arange(nc)))
    return out.transpose(1, 0, 3, 2, 4).reshape(B, S, H * D)

def causal_dwconv(u, w, b):
    C = u.shape[-1]
    y = lax.conv_general_dilated(u, w[:, None, :], window_strides=(1,),
                                 padding=[(CONV_WIDTH - 1, 0)],
                                 dimension_numbers=('NWC', 'WIO', 'NWC'),
                                 feature_group_count=C)
    return y + b

def conv_ffn(h, w_up, conv_w, conv_b, w_down):
    u = causal_dwconv(h @ w_up, conv_w, conv_b)
    g, up = jnp.split(u, 2, axis=-1)
    return (jax.nn.silu(g) * up) @ w_down

def first_inputs(seed: int = 0) -> dict:
    key = jax.random.key(seed)
    ks = jax.random.split(key, 14)
    f32 = jnp.float32
    nrm = lambda k, s: jax.random.normal(k, s, f32)
    resid = (2 * DEPTH) ** -0.5
    return {
        'x': nrm(ks[0], (BATCH, SEQ, D_MODEL)),
        'ln_attn_g': 1.0 + 0.02 * nrm(ks[1], (DEPTH, D_MODEL)),
        'w_in': nrm(ks[2], (DEPTH, D_MODEL, PROJ_WIDTH)) * D_MODEL ** -0.5,
        'qk_norm_g': 1.0 + 0.02 * nrm(ks[3], (DEPTH, 4, HEAD_DIM)),
        'diff_lambda': 0.1 * nrm(ks[4], (DEPTH, 4, HEAD_DIM)),
        'diff_subln_g': 1.0 + 0.02 * nrm(ks[5], (DEPTH, DIFF_V_DIM)),
        'w_out': nrm(ks[6], (DEPTH, MIX_WIDTH, D_MODEL)) * MIX_WIDTH ** -0.5 * resid,
        'ln_ffn_g': 1.0 + 0.02 * nrm(ks[7], (DEPTH, D_MODEL)),
        'w_up': nrm(ks[8], (DEPTH, D_MODEL, 2 * D_FF)) * D_MODEL ** -0.5,
        'conv_w': nrm(ks[9], (DEPTH, CONV_WIDTH, 2 * D_FF)) * CONV_WIDTH ** -0.5,
        'conv_b': 0.02 * nrm(ks[10], (DEPTH, 2 * D_FF)),
        'w_down': nrm(ks[11], (DEPTH, D_FF, D_MODEL)) * D_FF ** -0.5 * resid,
        'rel_bias': 0.5 * nrm(ks[12], (REL_BUCKETS, N_BIAS_HEADS)),
    }

def first_block(x, ln_attn_g, w_in, qk_norm_g, diff_lambda, diff_subln_g, w_out,
              ln_ffn_g, w_up, conv_w, conv_b, w_down, rel_bias):
    B, S = x.shape[:2]
    cuts = [DIFF_WIDTH, 2 * DIFF_WIDTH, 3 * DIFF_WIDTH,
            3 * DIFF_WIDTH + MOBA_WIDTH, 3 * DIFF_WIDTH + 2 * MOBA_WIDTH]
    bias_diff = rel_bias[:, :DIFF_HEADS]
    bias_moba = rel_bias[:, DIFF_HEADS:]
    for i in range(DEPTH):
        lam_init = 0.8 - 0.6 * math.exp(-0.3 * i)
        h = rms_norm(x, ln_attn_g[i])
        dq, dk, dv, mq, mk, mv = jnp.split(h @ w_in[i], cuts, axis=-1)
        dq = rms_norm(dq.reshape(B, S, DIFF_HEADS, 2, HEAD_DIM), qk_norm_g[i, 0])
        dk = rms_norm(dk.reshape(B, S, DIFF_HEADS, 2, HEAD_DIM), qk_norm_g[i, 1])
        dv = dv.reshape(B, S, DIFF_HEADS, DIFF_V_DIM)
        lf = diff_lambda[i].astype(jnp.float32)
        lam = jnp.exp(jnp.sum(lf[0] * lf[1])) - jnp.exp(jnp.sum(lf[2] * lf[3])) + lam_init
        y_diff = diff_attention(dq, dk, dv, lam, lam_init, diff_subln_g[i], bias_diff)
        mq = rms_norm(mq.reshape(B, S, MOBA_HEADS, HEAD_DIM), qk_norm_g[i, 2])
        mk = rms_norm(mk.reshape(B, S, MOBA_HEADS, HEAD_DIM), qk_norm_g[i, 3])
        mv = mv.reshape(B, S, MOBA_HEADS, HEAD_DIM)
        y_moba = moba_attention(mq, mk, mv, bias_moba)
        x = x + jnp.concatenate([y_diff, y_moba], axis=-1) @ w_out[i]
        x = x + conv_ffn(rms_norm(x, ln_ffn_g[i]), w_up[i], conv_w[i], conv_b[i], w_down[i])
    return x


N_HEADS = 8
HEAD_DIM_2 = 128
D_ATTN = N_HEADS * HEAD_DIM_2
Q_BLOCK = 128
FORGET_BIAS = 2.0
D_RNN = D_MODEL
N_RNN_BLOCKS = 16
RNN_BLOCK = D_RNN // N_RNN_BLOCKS
CONV_WIDTH_2 = 4
LRU_C = 8.0
D_FF_2 = 2816

SPLIT_POINTS = (
    D_ATTN,
    2 * D_ATTN,
    3 * D_ATTN,
    3 * D_ATTN + N_HEADS,
    3 * D_ATTN + N_HEADS + D_RNN,
    3 * D_ATTN + N_HEADS + 2 * D_RNN,
    3 * D_ATTN + N_HEADS + 2 * D_RNN + D_MODEL,
)
N_IN = 3 * D_ATTN + N_HEADS + 2 * D_RNN + 2 * D_MODEL


def rms_norm_2(x, g):
    xf = x.astype(jnp.float32)
    y = xf * lax.rsqrt(jnp.mean(xf * xf, axis=-1, keepdims=True) + NORM_EPS)
    return (y * g.astype(jnp.float32)).astype(x.dtype)

def swiglu(x, w_gate, w_up, w_down):
    return (jax.nn.silu(x @ w_gate) * (x @ w_up)) @ w_down

def forgetting_attention(q, k, v, log_f):
    B, S = q.shape[0], q.shape[1]
    nb = S // Q_BLOCK
    scale = HEAD_DIM_2 ** -0.5
    c = jnp.cumsum(log_f, axis=1).transpose(0, 2, 1)
    q = q.transpose(0, 2, 1, 3)
    k = k.transpose(0, 2, 1, 3)
    v = v.transpose(0, 2, 1, 3)
    qb = q.reshape(B, N_HEADS, nb, Q_BLOCK, HEAD_DIM_2).transpose(2, 0, 1, 3, 4)
    cb = c.reshape(B, N_HEADS, nb, Q_BLOCK).transpose(2, 0, 1, 3)
    k_pos = jnp.arange(S)

    def one_block(args):
        q_i, c_i, i = args
        s = jnp.einsum('bhqd,bhkd->bhqk', q_i, k).astype(jnp.float32) * scale
        s = s + (c_i[..., :, None] - c[:, :, None, :])
        q_pos = i * Q_BLOCK + jnp.arange(Q_BLOCK)
        mask = k_pos[None, :] <= q_pos[:, None]
        s = jnp.where(mask, s, -jnp.inf)
        p = jax.nn.softmax(s, axis=-1)
        return jnp.einsum('bhqk,bhkd->bhqd', p.astype(v.dtype), v)

    out = lax.map(one_block, (qb, cb, jnp.arange(nb)))
    return out.transpose(1, 0, 3, 2, 4).reshape(B, S, D_ATTN)

def causal_depthwise_conv(x, w, b):
    S = x.shape[1]
    xp = jnp.pad(x, ((0, 0), (CONV_WIDTH_2 - 1, 0), (0, 0)))
    y = b
    for tap in range(CONV_WIDTH_2):
        y = y + xp[:, tap:tap + S, :] * w[tap]
    return y

def block_diag_linear(x, w, b):
    B, S = x.shape[0], x.shape[1]
    xb = x.reshape(B, S, N_RNN_BLOCKS, RNN_BLOCK)
    return jnp.einsum('bsnc,ncd->bsnd', xb, w).reshape(B, S, D_RNN) + b

def rg_lru(x, w_a, b_a, w_x, b_x, lam):
    xf = x.astype(jnp.float32)
    r = jax.nn.sigmoid(block_diag_linear(x, w_a, b_a).astype(jnp.float32))
    i = jax.nn.sigmoid(block_diag_linear(x, w_x, b_x).astype(jnp.float32))
    log_a = -LRU_C * r * jax.nn.softplus(-lam.astype(jnp.float32))
    a = jnp.exp(log_a)
    u = jnp.sqrt(-jnp.expm1(2.0 * log_a)) * (i * xf)

    def combine(left, right):
        a1, b1 = left
        a2, b2 = right
        return a1 * a2, a2 * b1 + b2

    _, h = lax.associative_scan(combine, (a, u), axis=1)
    return h.astype(x.dtype)

def second_inputs(seed: int = 0) -> dict:
    key = jax.random.key(seed)
    ks = jax.random.split(key, 24)
    L, D, F = DEPTH, D_MODEL, D_FF_2
    nrm = lambda k, shape, fan_in: jax.random.normal(k, shape, jnp.float32) * (fan_in ** -0.5)
    gain = lambda k, shape: 1.0 + 0.02 * jax.random.normal(k, shape, jnp.float32)
    bias = lambda k, shape: 0.02 * jax.random.normal(k, shape, jnp.float32)

    x = jax.random.normal(ks[0], (BATCH, SEQ, D), jnp.float32)
    b_in = bias(ks[6], (L, N_IN))
    b_in = b_in.at[:, SPLIT_POINTS[2]:SPLIT_POINTS[3]].add(FORGET_BIAS)
    u = jax.random.uniform(ks[15], (L, D_RNN), jnp.float32, 0.9, 0.999)
    lru_lambda = jnp.log(u) - jnp.log1p(-u)
    return {
        "x": x,
        "ffn1_norm": gain(ks[1], (L, D)),
        "ffn1_w_gate": nrm(ks[2], (L, D, F), D),
        "ffn1_w_up": nrm(ks[3], (L, D, F), D),
        "ffn1_w_down": nrm(ks[4], (L, F, D), F),
        "mix_norm": gain(ks[5], (L, D)),
        "w_in": nrm(ks[7], (L, D, N_IN), D),
        "b_in": b_in,
        "q_norm": gain(ks[8], (L, HEAD_DIM_2)),
        "k_norm": gain(ks[9], (L, HEAD_DIM_2)),
        "conv_w": nrm(ks[10], (L, CONV_WIDTH_2, D_RNN), CONV_WIDTH_2),
        "conv_b": bias(ks[11], (L, D_RNN)),
        "lru_w_a": nrm(ks[12], (L, N_RNN_BLOCKS, RNN_BLOCK, RNN_BLOCK), RNN_BLOCK),
        "lru_b_a": bias(ks[13], (L, D_RNN)),
        "lru_w_x": nrm(ks[14], (L, N_RNN_BLOCKS, RNN_BLOCK, RNN_BLOCK), RNN_BLOCK),
        "lru_b_x": bias(ks[16], (L, D_RNN)),
        "lru_lambda": lru_lambda,
        "w_o_attn": nrm(ks[17], (L, D_ATTN, D), D_ATTN),
        "w_o_rnn": nrm(ks[18], (L, D_RNN, D), D_RNN),
        "w_out": nrm(ks[19], (L, D, D), D),
        "ffn2_norm": gain(ks[20], (L, D)),
        "ffn2_w_gate": nrm(ks[21], (L, D, F), D),
        "ffn2_w_up": nrm(ks[22], (L, D, F), D),
        "ffn2_w_down": nrm(ks[23], (L, F, D), F),
    }

def second_block(x, ffn1_norm, ffn1_w_gate, ffn1_w_up, ffn1_w_down, mix_norm, w_in, b_in,
              q_norm, k_norm, conv_w, conv_b, lru_w_a, lru_b_a, lru_w_x, lru_b_x, lru_lambda,
              w_o_attn, w_o_rnn, w_out, ffn2_norm, ffn2_w_gate, ffn2_w_up, ffn2_w_down):
    B, S = x.shape[0], x.shape[1]
    for l in range(DEPTH):
        x = x + 0.5 * swiglu(rms_norm_2(x, ffn1_norm[l]), ffn1_w_gate[l], ffn1_w_up[l], ffn1_w_down[l])

        h = rms_norm_2(x, mix_norm[l])
        proj = h @ w_in[l] + b_in[l]
        q, k, v, f_logit, xr, gr, g_attn, g_rnn = jnp.split(proj, SPLIT_POINTS, axis=-1)

        q = rms_norm_2(q.reshape(B, S, N_HEADS, HEAD_DIM_2), q_norm[l])
        k = rms_norm_2(k.reshape(B, S, N_HEADS, HEAD_DIM_2), k_norm[l])
        v = v.reshape(B, S, N_HEADS, HEAD_DIM_2)
        log_f = jax.nn.log_sigmoid(f_logit.astype(jnp.float32))
        y_attn = forgetting_attention(q, k, v, log_f) @ w_o_attn[l]

        xr = causal_depthwise_conv(xr, conv_w[l], conv_b[l])
        yr = rg_lru(xr, lru_w_a[l], lru_b_a[l], lru_w_x[l], lru_b_x[l], lru_lambda[l]) * jax.nn.gelu(gr)
        y_rnn = yr @ w_o_rnn[l]

        merged = jax.nn.sigmoid(g_attn) * y_attn + jax.nn.sigmoid(g_rnn) * y_rnn
        x = x + merged @ w_out[l]

        x = x + 0.5 * swiglu(rms_norm_2(x, ffn2_norm[l]), ffn2_w_gate[l], ffn2_w_up[l], ffn2_w_down[l])
    return x


def setup_inputs(seed=0):
    out = dict(first_inputs(seed))
    for name, value in second_inputs(seed + 1).items():
        if name != "x":
            out[name + "_2"] = value
    return out


def reference(
    x, ln_attn_g, w_in, qk_norm_g, diff_lambda, diff_subln_g, w_out, ln_ffn_g, w_up, conv_w,
    conv_b, w_down, rel_bias, ffn1_norm_2, ffn1_w_gate_2, ffn1_w_up_2, ffn1_w_down_2,
    mix_norm_2, w_in_2, b_in_2, q_norm_2, k_norm_2, conv_w_2, conv_b_2, lru_w_a_2, lru_b_a_2,
    lru_w_x_2, lru_b_x_2, lru_lambda_2, w_o_attn_2, w_o_rnn_2, w_out_2, ffn2_norm_2,
    ffn2_w_gate_2, ffn2_w_up_2, ffn2_w_down_2,
):
    x = first_block(
        x, ln_attn_g, w_in, qk_norm_g, diff_lambda, diff_subln_g, w_out, ln_ffn_g, w_up, conv_w,
        conv_b, w_down, rel_bias,
    )
    return second_block(
        x, ffn1_norm_2, ffn1_w_gate_2, ffn1_w_up_2, ffn1_w_down_2, mix_norm_2, w_in_2, b_in_2,
        q_norm_2, k_norm_2, conv_w_2, conv_b_2, lru_w_a_2, lru_b_a_2, lru_w_x_2, lru_b_x_2,
        lru_lambda_2, w_o_attn_2, w_o_rnn_2, w_out_2, ffn2_norm_2, ffn2_w_gate_2, ffn2_w_up_2,
        ffn2_w_down_2,
    )


_drawn_inputs = setup_inputs


def setup_inputs(seed=0):
    import zlib

    import numpy as np

    out = dict(_drawn_inputs(seed))
    spreads = {}
    factors = {'ln_attn_g': 3.287,
     'qk_norm_g': 4.87,
     'diff_subln_g': 5.6,
     'ln_ffn_g': 4.079,
     'conv_b': 3.971,
     'ffn1_norm_2': 5.185,
     'mix_norm_2': 4.953,
     'q_norm_2': 8.0,
     'k_norm_2': 8.0,
     'conv_b_2': 3.241,
     'lru_b_a_2': 8.0,
     'lru_b_x_2': 8.0,
     'ffn2_norm_2': 5.849}
    for name, (base, spread) in spreads.items():
        noise = np.random.default_rng([zlib.crc32(name.encode()), seed]).standard_normal(out[name].shape)
        drawn = base * np.exp(spread * noise) if base else spread * noise
        out[name] = __import__('jax').numpy.asarray(drawn.astype(out[name].dtype))
    for name, factor in factors.items():
        out[name] = (out[name] * factor).astype(out[name].dtype)
    return out
```

```python
import math
from contextlib import ExitStack

import concourse.bass as bass
from concourse import mybir

F32 = mybir.dt.float32
F32R = mybir.dt.float32r
BF16 = mybir.dt.bfloat16
ALU = mybir.AluOpType
ACT = mybir.ActivationFunctionType
AX_X = mybir.AxisListType.X

P = 128
LAYERS = 2
SEQ = 256
TB = SEQ // P
D = 1024
KT = D // P
F = 2816
FT = F // P
UW = 256
UNIT = KT * UW
STEPS = F // UW
NS = 3
EPS = 1e-6
NEG = -1e30
BUCKETS = 32
BIAS_HEADS = 12
DIFF_HEADS = 4
HD1 = 64
HD2 = 128
H2 = 8
LRU_C = 8.0
QKV2 = 3 * D
REST2 = QKV2 + H2
LAM_INIT = [0.8 - 0.6 * math.exp(-0.3 * i) for i in range(LAYERS)]

SKIP = 2
V1_WIN, V1_WOUT, V1_FFN = 0, 14, 18
V1 = 51
V2_FFN1, V2_WIN, V2_GATED, V2_WOUT, V2_FFN2 = 0, 33, 55, 71, 75
V2 = 108
LAST_BEFORE_SKIP = {1: 11, 2: 52}
O1_WIN, O1_WOUT, O1_FFN, O1 = 0, 12, 16, 38
O2_FFN1, O2_WIN, O2_GATED, O2_WOUT, O2_FFN2, O2 = 0, 22, 42, 58, 62, 84

C1_ATTN, C1_FFN, C1_SUB, C1_QK, C1_CONV, C1 = 0, 8, 16, 17, 21, 197
C2_FFN1, C2_MIX, C2_FFN2, C2_BQK, C2_BREST, C2_QN, C2_KN = 0, 8, 16, 24, 40, 72, 73
C2_CB, C2_BA, C2_BX, C2_LAM, C2_CONV, C2_POS, C2 = 74, 82, 90, 98, 106, 138, 146

K_ID, K_TRI, K_ONEU, K_MASK, K_G64, K_G128, K_MEAN, K_N = 0, 128, 256, 512, 768, 896, 1024, 1152


class Signal:

    def __init__(self, sem, per1, per2, credit=0):
        self.sem, self.per, self.credit = sem, {1: per1, 2: per2}, credit

    def at(self, where, k):
        block, layer = where
        before = self.credit + (LAYERS * self.per[1] if block == 2 else 0)
        return layer * self.per[block] + (before + k)


class Chain:

    def __init__(self, eng, sem):
        self.eng, self.sem, self.n = eng, sem, 0

    def link(self, ins):
        self.n += 1
        ins.then_inc(self.sem, 1)
        return self.n

    def wait(self, n=None):
        self.eng.wait_ge(self.sem, self.n if n is None else n)

    def tick(self):
        self.eng.sem_inc(self.sem, 1)
        self.n += 1

    def restart(self):
        if self.n:
            self.wait()
            self.eng.sem_clear(self.sem)
            self.n = 0


def build_program(nc, a, out):
    with ExitStack() as ctx:
        def sb(name, shape, dt=F32):
            return ctx.enter_context(nc.sbuf_tensor(name, shape, dt))

        def sem(name):
            return ctx.enter_context(nc.semaphore(name))

        raw = sb("raw", [P, NS, UNIT])
        w_hi = sb("w_hi", [P, NS, UNIT], F32R)
        w_lo = sb("w_lo", [P, NS, UNIT], F32R)
        x = sb("x", [P, KT, SEQ])
        h_hi, h_lo = sb("h_hi", [P, KT, SEQ], F32R), sb("h_lo", [P, KT, SEQ], F32R)
        y_hi, y_lo = sb("y_hi", [P, KT, SEQ], F32R), sb("y_lo", [P, KT, SEQ], F32R)
        r_hi, r_lo = sb("r_hi", [P, KT, SEQ], F32R), sb("r_lo", [P, KT, SEQ], F32R)
        g_hi = sb("g_hi", [P, 2, 2, SEQ], F32R)
        g_lo = sb("g_lo", [P, 2, 2, SEQ], F32R)
        qk = sb("qk", [P, 16, SEQ])
        v = sb("v", [P, TB, D])
        t4 = sb("t4", [P, 4, SEQ])
        tmp = sb("tmp", [P, 3072])
        big = sb("big", [P, 3072])
        cst = sb("cst", [P, K_N])
        spread = sb("spread", [16, KT * P])
        par1 = sb("par1", [P, LAYERS, C1])
        par2 = sb("par2", [P, LAYERS, C2])
        cur = sb("cur", [P, C1])
        prm = sb("prm", [P, 2, 4, 2, 2])
        wf_raw = sb("wf_raw", [P, LAYERS, KT, H2])
        wf_hi = sb("wf_hi", [P, LAYERS, KT, H2], F32R)
        wf_lo = sb("wf_lo", [P, LAYERS, KT, H2], F32R)
        bf = sb("bf", [P, LAYERS, TB * H2])
        zeros = sb("zeros", [1, 512], BF16)
        eps = sb("eps", [P, 1])
        neglam = sb("neglam", [P, LAYERS])
        std = sb("std", [P, SEQ])
        rstd = sb("rstd", [P, SEQ])
        nmax = sb("nmax", [P, 2, 4])
        esum = sb("esum", [P, 2, 4])
        esc = sb("esc", [P, 2, 4])
        lgs = sb("lgs", [P, 8, 16])
        lf = sb("lf", [P, TB * H2])

        ident, tri = cst[:, K_ID:K_ID + P], cst[:, K_TRI:K_TRI + P]
        one_u = cst[:, K_ONEU:K_ONEU + 256]
        mask = cst[:, K_MASK:K_MASK + 256]
        g64, g128 = cst[:, K_G64:K_G64 + P], cst[:, K_G128:K_G128 + P]
        mean = cst[:, K_MEAN:K_MEAN + P]
        bias = big[:, :].rearrange("p (h k) -> p h k", h=BIAS_HEADS)
        bv = big[:, 0:D]
        lin_a = big[:, D:D + KT * P].rearrange("p (t c) -> p t c", t=KT)
        lin_x = big[:, 2 * D:2 * D + KT * P].rearrange("p (t c) -> p t c", t=KT)

        def pair512(at):
            return tmp[:, at:at + 512].rearrange("p (m s) -> p m s", m=2)

        gate_s, up_s, prod_s = pair512(0), pair512(512), pair512(1024)
        lru_x, lru_c, lru_g, lru_r, lru_i, lru_a = (pair512(512 * n) for n in range(6))
        sig_s, part_s = pair512(0), pair512(512)
        probs = tmp[:, 0:1536].rearrange("p (e m k) -> p e m k", e=2, m=2)
        probs_t = tmp[:, 1536:2304].rearrange("p (m k) -> p m k", m=2)
        t4_flat = t4[:, :, :].rearrange("p t s -> p (t s)")
        decay = [tmp[:, 2304:3072].rearrange("p (m k) -> p m k", m=2),
                 t4_flat[:, 0:768].rearrange("p (m k) -> p m k", m=2)]
        x_tok = v
        prow = tmp[:, 0:1024].rearrange("p (n c) -> p n c", n=8)
        dlam = tmp[:, 1024:1536]
        dprod = tmp[:, 1536:1792].rearrange("p (n d) -> p n d", n=4)
        qk_flat = qk[:, :, :].rearrange("p t s -> p (t s)")
        bflip = qk_flat[:, 0:3072].rearrange("p (h k) -> p h k", h=BIAS_HEADS)
        onehot, relb = qk_flat[0:BUCKETS, 3072:3456], qk_flat[0:BUCKETS, 3456:3468]
        tsb = qk_flat[0:BIAS_HEADS, 3468:3852]
        flip = qk_flat[:, 3852:3980]
        trev = nc.dram_tensor("trev", (BIAS_HEADS, 384), F32, kind="Internal").ap()

        bank = [ctx.enter_context(nc.psum_tensor(f"bank{i}", [P, 512], F32)) for i in range(8)]

        def acc(m):
            return bank[4 + m // 2][:, (m % 2) * SEQ:(m % 2 + 1) * SEQ]

        raw_full = [sem(f"raw_full{s}") for s in range(NS)]
        hi_ready = Signal(sem("hi_ready"), V1, V2)
        lo_ready = Signal(sem("lo_ready"), V1, V2, credit=NS)
        unit_done = Signal(sem("unit_done"), V1, V2, credit=NS)
        evacuated = Signal(sem("evacuated"), O1, O2, credit=2)
        x_ready = Signal(sem("x_ready"), 2 * KT, 3 * KT)
        sq_ready = Signal(sem("sq_ready"), 2 * KT, 3 * KT)
        sq_used = Signal(sem("sq_used"), 2 * KT, 3 * KT)
        std_ready = Signal(sem("std_ready"), 2, 3)
        hf_ready = Signal(sem("hf_ready"), 2 * KT, 3 * KT)
        hh_ready = Signal(sem("hh_ready"), 2 * KT, 3 * KT)
        h_ready = Signal(sem("h_ready"), 2 * KT, 3 * KT)
        gsq_ready = Signal(sem("gsq_ready"), 8, 8)
        gsq_used = Signal(sem("gsq_used"), 8, 8, credit=2)
        gstd_ready = Signal(sem("gstd_ready"), 3, 2)
        grstd_ready = Signal(sem("grstd_ready"), 3, 2)
        bc_done = Signal(sem("bc_done"), 10, 8)
        bc_used = Signal(sem("bc_used"), 10, 8, credit=2)
        scored = Signal(sem("scored"), 8, 4)
        logits_ready = Signal(sem("logits_ready"), 8, 4, credit=1)
        exp_ready = Signal(sem("exp_ready"), 8, 4)
        probs_ready = Signal(sem("probs_ready"), 8, 4)
        turned = Signal(sem("turned"), 8, 4, credit=2)
        pt_ready = Signal(sem("pt_ready"), 8, 4, credit=1)
        pv_done = Signal(sem("pv_done"), 8, 4, credit=1)
        att_hi = Signal(sem("att_hi"), 4, 4, credit=1)
        att_out = Signal(sem("att_out"), 8, 4, credit=1)
        dsq_used = Signal(sem("dsq_used"), 1, 0)
        dn_ready = Signal(sem("dn_ready"), 4, 0)
        dn_hi = Signal(sem("dn_hi"), 4, 0)
        y_ready = Signal(sem("y_ready"), 1, 1)
        prm_ready = Signal(sem("prm_ready"), STEPS, 0)
        conv_main = Signal(sem("conv_main"), 2 * STEPS, 0)
        silu_ready = Signal(sem("silu_ready"), STEPS, 2 * STEPS)
        prod_ready = Signal(sem("prod_ready"), STEPS, 2 * STEPS)
        prod_hi = Signal(sem("prod_hi"), STEPS, 2 * STEPS)
        g_ready = Signal(sem("g_ready"), STEPS, 2 * STEPS)
        cur_ready = Signal(sem("cur_ready"), 1, 1)
        lru_conv_main = Signal(sem("lru_conv_main"), 0, 4)
        lru_conv = Signal(sem("lru_conv"), 0, 4)
        lru_lin = Signal(sem("lru_lin"), 0, 4)
        lru_gates = Signal(sem("lru_gates"), 0, 4)
        lru_m = Signal(sem("lru_m"), 0, 4)
        lru_sqrt = Signal(sem("lru_sqrt"), 0, 4)
        lru_y = Signal(sem("lru_y"), 0, 4)
        lru_hi = Signal(sem("lru_hi"), 0, 4)
        r_ready = Signal(sem("r_ready"), 0, 4)
        f_done = Signal(sem("f_done"), 0, 1)
        f_abs = Signal(sem("f_abs"), 0, 1)
        f_exp = Signal(sem("f_exp"), 0, 1)
        f_ready = Signal(sem("f_ready"), 0, 1)
        decay_ready = Signal(sem("decay_ready"), 0, 4)
        sig_ready = Signal(sem("sig_ready"), 0, 8)
        merged_ready = Signal(sem("merged_ready"), 0, 4)
        merged_hi = Signal(sem("merged_hi"), 0, 4)
        m_ready = Signal(sem("m_ready"), 0, 4)
        side_loaded = Signal(sem("side_loaded"), 0, 1)
        lin_cleared = sem("lin_cleared")
        ld_x, ld_cst, ld_par, ld_rel, ld_wf = (sem(n) for n in ("ld_x", "ld_cst", "ld_par", "ld_rel", "ld_wf"))
        ld_trev, st_trev, st_out = sem("ld_trev"), sem("st_trev"), sem("st_out")
        pro_pe, pro_dve, pro_act = sem("pro_pe"), sem("pro_dve"), sem("pro_act")
        fin_pe, fin_sb = sem("fin_pe"), sem("fin_sb")
        dve_own, act_own, pool_own = sem("dve_own"), sem("act_own"), sem("pool_own")
        loads_issued = sem("loads_issued")

        def full_at(where, vv, i):
            block, layer = where
            per = {1: V1, 2: V2}[block]
            if vv >= per:
                return full_at((block, layer + 1), vv - per, i)
            s = vv % NS
            skipped = [u % NS for u in range(LAST_BEFORE_SKIP[block] + 1, LAST_BEFORE_SKIP[block] + 1 + SKIP)]
            behind = vv > LAST_BEFORE_SKIP[block]
            uses = vv // NS - (behind and s in skipped)
            each = per // NS - (s in skipped)
            skipped1 = [u % NS for u in range(LAST_BEFORE_SKIP[1] + 1, LAST_BEFORE_SKIP[1] + 1 + SKIP)]
            before = LAYERS * (V1 // NS - (s in skipped1)) if block == 2 else 0
            return layer * (16 * each) + i * (16 * 6 // NS) + 16 * (before + uses + 1)

        def raises(block, vv):
            return 1 + SKIP if vv == LAST_BEFORE_SKIP[block] else 1

        block_ = ctx.enter_context(nc.Block())

        @block_.sync
        def _(sp):
            sp.dma_start(x_tok[:, :, :], a["x"].rearrange("a (b p) d -> (a p) b d", p=P)).then_inc(ld_x, 16)
            sp.dma_start(cst[:, :], a["const_main"]).then_inc(ld_cst, 16)
            sp.dma_start(spread[:, :], a["const_spread"]).then_inc(ld_cst, 16)

            def slot(where, vv, i, src, rows):
                s = vv % NS
                sp.wait_ge(lo_ready.sem, lo_ready.at(where, vv + 1 - NS) + i * 6)
                sp.sem_inc(loads_issued, 1)
                dst = raw[:, s, :].rearrange("p (k m) -> p k m", k=rows)
                sp.dma_start(dst, src).then_inc(raw_full[s], 16)

            def cols(where, vv, w, col, i=0, step=0):
                wv = w.rearrange("l (k p) m -> l p k m", p=P)
                at = i * step + col
                src = wv[bass.ds(where[1], 1), :, :, bass.ds(at, UW)].rearrange("l p k m -> (l p) k m")
                slot(where, vv, i, src, KT)

            def rows(where, vv, w, tile, i=0, step=0):
                wv = w.rearrange("l (t p) m -> l p t m", p=P)
                at = i * step + tile
                src = wv[bass.ds(where[1], 1), :, bass.ds(at, 2), :].rearrange("l p t m -> (l p) t m")
                slot(where, vv, i, src, 2)

            def ffn(where, vv, gate, up, up_col, down):
                cols(where, vv, gate, 0)
                cols(where, vv + 1, up, up_col)
                with sp.Fori(0, STEPS // 2) as i:
                    for e in range(2):
                        cols(where, vv + 2 + 3 * e, gate, UW * (e + 1), i, 2 * UW)
                        cols(where, vv + 3 + 3 * e, up, up_col + UW * (e + 1), i, 2 * UW)
                        rows(where, vv + 4 + 3 * e, down, 2 * e, i, 4)
                rows(where, vv + 3 * STEPS - 1, down, 2 * (STEPS - 1))

            with sp.Fori(0, LAYERS) as l:
                where = (1, l)
                for u in range(12):
                    cols(where, V1_WIN + u, a["w_in"], UW * u)
                for u in range(4):
                    cols(where, V1_WOUT + u, a["w_out"], UW * u)
                ffn(where, V1_FFN, a["w_up"], a["w_up"], F, a["w_down"])
            with sp.Fori(0, LAYERS) as l:
                where = (2, l)
                ffn(where, V2_FFN1, a["ffn1_w_gate_2"], a["ffn1_w_up_2"], 0, a["ffn1_w_down_2"])
                w = a["w_in_2"]
                for j in range(4):
                    cols(where, V2_WIN + 3 * j, w, REST2 + UW * j)
                    cols(where, V2_WIN + 3 * j + 1, w, REST2 + D + UW * j)
                    cols(where, V2_WIN + 3 * j + 2, w, UW * j)
                for j in range(8):
                    cols(where, V2_WIN + 12 + j, w, D + UW * j)
                for n, o in ((3, "w_o_rnn_2"), (2, "w_o_attn_2")):
                    for j in range(4):
                        at = V2_GATED + 8 * (3 - n) + 2 * j
                        cols(where, at, w, REST2 + n * D + UW * j)
                        cols(where, at + 1, a[o], UW * j)
                for u in range(4):
                    cols(where, V2_WOUT + u, a["w_out_2"], UW * u)
                ffn(where, V2_FFN2, a["ffn2_w_gate_2"], a["ffn2_w_up_2"], 0, a["ffn2_w_down_2"])
            sp.wait_ge(fin_sb, 4)
            sp.dma_start(out.rearrange("a (b p) d -> (a p) b d", p=P), x_tok[:, :, :]).then_inc(st_out, 16)
            sp.wait_ge(st_out, 16)

        @block_.gpsimd
        def _(pool):
            nc.gpsimd.memset(zeros[:, :], 0.0).then_inc(ld_cst, 1)
            nc.gpsimd.memset(eps[:, :], EPS).then_inc(ld_cst, 1)
            pool.dma_start(onehot, a["const_onehot"]).then_inc(ld_rel, 16)
            pool.dma_start(relb, a["rel_bias"]).then_inc(ld_rel, 16)
            pool.dma_start(flip, a["const_flip"]).then_inc(ld_rel, 16)
            pool.wait_ge(pro_dve, 13)
            pool.dma_start(trev, tsb).then_inc(st_trev, 16)
            pool.wait_ge(st_trev, 16)
            for h in range(BIAS_HEADS):
                pool.dma_start(bflip[:, h, :], bass.AP(trev.tensor, trev.offset + h * 384, [[1, P], [1, 256]])
                               ).then_inc(ld_trev, 16)
            with pool.Fori(0, LAYERS) as l:
                where = (2, l)
                pool.wait_ge(cur_ready.sem, cur_ready.at(where, 1))
                pool.wait_ge(lin_cleared, 2)
                bsrc = a["b_in_2"][bass.ds(l, 1), 2 * D:3 * D].rearrange("l d -> (l d)").partition_broadcast(P)
                pool.dma_start(bv, bsrc).then_inc(side_loaded.sem, 16)
                for dst, name in ((lin_a, "lru_w_a_2"), (lin_x, "lru_w_x_2")):
                    wv = a[name].rearrange("l (t e) c d -> l e c t d", e=2)
                    for e in range(2):
                        src = wv[bass.ds(l, 1), e, :, :, :].rearrange("l c t d -> (l c) t d")
                        pool.dma_start(dst[64 * e:64 * e + 64, :, 64 * e:64 * e + 64], src
                                       ).then_inc(side_loaded.sem, 16)
                pool.wait_ge(f_ready.sem, f_ready.at(where, 1))
                pool.wait_ge(r_ready.sem, r_ready.at(where, 4))
                for p in range(4):
                    if p == 1:
                        pool.wait_ge(gsq_used.sem, gsq_used.at(where, 8))
                    if p >= 2:
                        pool.wait_ge(scored.sem, scored.at(where, p - 1))
                    pool.sem_inc(pool_own, 1)
                    for m in range(2):
                        h = 2 * p + m
                        dst = decay[p % 2]
                        nc.gpsimd.tensor_scalar(dst[:, m, 0:256], one_u, lf[:, H2 + h:H2 + h + 1], 1.0,
                                                ALU.mult, ALU.mult)
                        last = nc.gpsimd.tensor_scalar(dst[:, m, 256:384], one_u[:, 128:256], lf[:, h:h + 1], 1.0,
                                                       ALU.mult, ALU.mult)
                    last.then_inc(decay_ready.sem, 1)

        @block_.tensor
        def _(pe):
            def three(out_, lh, ll, rh, rl, start, stop):
                pe.matmul(out_, lh, rh, start=start, stop=False, skip_group_check=True)
                pe.matmul(out_, lh, rl, start=False, stop=False, skip_group_check=True)
                return pe.matmul(out_, ll, rh, start=False, stop=stop, skip_group_check=True)

            def begin(where, vv, o, i=0, ostep=0):
                pe.wait_ge(lo_ready.sem, lo_ready.at(where, vv + 1) + i * 6)
                if o is not None:
                    pe.wait_ge(evacuated.sem, evacuated.at(where, o - 1) + i * ostep)

            def unit(where, vv, o, b, oh, ol, i=0, ostep=0, ready=None):
                begin(where, vv, o, i, ostep)
                s = vv % NS
                for m in range(2):
                    for k in range(KT):
                        if ready is not None and m == 0:
                            pe.wait_ge(ready[0].sem, ready[0].at(where, ready[1] + k + 1))
                        c = k * UW + m * P
                        mm = three(bank[b][:, m * SEQ:(m + 1) * SEQ], w_hi[:, s, c:c + P], w_lo[:, s, c:c + P],
                                   oh[:, k, :], ol[:, k, :], k == 0, k == KT - 1)
                mm.then_inc(unit_done.sem, raises(where[0], vv))

            def unit_tok(where, vv, o, b):
                begin(where, vv, o)
                s = vv % NS
                for t in range(TB):
                    for k in range(KT):
                        mm = three(bank[b][:, t * UW:(t + 1) * UW], h_hi[:, k, t * P:(t + 1) * P],
                                   h_lo[:, k, t * P:(t + 1) * P], w_hi[:, s, k * UW:(k + 1) * UW],
                                   w_lo[:, s, k * UW:(k + 1) * UW], k == 0, k == KT - 1)
                mm.then_inc(unit_done.sem, raises(where[0], vv))

            def clear_acc():
                for b in range(4, 8):
                    pe.matmul(bank[b][:, :], zeros[:, 0:P], zeros[:, :], start=True, stop=False,
                              skip_group_check=True)

            def down(where, vv, par, step, i=0):
                begin(where, vv, None, i)
                pe.wait_ge(g_ready.sem, g_ready.at(where, step + 1) + i * 2)
                s = vv % NS
                for t in range(2):
                    for m in range(KT):
                        c = t * D + m * P
                        mm = three(acc(m), w_hi[:, s, c:c + P], w_lo[:, s, c:c + P],
                                   g_hi[:, par, t, :], g_lo[:, par, t, :], False, False)
                mm.then_inc(unit_done.sem, 1)

            def ffn(where, vv, o, norm, steps0):
                clear_acc()
                unit(where, vv, o, 0, h_hi, h_lo, ready=(h_ready, norm * KT))
                unit(where, vv + 1, o + 1, 1, h_hi, h_lo)
                with pe.Fori(0, STEPS // 2) as i:
                    for e in range(2):
                        b = 2 * ((e + 1) % 2)
                        unit(where, vv + 2 + 3 * e, o + 2 + 2 * e, b, h_hi, h_lo, i, 4)
                        unit(where, vv + 3 + 3 * e, o + 3 + 2 * e, b + 1, h_hi, h_lo, i, 4)
                        down(where, vv + 4 + 3 * e, e, steps0 + e, i)
                down(where, vv + 3 * STEPS - 1, 0, steps0 + STEPS - 1)

            def norm_sums(where, n):
                for t in range(KT):
                    pe.wait_ge(sq_ready.sem, sq_ready.at(where, n * KT + t + 1))
                    pe.matmul(bank[2][:, 0:SEQ], mean, t4[:, t % 4, :], start=(t == 0), stop=(t == KT - 1)
                              ).then_inc(sq_used.sem, 1)

            def group_sums(where, n, sel):
                if n % 4 == 0 and n:
                    pe.wait_ge(gstd_ready.sem, gstd_ready.at(where, n // 4))
                pe.wait_ge(gsq_ready.sem, gsq_ready.at(where, n + 1))
                for m in range(2):
                    t = 2 * (n % 4) + m
                    mm = pe.matmul(bank[3][0:16, 0:SEQ], sel[:, 16 * t:16 * t + 16], t4[:, 2 * (n % 2) + m, :],
                                   start=(t == 0), stop=(t == KT - 1))
                mm.then_inc(gsq_used.sem, 1)

            def group_spread(where, n, first, pairs, banks):
                pe.wait_ge(grstd_ready.sem, grstd_ready.at(where, n + 1))
                for c in range(pairs):
                    pe.wait_ge(bc_used.sem, bc_used.at(where, first + c - 1))
                    for m in range(2):
                        t = 2 * c + m
                        mm = pe.matmul(bank[banks[c % 2]][:, m * SEQ:(m + 1) * SEQ], spread[:, t * P:(t + 1) * P],
                                       rstd[0:16, :], start=True, stop=True)
                    mm.then_inc(bc_done.sem, 1)

            def scores(where, p):
                b, _ = where
                pe.wait_ge(logits_ready.sem, logits_ready.at(where, p))
                for m in range(2):
                    s = bank[4 + m]
                    if b == 1:
                        qt, kt = (p, 4 + p) if p < 4 else (8 + p - 4, 12 + p - 4)
                        r = slice(64 * m, 64 * m + 64)
                    else:
                        qt, kt = 2 * p + m, 8 + 2 * p + m
                        r = slice(0, P)
                    mm = pe.matmul(s[:, 0:256], qk[r, qt, 128:256], qk[r, kt, 0:256], start=True,
                                   stop=(b == 1), skip_group_check=True)
                    if b == 2:
                        if m == 0:
                            pe.wait_ge(decay_ready.sem, decay_ready.at(where, p + 1))
                        dc = decay[p % 2]
                        pe.matmul(s[:, 0:256], tri, dc[:, m, 0:256], start=False, stop=False,
                                  skip_group_check=True)
                        pe.matmul(s[:, 0:128], one_u[:, 0:128], dc[:, m, 256:384], start=False, stop=True,
                                  skip_group_check=True)
                    mm = pe.matmul(s[:, 256:384], qk[r, qt, 0:128], qk[r, kt, 0:128], start=True,
                                   stop=(b == 1), skip_group_check=True)
                    if b == 2:
                        mm = pe.matmul(s[:, 256:384], tri, dc[:, m, 256:384], start=False, stop=True,
                                       skip_group_check=True)
                mm.then_inc(scored.sem, 1)

            def turn(where, p):
                pe.wait_ge(probs_ready.sem, probs_ready.at(where, p + 1))
                pe.wait_ge(pt_ready.sem, pt_ready.at(where, p))
                maps = 1 if where[0] == 1 and p < 4 else 2
                for m in range(maps):
                    e = probs[:, p % 2, m, :]
                    for c, at in ((0, 256), (1, 0), (2, 128)):
                        mm = pe.transpose(bank[6 + m][:, 128 * c:128 * c + 128], e[:, at:at + 128], ident)
                mm.then_inc(turned.sem, 1)

            def weigh(where, p):
                pe.wait_ge(pt_ready.sem, pt_ready.at(where, p + 1))
                pe.wait_ge(att_out.sem, att_out.at(where, p))
                for m in range(2):
                    if where[0] == 1 and p < 4:
                        if m:
                            break
                        o, c0, n = bank[2][:, :], p * P, P
                    elif where[0] == 1:
                        o, c0, n = bank[2][64 * m:64 * m + 64, :], 512 + (2 * (p - 4) + m) * 64, 64
                    else:
                        o, c0, n = bank[2 + m][:, :], (2 * p + m) * P, P
                    pe.matmul(o[:, 0:256], v[:, 0, c0:c0 + n], probs_t[:, m, 0:256], start=True, stop=False,
                              skip_group_check=True)
                    mm = pe.matmul(o[:, 128:256], v[:, 1, c0:c0 + n], probs_t[:, m, 256:384], start=False,
                                   stop=True, skip_group_check=True)
                mm.then_inc(pv_done.sem, 1)

            def attention(where, pairs):
                scores(where, 0)
                scores(where, 1)
                for p in range(pairs):
                    turn(where, p)
                    if p + 2 < pairs:
                        scores(where, p + 2)
                    weigh(where, p)
                    if where[0] == 1 and p == 5:
                        for t in range(4):
                            mm = pe.matmul(bank[3][0:16, 0:SEQ], g128[:, 16 * t:16 * t + 16], t4[:, t, :],
                                           start=(t == 0), stop=(t == 3))
                        mm.then_inc(dsq_used.sem, 1)
                if where[0] == 1:
                    group_spread(where, 2, 8, 2, (0, 1))

            pe.wait_ge(ld_cst, 34)
            pe.wait_ge(ld_x, 16)
            for c in range(4):
                for m in range(2):
                    for t in range(TB):
                        mm = pe.transpose(bank[c][:, m * SEQ + t * P:m * SEQ + (t + 1) * P],
                                          x_tok[:, t, (2 * c + m) * P:(2 * c + m + 1) * P], ident)
                mm.then_inc(pro_pe, 1)
            mm = pe.matmul(bank[7][:, :], zeros[:, 0:P], zeros[:, :], start=True, stop=True)
            mm.then_inc(unit_done.sem, NS)
            pe.wait_ge(ld_par, PAR_DMAS * 16)
            for n in range(8):
                if n == 4:
                    pe.wait_ge(pro_dve, 4)
                nr = PAR_ROWS[n]
                pe.transpose(bank[(4 + n) % 8][:, 0:nr], prow[0:nr, n, :], ident[0:nr, 0:nr]).then_inc(pro_pe, 1)
            pe.wait_ge(ld_rel, 48)
            pe.wait_ge(pro_dve, 12)
            pe.matmul(bank[4][0:BIAS_HEADS, 0:384], relb, onehot, start=True, stop=True).then_inc(pro_pe, 1)
            pe.wait_ge(ld_trev, 16 * BIAS_HEADS)
            for h in range(0, BIAS_HEADS, 2):
                for m in range(2):
                    mm = pe.matmul(bank[2 + h // 2][:, m * SEQ:(m + 1) * SEQ], flip, bflip[:, h + m, :],
                                   start=True, stop=True)
                mm.then_inc(pro_pe, 1)
            pe.wait_ge(pro_dve, 19)

            with pe.Fori(0, LAYERS) as l:
                where = (1, l)
                norm_sums(where, 0)
                for u in range(12):
                    vv, o, b = V1_WIN + u, O1_WIN + u, u % 2
                    if u % 6 < 4:
                        unit(where, vv, o, b, h_hi, h_lo, ready=(h_ready, 0) if u == 0 else None)
                    else:
                        unit_tok(where, vv, o, b)
                    if 1 <= u % 6 <= 4:
                        group_sums(where, 4 * (u // 6) + u % 6 - 1, g64)
                    if u % 6 == 5:
                        group_spread(where, u // 6, 4 * (u // 6), 4, (6, 7))
                pe.wait_ge(bc_used.sem, bc_used.at(where, 8))
                pe.wait_ge(evacuated.sem, evacuated.at(where, 12))
                attention(where, 8)
                for u in range(4):
                    if u == 0:
                        pe.wait_ge(y_ready.sem, y_ready.at(where, 1))
                    unit(where, V1_WOUT + u, O1_WOUT + u, u % 2, y_hi, y_lo)
                norm_sums(where, 1)
                ffn(where, V1_FFN, O1_FFN, 1, 0)

            with pe.Fori(0, LAYERS) as l:
                where = (2, l)
                norm_sums(where, 0)
                ffn(where, V2_FFN1, O2_FFN1, 0, 0)
                norm_sums(where, 1)

                def lru_linear(j):
                    if j == 0:
                        pe.wait_ge(side_loaded.sem, l * 80 + 80)
                    pe.wait_ge(lru_conv.sem, lru_conv.at(where, j + 1))
                    for b, lin in ((4, lin_a), (5, lin_x)):
                        for m in range(2):
                            mm = pe.matmul(bank[b][:, m * SEQ:(m + 1) * SEQ], lin[:, 2 * j + m, :],
                                           lru_c[:, m, :], start=True, stop=True)
                    mm.then_inc(lru_lin.sem, 1)

                def forget_logits():
                    for t in range(TB):
                        for k in range(KT):
                            wh = wf_hi[:, bass.ds(l, 1), k, :].rearrange("p l h -> p (l h)")
                            wl = wf_lo[:, bass.ds(l, 1), k, :].rearrange("p l h -> p (l h)")
                            mm = three(bank[2][:, t * H2:(t + 1) * H2], h_hi[:, k, t * P:(t + 1) * P],
                                       h_lo[:, k, t * P:(t + 1) * P], wh, wl, k == 0, k == KT - 1)
                    mm.then_inc(f_done.sem, 1)

                for j in range(4):
                    vv, o = V2_WIN + 3 * j, O2_WIN + 3 * j
                    unit(where, vv, o, o % 2, h_hi, h_lo, ready=(h_ready, KT) if j == 0 else None)
                    if j:
                        group_sums(where, j - 1, g128)
                    unit(where, vv + 1, o + 1, (o + 1) % 2, h_hi, h_lo)
                    lru_linear(j)
                    unit(where, vv + 2, o + 2, (o + 2) % 2, h_hi, h_lo)
                for j in range(4):
                    o = O2_WIN + 12 + j
                    unit(where, V2_WIN + 12 + j, o, o % 2, h_hi, h_lo)
                    group_sums(where, 3 + j, g128)
                    if j == 0:
                        forget_logits()
                    if j == 1:
                        group_spread(where, 0, 0, 4, (6, 7))
                for j in range(4):
                    o = O2_WIN + 16 + j
                    unit_tok(where, V2_WIN + 16 + j, o, o % 2)
                    if j == 0:
                        group_sums(where, 7, g128)
                    if j == 2:
                        group_spread(where, 1, 4, 4, (6, 7))
                pe.wait_ge(bc_used.sem, bc_used.at(where, 8))
                pe.wait_ge(evacuated.sem, evacuated.at(where, O2_GATED))
                attention(where, 4)
                for j in range(8):
                    vv, o = V2_GATED + 2 * j, O2_GATED + 2 * j
                    unit(where, vv, o, 0, h_hi, h_lo)
                    if j == 0:
                        pe.wait_ge(r_ready.sem, r_ready.at(where, 4))
                    if j == 4:
                        pe.wait_ge(y_ready.sem, y_ready.at(where, 1))
                    oh, ol = (r_hi, r_lo) if j < 4 else (y_hi, y_lo)
                    unit(where, vv + 1, o + 1, 1, oh, ol)
                for u in range(4):
                    if u == 0:
                        pe.wait_ge(m_ready.sem, m_ready.at(where, 4))
                    unit(where, V2_WOUT + u, O2_WOUT + u, u % 2, r_hi, r_lo)
                norm_sums(where, 2)
                ffn(where, V2_FFN2, O2_FFN2, 2, STEPS)

            for c in range(4):
                pe.wait_ge(x_ready.sem, x_ready.at((2, LAYERS), 2 * c + 2))
                for m in range(2):
                    for t in range(TB):
                        mm = pe.transpose(bank[c][:, t * 256 + m * P:t * 256 + (m + 1) * P],
                                          x[:, 2 * c + m, t * P:(t + 1) * P], ident)
                mm.then_inc(fin_pe, 1)

        @block_.scalar
        def _(act):
            own = Chain(act, act_own)
            A = nc.scalar.activation

            def split_hi(where, vv, i=0):
                s = vv % NS
                act.wait_ge(raw_full[s], full_at(where, vv, i))
                act.wait_ge(unit_done.sem, unit_done.at(where, vv + 1 - NS) + i * 6)
                per = {1: V1, 2: V2}[where[0]]
                A(w_hi[:, s, :], raw[:, s, :], ACT.Copy).then_inc(hi_ready.sem, raises(where[0], vv % per))

            def next_hi(where, vv, i=0):
                skip = LAST_BEFORE_SKIP[where[0]]
                if not skip < vv + NS <= skip + SKIP:
                    split_hi(where, vv + NS, i)

            def guarded_hi(where, vv, i, last):
                if last is None:
                    next_hi(where, vv, i)
                else:
                    with act.If(last < LAYERS * (STEPS // 2) - 1):
                        next_hi(where, vv, i)

            def after_skip(where):
                for n in range(SKIP):
                    split_hi(where, LAST_BEFORE_SKIP[where[0]] + 1 + n + NS)

            def unit_wait(where, vv, i=0):
                act.wait_ge(unit_done.sem, unit_done.at(where, vv + 1) + i * 6)

            def norm(where, n):
                for t in range(KT):
                    act.wait_ge(x_ready.sem, x_ready.at(where, n * KT + t + 1))
                    if t >= 4:
                        act.wait_ge(sq_used.sem, sq_used.at(where, n * KT + t - 3))
                    A(t4[:, t % 4, :], x[:, t, :], ACT.Square).then_inc(sq_ready.sem, 1)
                act.wait_ge(sq_used.sem, sq_used.at(where, n * KT + KT))
                A(std[:, :], bank[2][:, 0:SEQ], ACT.Sqrt, bias=eps[:, :]).then_inc(std_ready.sem, 1)
                for t in range(KT):
                    act.wait_ge(hf_ready.sem, hf_ready.at(where, n * KT + t + 1))
                    A(h_hi[:, t, :], t4[:, t % 4, :], ACT.Copy).then_inc(hh_ready.sem, 1)

            def ffn1_step(where, vv, step, i=0):
                for half, dst in ((0, gate_s), (1, up_s)):
                    if half == 0:
                        act.wait_ge(prm_ready.sem, prm_ready.at(where, step + 1) + i * 2)
                    unit_wait(where, vv + half, i)
                    for m in range(2):
                        b = 2 * PAR(step) + half
                        last = A(dst[:, m, :], bank[b][:, m * SEQ:(m + 1) * SEQ], ACT.Identity,
                                 bias=prm[:, PAR(step), 0, half, m:m + 1], scale=prm[:, PAR(step), 1, half, m:m + 1])
                    last.then_inc(conv_main.sem, 1)
                    next_hi(where, vv + half, i)
                act.wait_ge(evacuated.sem, evacuated.at(where, O1_FFN + 2 * step + 1) + i * 4)
                A(gate_s, gate_s, ACT.Silu).then_inc(silu_ready.sem, 1)
                act.wait_ge(prod_ready.sem, prod_ready.at(where, step + 1) + i * 2)
                A(g_hi[:, PAR(step), :, :], prod_s, ACT.Copy).then_inc(prod_hi.sem, 1)

            def ffn2_step(where, vv, step, n, i=0, last=None):
                unit_wait(where, vv, i)
                b = 2 * PAR(step)
                A(gate_s, bank[b][:, :].rearrange("p (m s) -> p m s", m=2), ACT.Silu).then_inc(silu_ready.sem, 1)
                next_hi(where, vv, i)
                guarded_hi(where, vv + 1, i, last)
                act.wait_ge(prod_ready.sem, prod_ready.at(where, n + step + 1) + i * 2)
                A(g_hi[:, PAR(step), :, :], prod_s, ACT.Copy).then_inc(prod_hi.sem, 1)

            def ffn(where, vv, one_step, last_layer):
                one_step(vv, 0, 0, None)
                own.restart()
                with act.Fori(0, STEPS // 2) as i:
                    for e in range(2):
                        last = None if last_layer is None or e == 0 else last_layer * (STEPS // 2) + i
                        one_step(vv + 2 + 3 * e, 1 + e, i, last)
                        guarded_hi(where, vv + 4 + 3 * e, i, last)
                    own.restart()
                if last_layer is None:
                    next_hi(where, vv + 3 * STEPS - 1)
                else:
                    with act.If(last_layer < LAYERS - 1):
                        next_hi(where, vv + 3 * STEPS - 1)

            def group_std(where, n):
                act.wait_ge(gsq_used.sem, gsq_used.at(where, 4 * n + 4))
                if n:
                    act.wait_ge(grstd_ready.sem, grstd_ready.at(where, n))
                A(std[0:16, :], bank[3][0:16, 0:SEQ], ACT.Sqrt, bias=eps[0:16, :]).then_inc(gstd_ready.sem, 1)

            def exps(where, p):
                act.wait_ge(logits_ready.sem, logits_ready.at(where, p + 1))
                e = p % 2
                for m in range(2):
                    for c, cs in ((0, slice(0, 256)), (1, slice(256, 384))):
                        n = 2 * m + c
                        last = A(probs[:, e, m, cs], probs[:, e, m, cs], ACT.Exp, bias=nmax[:, e, n:n + 1],
                                 scale=-1.0, accum_out=esum[:, e, n:n + 1])
                last.then_inc(exp_ready.sem, 1)

            def copy_turned(where, p):
                act.wait_ge(turned.sem, turned.at(where, p + 1))
                act.wait_ge(pv_done.sem, pv_done.at(where, p))
                for m in range(1 if where[0] == 1 and p < 4 else 2):
                    last = A(probs_t[:, m, :], bank[6 + m][:, 0:384], ACT.Copy)
                last.then_inc(pt_ready.sem, 1)

            def att_high(where, p):
                act.wait_ge(pv_done.sem, pv_done.at(where, p + 1))
                if where[0] == 1 and p < 4:
                    A(qk[:, p, :], bank[2][:, 0:SEQ], ACT.Copy)
                    last = A(t4[:, p, :], bank[2][:, 0:SEQ], ACT.Square)
                    last.then_inc(att_out.sem, 1)
                elif where[0] == 1:
                    A(y_hi[:, p, :], bank[2][:, 0:SEQ], ACT.Copy).then_inc(att_hi.sem, 1)
                else:
                    for m in range(2):
                        last = A(y_hi[:, 2 * p + m, :], bank[2 + m][:, 0:SEQ], ACT.Copy)
                    last.then_inc(att_hi.sem, 1)

            def attention(where, pairs):
                exps(where, 0)
                exps(where, 1)
                for p in range(pairs):
                    copy_turned(where, p)
                    if p + 2 < pairs:
                        exps(where, p + 2)
                    att_high(where, p)
                    if where[0] == 1 and p == 6:
                        act.wait_ge(dsq_used.sem, dsq_used.at(where, 1))
                        A(std[0:16, :], bank[3][0:16, 0:SEQ], ACT.Sqrt, bias=eps[0:16, :]
                          ).then_inc(gstd_ready.sem, 1)
                if where[0] == 1:
                    for t in range(4):
                        act.wait_ge(dn_ready.sem, dn_ready.at(where, t + 1))
                        A(y_hi[:, t, :], t4[:, t, :], ACT.Copy).then_inc(dn_hi.sem, 1)

            n = 0
            for l in range(LAYERS):
                for dst, src in param_loads(a, prow, l):
                    act.dma_start(dst, src).then_inc(ld_par, 16)
                    n += 1
            act.dma_start(dlam, a["diff_lambda"].rearrange("l n d -> (l n d)").partition_broadcast(P)
                          ).then_inc(ld_wf, 16)
            for l in range(LAYERS):
                for t in range(TB):
                    act.dma_start(bf[:, l, t * H2:(t + 1) * H2], a["b_in_2"][l, QKV2:REST2].partition_broadcast(P)
                                  ).then_inc(ld_wf, 16)
                act.dma_start(wf_raw[:, l, :, :], a["w_in_2"][l].rearrange("(k p) m -> p k m", p=P)[:, :, QKV2:REST2]
                              ).then_inc(ld_wf, 16)
            assert n == PAR_DMAS
            for vv in range(NS):
                split_hi_first = raw_full[vv]
                act.wait_ge(split_hi_first, 16)
                if vv == 0:
                    act.wait_ge(ld_cst, 34)
                A(w_hi[:, vv, :], raw[:, vv, :], ACT.Copy).then_inc(hi_ready.sem, 1)
            act.wait_ge(ld_wf, 16 * (1 + LAYERS * (TB + 1)))
            A(wf_hi[:, :, :, :].rearrange("p l k h -> p (l k h)"), wf_raw[:, :, :, :].rearrange("p l k h -> p (l k h)"),
              ACT.Copy).then_inc(pro_act, 1)
            act.wait_ge(pro_dve, 20)
            A(lgs[:, 7, 4:8], lgs[:, 7, 0:4], ACT.Exp).then_inc(pro_act, 1)
            act.wait_ge(pro_dve, 21)
            own.link(A(lgs[:, 1, :], lgs[:, 0, :], ACT.Exp))
            own.wait()
            A(lgs[:, 2, :], lgs[:, 1, :], ACT.Ln, bias=1.0).then_inc(pro_act, 1)
            own.restart()

            with act.Fori(0, LAYERS) as l:
                where = (1, l)
                norm(where, 0)
                for u in range(12):
                    vv, b = V1_WIN + u, u % 2
                    unit_wait(where, vv)
                    if u % 6 < 4:
                        n = 4 * (u // 6) + u % 6
                        t = 8 * (u // 6) + 2 * (u % 6)
                        two = bank[b][:, :].rearrange("p (m s) -> p m s", m=2)
                        A(qk[:, t:t + 2, :], two, ACT.Copy)
                        act.wait_ge(gsq_used.sem, gsq_used.at(where, n - 1))
                        last = A(t4[:, 2 * (n % 2):2 * (n % 2) + 2, :], two, ACT.Square)
                        own.link(last)
                        own.wait()
                        act.sem_inc(gsq_ready.sem, 1)
                        act.sem_inc(evacuated.sem, 1)
                    else:
                        c = 512 * (u // 6) + UW * (u % 6 - 4)
                        A(v[:, :, c:c + UW], bank[b][:, :].rearrange("p (t c) -> p t c", t=TB), ACT.Copy
                          ).then_inc(evacuated.sem, 1)
                    next_hi(where, vv)
                    if u % 6 == 5:
                        pass
                    if u % 6 == 4:
                        group_std(where, u // 6)
                after_skip(where)
                attention(where, 8)
                for u in range(4):
                    if u == 0:
                        pass
                    next_hi(where, V1_WOUT + u)
                norm(where, 1)
                act.wait_ge(cur_ready.sem, cur_ready.at(where, 1))
                ffn(where, V1_FFN, lambda vv, step, i, last: ffn1_step(where, vv, step, i), None)
                own.restart()

            with act.Fori(0, LAYERS) as l:
                where = (2, l)
                norm(where, 0)
                ffn(where, V2_FFN1, lambda vv, step, i, last: ffn2_step(where, vv, step, 0, i), None)
                norm(where, 1)
                act.wait_ge(cur_ready.sem, cur_ready.at(where, 1))

                def lru_gates_(j):
                    act.wait_ge(lru_lin.sem, lru_lin.at(where, j + 1))
                    if j:
                        act.wait_ge(r_ready.sem, r_ready.at(where, j))
                    for b, dst, cb in ((4, lru_r, C2_BA), (5, lru_i, C2_BX)):
                        for m in range(2):
                            t = 2 * j + m
                            k = own.link(A(dst[:, m, :], bank[b][:, m * SEQ:(m + 1) * SEQ], ACT.Sigmoid,
                                           bias=cur[:, cb + t:cb + t + 1]))
                            if b == 4:
                                kr = k
                    own.wait(kr)
                    for m in range(2):
                        t = 2 * j + m
                        own.link(A(lru_x[:, m, :], lru_r[:, m, :], ACT.Tanh, scale=cur[:, C2_POS + t:C2_POS + t + 1]))
                    for m in range(2):
                        t = 2 * j + m
                        own.link(A(lru_a[:, m, :], lru_r[:, m, :], ACT.Exp, scale=cur[:, C2_LAM + t:C2_LAM + t + 1]))
                    own.wait()
                    A(lru_r, lru_a, ACT.Square).then_inc(lru_gates.sem, 1)

                def lru_root(j):
                    act.wait_ge(lru_m.sem, lru_m.at(where, j + 1))
                    A(lru_r, lru_r, ACT.Sqrt).then_inc(lru_sqrt.sem, 1)

                def lru_high(j):
                    act.wait_ge(lru_y.sem, lru_y.at(where, j + 1))
                    A(r_hi[:, 2 * j:2 * j + 2, :], lru_r, ACT.Copy).then_inc(lru_hi.sem, 1)

                def qk_unit(n, vv, b):
                    unit_wait(where, vv)
                    if n in (1, 2, 3):
                        pass
                    act.wait_ge(gsq_used.sem, gsq_used.at(where, n - 1))
                    for m in range(2):
                        t = 2 * n + m
                        src = bank[b][:, m * SEQ:(m + 1) * SEQ]
                        cb = cur[:, C2_BQK + t:C2_BQK + t + 1]
                        own.link(A(qk[:, t, :], src, ACT.Identity, bias=cb))
                        own.link(A(t4[:, 2 * (n % 2) + m, :], src, ACT.Square, bias=cb))
                    own.wait()
                    act.sem_inc(gsq_ready.sem, 1)
                    act.sem_inc(evacuated.sem, 1)
                    next_hi(where, vv)

                for j in range(4):
                    vv, o = V2_WIN + 3 * j, O2_WIN + 3 * j
                    unit_wait(where, vv)
                    if j:
                        act.wait_ge(lru_m.sem, lru_m.at(where, j))
                    ks = []
                    for m in range(2):
                        t = 2 * j + m
                        ks.append(own.link(A(lru_x[:, m, :], bank[o % 2][:, m * SEQ:(m + 1) * SEQ], ACT.Identity,
                                             bias=cur[:, C2_BREST + t:C2_BREST + t + 1])))
                    own.wait()
                    act.sem_inc(evacuated.sem, 1)
                    for m in range(2):
                        t = 2 * j + m
                        last = A(lru_c[:, m, :], lru_x[:, m, :], ACT.Identity, bias=cur[:, C2_CB + t:C2_CB + t + 1],
                                 scale=cur[:, C2_CONV + 24 + t:C2_CONV + 25 + t])
                    last.then_inc(lru_conv_main.sem, 1)
                    next_hi(where, vv)
                    if j:
                        lru_root(j - 1)
                    unit_wait(where, vv + 1)
                    if j:
                        lru_high(j - 1)
                    for m in range(2):
                        t = 2 * j + m
                        last = A(lru_g[:, m, :], bank[(o + 1) % 2][:, m * SEQ:(m + 1) * SEQ], ACT.Gelu_apprx_tanh,
                                 bias=cur[:, C2_BREST + KT + t:C2_BREST + KT + t + 1])
                    last.then_inc(evacuated.sem, 1)
                    next_hi(where, vv + 1)
                    qk_unit(j, vv + 2, (o + 2) % 2)
                    lru_gates_(j)
                for j in range(4):
                    qk_unit(4 + j, V2_WIN + 12 + j, (O2_WIN + 12 + j) % 2)
                    if j == 0:
                        lru_root(3)
                        group_std(where, 0)
                    if j == 1:
                        lru_high(3)
                        act.wait_ge(f_abs.sem, f_abs.at(where, 1))
                        own.link(A(lgs[:, 1, :], lgs[:, 0, :], ACT.Exp))
                        own.wait()
                        A(lgs[:, 2, :], lgs[:, 1, :], ACT.Ln, bias=1.0).then_inc(f_exp.sem, 1)
                for j in range(4):
                    vv = V2_WIN + 16 + j
                    next_hi(where, vv)
                    if j == 1:
                        group_std(where, 1)
                after_skip(where)
                attention(where, 4)
                for j in range(8):
                    vv = V2_GATED + 2 * j
                    unit_wait(where, vv)
                    if j:
                        act.wait_ge(evacuated.sem, evacuated.at(where, O2_GATED + 2 * j))
                    else:
                        act.wait_ge(y_ready.sem, y_ready.at(where, 1))
                    for m in range(2):
                        cb = C2_BREST + (24 if j < 4 else 16) + 2 * (j % 4) + m
                        own.link(A(sig_s[:, m, :], bank[0][:, m * SEQ:(m + 1) * SEQ], ACT.Sigmoid,
                                   bias=cur[:, cb:cb + 1]))
                    own.wait()
                    act.sem_inc(sig_ready.sem, 1)
                    act.sem_inc(evacuated.sem, 1)
                    next_hi(where, vv)
                    next_hi(where, vv + 1)
                    if j >= 4:
                        act.wait_ge(merged_ready.sem, merged_ready.at(where, j - 3))
                        A(r_hi[:, 2 * j - 8:2 * j - 6, :], part_s, ACT.Copy).then_inc(merged_hi.sem, 1)
                for u in range(4):
                    next_hi(where, V2_WOUT + u)
                norm(where, 2)
                own.restart()
                ffn(where, V2_FFN2, lambda vv, step, i, last: ffn2_step(where, vv, step, STEPS, i, last), l)
                own.restart()

        @block_.vector
        def _(dve):
            own = Chain(dve, dve_own)
            V = nc.vector

            def lo_part(dst, src, hi):
                return V.tensor_tensor(dst, src, hi.bitcast(F32), ALU.subtract)

            def split_lo(where, vv, i=0):
                s = vv % NS
                dve.wait_ge(hi_ready.sem, hi_ready.at(where, vv + 1) + i * 6)
                per = {1: V1, 2: V2}[where[0]]
                lo_part(w_lo[:, s, :], raw[:, s, :], w_hi[:, s, :]).then_inc(
                    lo_ready.sem, raises(where[0], vv % per))

            def next_lo(where, vv, i=0):
                skip = LAST_BEFORE_SKIP[where[0]]
                if not skip < vv + NS <= skip + SKIP:
                    split_lo(where, vv + NS, i)

            def guarded_lo(where, vv, i, last):
                if last is None:
                    next_lo(where, vv, i)
                else:
                    with dve.If(last < LAYERS * (STEPS // 2) - 1):
                        next_lo(where, vv, i)

            def after_skip(where):
                for n in range(SKIP):
                    split_lo(where, LAST_BEFORE_SKIP[where[0]] + 1 + n + NS)

            def unit_wait(where, vv, i=0):
                dve.wait_ge(unit_done.sem, unit_done.at(where, vv + 1) + i * 6)

            def norm(where, n, col):
                dve.wait_ge(std_ready.sem, std_ready.at(where, n + 1))
                own.link(V.reciprocal(rstd[:, :], std[:, :]))
                own.wait()
                for t in range(KT + 1):
                    if t < KT:
                        V.scalar_tensor_tensor(out=t4[:, t % 4, :], in0=x[:, t, :], scalar=cur[:, col + t:col + t + 1],
                                               in1=rstd[:, :], op0=ALU.mult, op1=ALU.mult).then_inc(hf_ready.sem, 1)
                    if t:
                        dve.wait_ge(hh_ready.sem, hh_ready.at(where, n * KT + t))
                        lo_part(h_lo[:, t - 1, :], t4[:, (t - 1) % 4, :], h_hi[:, t - 1, :]).then_inc(h_ready.sem, 1)

            def add_down(where, scale):
                for t in range(KT):
                    V.scalar_tensor_tensor(out=x[:, t, :], in0=acc(t), scalar=scale, in1=x[:, t, :],
                                           op0=ALU.mult, op1=ALU.add).then_inc(x_ready.sem, 1)

            def product(where, step, n, i, gate, up):
                dve.wait_ge(silu_ready.sem, silu_ready.at(where, n + step + 1) + i * 2)
                if where[0] == 2:
                    dve.wait_ge(g_ready.sem, g_ready.at(where, n + step) + i * 2)
                own.link(V.tensor_tensor(prod_s, gate, up, ALU.mult))
                own.wait()
                dve.sem_inc(prod_ready.sem, 1)

            def product_lo(where, step, n, i):
                dve.wait_ge(prod_hi.sem, prod_hi.at(where, n + step + 1) + i * 2)
                lo_part(g_lo[:, PAR(step), :, :], prod_s, g_hi[:, PAR(step), :, :]).then_inc(g_ready.sem, 1)

            def step_params(where, step, i):
                kinds = cur[:, C1_CONV:C1_CONV + 8 * FT].rearrange("p (k f t) -> p k f t", k=4, f=2)
                at = i * 4 + 2 * step
                for half in range(2):
                    src = kinds[:, :, half, bass.ds(at, 2)]
                    last = V.tensor_copy(prm[:, PAR(step), :, half, :], src)
                own.link(last)
                own.wait()
                dve.sem_inc(prm_ready.sem, 1)

            def ffn1_step(where, vv, step, i=0):
                step_params(where, step, i)
                par = PAR(step)
                for half, dst in ((0, gate_s), (1, up_s)):
                    dve.wait_ge(conv_main.sem, conv_main.at(where, 2 * step + half + 1) + i * 4)
                    ks = []
                    for tap, kind in ((1, 3), (2, 2)):
                        for m in range(2):
                            if tap == 2:
                                own.wait(ks[m])
                            b = 2 * par + half
                            ks.append(own.link(V.scalar_tensor_tensor(
                                out=dst[:, m, tap:SEQ], in0=bank[b][:, m * SEQ:(m + 1) * SEQ - tap],
                                scalar=prm[:, par, kind, half, m:m + 1], in1=dst[:, m, tap:SEQ],
                                op0=ALU.mult, op1=ALU.add)))
                    own.wait()
                    dve.sem_inc(evacuated.sem, 1)
                    next_lo(where, vv + half, i)
                product(where, step, 0, i, gate_s, up_s)
                product_lo(where, step, 0, i)

            def ffn2_step(where, vv, step, n, i=0, last=None):
                next_lo(where, vv, i)
                unit_wait(where, vv + 1, i)
                up = bank[2 * PAR(step) + 1][:, :].rearrange("p (m s) -> p m s", m=2)
                product(where, step, n, i, gate_s, up)
                dve.sem_inc(evacuated.sem, 2)
                guarded_lo(where, vv + 1, i, last)
                product_lo(where, step, n, i)

            def ffn(where, vv, one_step, last_layer, scale):
                one_step(vv, 0, 0, None)
                own.restart()
                with dve.Fori(0, STEPS // 2) as i:
                    for e in range(2):
                        last = None if last_layer is None or e == 0 else last_layer * (STEPS // 2) + i
                        one_step(vv + 2 + 3 * e, 1 + e, i, last)
                        guarded_lo(where, vv + 4 + 3 * e, i, last)
                    own.restart()
                unit_wait(where, vv + 3 * STEPS - 1)
                add_down(where, scale)
                if last_layer is None:
                    next_lo(where, vv + 3 * STEPS - 1)
                else:
                    with dve.If(last_layer < LAYERS - 1):
                        next_lo(where, vv + 3 * STEPS - 1)

            def group_rstd(where, n):
                dve.wait_ge(gstd_ready.sem, gstd_ready.at(where, n + 1))
                V.reciprocal(rstd[0:16, :], std[0:16, :]).then_inc(grstd_ready.sem, 1)

            def group_apply(where, first, tile0, gains):
                for c in range(4):
                    dve.wait_ge(bc_done.sem, bc_done.at(where, first + c + 1))
                    for m in range(2):
                        t = tile0 + 2 * c + m
                        g = gains[(2 * c + m) // 4]
                        own.link(V.scalar_tensor_tensor(
                            out=qk[:, t, :], in0=qk[:, t, :], scalar=cur[:, g:g + 1],
                            in1=bank[6 + c % 2][:, m * SEQ:(m + 1) * SEQ], op0=ALU.mult, op1=ALU.mult))
                    own.wait()
                    dve.sem_inc(bc_used.sem, 1)

            def logits(where, p):
                dve.wait_ge(scored.sem, scored.at(where, p + 1))
                dve.wait_ge(turned.sem, turned.at(where, p - 1))
                own.tick()
                e = p % 2
                for m in range(2):
                    if where[0] == 1:
                        h = p if p < 4 else 4 + 2 * (p - 4) + m
                        add = bias[:, h, :]
                    else:
                        add = mask
                    for c, ps, ad in ((0, slice(0, 256), add), (1, slice(256, 384), add[:, 128:256])):
                        n = 2 * m + c
                        last = V.tensor_tensor_reduce(out=probs[:, e, m, ps], in0=bank[4 + m][:, ps], in1=ad,
                                                      scale=-1.0, scalar=3e38, op0=ALU.add, op1=ALU.min,
                                                      accum_out=nmax[:, e, n:n + 1])
                last.then_inc(logits_ready.sem, 1)

            def normalise(where, p, l):
                dve.wait_ge(exp_ready.sem, exp_ready.at(where, p + 1))
                e = p % 2
                own.link(V.reciprocal(esc[:, e, :], esum[:, e, :]))
                own.wait()
                if where[0] == 1 and p < 4:
                    own.link(V.tensor_scalar(esc[:, e, 2:4], esc[:, e, 2:4], neglam[:, bass.ds(l, 1)], None, ALU.mult))
                    for c, cs in ((0, slice(0, 256)), (1, slice(256, 384))):
                        own.link(V.tensor_scalar(probs[:, e, 0, cs], probs[:, e, 0, cs], esc[:, e, c:c + 1], None,
                                                 ALU.mult))
                    own.wait()
                    for c, cs in ((0, slice(0, 256)), (1, slice(256, 384))):
                        last = V.scalar_tensor_tensor(out=probs[:, e, 0, cs], in0=probs[:, e, 1, cs],
                                                      scalar=esc[:, e, 2 + c:3 + c], in1=probs[:, e, 0, cs],
                                                      op0=ALU.mult, op1=ALU.add)
                else:
                    for m in range(2):
                        for c, cs in ((0, slice(0, 256)), (1, slice(256, 384))):
                            n = 2 * m + c
                            last = V.tensor_scalar(probs[:, e, m, cs], probs[:, e, m, cs], esc[:, e, n:n + 1], None,
                                                   ALU.mult)
                last.then_inc(probs_ready.sem, 1)

            def att_low(where, p):
                if where[0] == 1 and p < 4:
                    return
                dve.wait_ge(att_hi.sem, att_hi.at(where, p - 3 if where[0] == 1 else p + 1))
                if where[0] == 1:
                    last = lo_part(y_lo[:, p, :], bank[2][:, 0:SEQ], y_hi[:, p, :])
                else:
                    for m in range(2):
                        last = lo_part(y_lo[:, 2 * p + m, :], bank[2 + m][:, 0:SEQ], y_hi[:, 2 * p + m, :])
                last.then_inc(att_out.sem, 1)

            def attention(where, pairs, l):
                logits(where, 0)
                logits(where, 1)
                normalise(where, 0, l)
                for p in range(pairs):
                    if p + 1 < pairs:
                        normalise(where, p + 1, l)
                    if p + 2 < pairs:
                        logits(where, p + 2)
                    att_low(where, p)
                    if where[0] == 1 and p == 7:
                        group_rstd(where, 2)
                if where[0] == 1:
                    for c in range(2):
                        dve.wait_ge(bc_done.sem, bc_done.at(where, 8 + c + 1))
                        for m in range(2):
                            t = 2 * c + m
                            own.link(V.scalar_tensor_tensor(
                                out=t4[:, t, :], in0=qk[:, t, :], scalar=cur[:, C1_SUB:C1_SUB + 1],
                                in1=bank[c][:, m * SEQ:(m + 1) * SEQ], op0=ALU.mult, op1=ALU.mult))
                        own.wait()
                        dve.sem_inc(bc_used.sem, 1)
                        dve.sem_inc(dn_ready.sem, 2)
                    for t in range(4):
                        dve.wait_ge(dn_hi.sem, dn_hi.at(where, t + 1))
                        last = lo_part(y_lo[:, t, :], t4[:, t, :], y_hi[:, t, :])
                    last.then_inc(y_ready.sem, 1)
                else:
                    own.link(V.tensor_copy(lgs[:, 7, 8:9], lgs[:, 7, 8:9]))
                    own.wait()
                    dve.sem_inc(y_ready.sem, 1)

            def log_sigmoid_rest(f, dst, mul):
                e, ln, d, k = lgs[:, 1, :], lgs[:, 2, :], lgs[:, 3, :], lgs[:, 4, :]
                own.link(V.tensor_scalar(d, e, 1.0, -1.0, ALU.add, ALU.add))
                own.wait()
                own.link(V.tensor_scalar(k, d, 0.0, None, ALU.is_equal))
                own.wait()
                own.link(V.tensor_tensor(d, d, k, ALU.add))
                own.wait()
                own.link(V.reciprocal(d, d))
                own.wait()
                own.link(V.tensor_tensor(d, d, ln, ALU.mult))
                own.wait()
                own.link(V.tensor_tensor(d, d, k, ALU.add))
                own.wait()
                own.link(V.tensor_tensor(d, d, e, ALU.mult))
                own.wait()
                own.link(V.scalar_tensor_tensor(out=dst, in0=f, scalar=0.0, in1=d, op0=ALU.min, op1=ALU.subtract))
                own.wait()
                if mul is not None:
                    own.link(V.tensor_scalar(dst, dst, mul, None, ALU.mult))
                    own.wait()

            V.memset(lgs[:, 7, :], 0.0).then_inc(lo_ready.sem, NS)
            for c, (s, k) in enumerate(((evacuated, 2), (gsq_used, 2), (bc_used, 2), (logits_ready, 1), (turned, 2),
                                        (pt_ready, 1), (pv_done, 1), (att_hi, 1), (att_out, 1))):
                dve.sem_inc(s.sem, k)
            for c in range(4):
                dve.wait_ge(pro_pe, c + 1)
                own.link(V.tensor_copy(x[:, 2 * c:2 * c + 2, :], bank[c][:, :].rearrange("p (m s) -> p m s", m=2)))
                own.wait()
                dve.sem_inc(x_ready.sem, 2)
                dve.sem_inc(pro_dve, 1)
            for n in range(8):
                dve.wait_ge(pro_pe, 5 + n)
                l, first = (n // 2) % 2, n % 2 == 0
                if n < 4:
                    dst = par1[:, l, 0:109] if first else par1[:, l, 109:197]
                else:
                    dst = par2[:, l, 0:106] if first else par2[:, l, 106:138]
                V.tensor_copy(dst, bank[(4 + n) % 8][:, 0:PAR_ROWS[n]]).then_inc(pro_dve, 1)
            dve.wait_ge(pro_dve, 12)
            dve.wait_ge(pro_pe, 13)
            V.tensor_copy(tsb, bank[4][0:BIAS_HEADS, 0:384]).then_inc(pro_dve, 1)
            for vv in range(NS):
                dve.wait_ge(hi_ready.sem, vv + 1)
                lo_part(w_lo[:, vv, :], raw[:, vv, :], w_hi[:, vv, :]).then_inc(lo_ready.sem, 1)
            for l in range(LAYERS):
                for col, by in ((C1_QK, HD1 ** -0.5), (C1_QK + 2, HD1 ** -0.5), (C1_SUB, 1.0 - LAM_INIT[l])):
                    own.link(V.tensor_scalar(par1[:, l, col:col + 1], par1[:, l, col:col + 1], by, None, ALU.mult))
                own.link(V.tensor_scalar(par2[:, l, C2_QN:C2_QN + 1], par2[:, l, C2_QN:C2_QN + 1], HD2 ** -0.5, None,
                                         ALU.mult))
            dve.wait_ge(ld_trev, 16 * BIAS_HEADS)
            for h in range(0, BIAS_HEADS, 2):
                dve.wait_ge(pro_pe, 14 + h // 2)
                for m in range(2):
                    last = V.tensor_tensor(bias[:, h + m, :], bank[2 + h // 2][:, m * SEQ:(m + 1) * SEQ], mask, ALU.add)
                last.then_inc(pro_dve, 1)
            dve.wait_ge(ld_wf, 16 * (1 + LAYERS * (TB + 1)))
            dve.wait_ge(pro_act, 1)
            lo_part(wf_lo[:, :, :, :].rearrange("p l k h -> p (l k h)"),
                    wf_raw[:, :, :, :].rearrange("p l k h -> p (l k h)"),
                    wf_hi[:, :, :, :].rearrange("p l k h -> p (l k h)"))
            pairs = dlam.rearrange("p (n e d) -> p n e d", n=4, e=2)
            own.link(V.tensor_tensor(dprod, pairs[:, :, 0, :], pairs[:, :, 1, :], ALU.mult))
            own.wait()
            V.tensor_reduce(lgs[:, 7, 0:4], dprod, AX_X, ALU.add).then_inc(pro_dve, 1)
            lam2 = lgs[:, 6, :].rearrange("p (l t) -> p l t", l=LAYERS)
            own.link(V.tensor_copy(lam2, par2[:, :, C2_LAM:C2_LAM + KT]))
            own.wait()
            V.scalar_tensor_tensor(out=lgs[:, 0, :], in0=lgs[:, 6, :], scalar=-1.0, in1=lgs[:, 6, :], op0=ALU.mult,
                                   op1=ALU.min).then_inc(pro_dve, 1)
            dve.wait_ge(pro_act, 2)
            e4 = lgs[:, 7, 4:8].rearrange("p (l e) -> p l e", l=LAYERS)
            own.link(V.tensor_tensor(neglam[:, :], e4[:, :, 1], e4[:, :, 0], ALU.subtract))
            own.wait()
            for l in range(LAYERS):
                own.link(V.tensor_scalar(neglam[:, l:l + 1], neglam[:, l:l + 1], -LAM_INIT[l], None, ALU.add))
            dve.wait_ge(pro_act, 3)
            log_sigmoid_rest(lgs[:, 6, :], lgs[:, 5, :], LRU_C)
            c5 = lgs[:, 5, :].rearrange("p (l t) -> p l t", l=LAYERS)
            own.link(V.tensor_copy(par2[:, :, C2_LAM:C2_LAM + KT], c5))
            own.link(V.tensor_scalar(par2[:, :, C2_POS:C2_POS + KT], c5, -1.0, None, ALU.mult))
            own.restart()

            with dve.Fori(0, LAYERS) as l:
                where = (1, l)
                own.link(V.tensor_copy(cur[:, :], par1[:, bass.ds(l, 1), :].rearrange("p l c -> p (l c)")))
                own.wait()
                dve.sem_inc(cur_ready.sem, 1)
                norm(where, 0, C1_ATTN)
                for u in range(12):
                    next_lo(where, V1_WIN + u)
                    if u % 6 == 5:
                        group_rstd(where, u // 6)
                        group_apply(where, 4 * (u // 6), 8 * (u // 6), (C1_QK + 2 * (u // 6), C1_QK + 2 * (u // 6) + 1))
                after_skip(where)
                attention(where, 8, l)
                for u in range(4):
                    vv = V1_WOUT + u
                    unit_wait(where, vv)
                    for m in range(2):
                        t = 2 * u + m
                        last = V.tensor_tensor(x[:, t, :], bank[u % 2][:, m * SEQ:(m + 1) * SEQ], x[:, t, :], ALU.add)
                    own.link(last)
                    own.wait()
                    dve.sem_inc(evacuated.sem, 1)
                    dve.sem_inc(x_ready.sem, 2)
                    next_lo(where, vv)
                norm(where, 1, C1_FFN)
                ffn(where, V1_FFN, lambda vv, step, i, last: ffn1_step(where, vv, step, i), None, 1.0)
                own.restart()

            V.memset(lin_a, 0.0).then_inc(lin_cleared, 1)
            V.memset(lin_x, 0.0).then_inc(lin_cleared, 1)
            with dve.Fori(0, LAYERS) as l:
                where = (2, l)
                own.link(V.tensor_copy(cur[:, 0:C2], par2[:, bass.ds(l, 1), :].rearrange("p l c -> p (l c)")))
                own.wait()
                dve.sem_inc(cur_ready.sem, 1)
                norm(where, 0, C2_FFN1)
                ffn(where, V2_FFN1, lambda vv, step, i, last: ffn2_step(where, vv, step, 0, i), None, 0.5)
                norm(where, 1, C2_MIX)

                def lru_taps(j):
                    dve.wait_ge(lru_conv_main.sem, lru_conv_main.at(where, j + 1))
                    ks = []
                    for tap in (1, 2, 3):
                        for m in range(2):
                            if tap > 1:
                                own.wait(ks[-2])
                            cc = C2_CONV + (3 - tap) * KT + 2 * j + m
                            ks.append(own.link(V.scalar_tensor_tensor(
                                out=lru_c[:, m, tap:SEQ], in0=lru_x[:, m, 0:SEQ - tap], scalar=cur[:, cc:cc + 1],
                                in1=lru_c[:, m, tap:SEQ], op0=ALU.mult, op1=ALU.add)))
                    own.wait()
                    dve.sem_inc(lru_conv.sem, 1)

                def lru_gains(j):
                    dve.wait_ge(lru_gates.sem, lru_gates.at(where, j + 1))
                    own.link(V.tensor_tensor(lru_i, lru_i, lru_c, ALU.mult))
                    own.link(V.scalar_tensor_tensor(out=lru_r, in0=lru_r, scalar=1.0, in1=lru_x, op0=ALU.add,
                                                    op1=ALU.mult))
                    own.wait()
                    dve.sem_inc(lru_m.sem, 1)

                def lru_scan(j):
                    dve.wait_ge(lru_sqrt.sem, lru_sqrt.at(where, j + 1))
                    own.link(V.tensor_tensor(lru_i, lru_i, lru_r, ALU.mult))
                    own.wait()
                    for m in range(2):
                        own.link(V.tensor_tensor_scan(lru_r[:, m, :], lru_a[:, m, :], lru_i[:, m, :], 0.0, ALU.mult,
                                                      ALU.add))
                    own.wait()
                    own.link(V.tensor_tensor(lru_r, lru_r, lru_g, ALU.mult))
                    own.wait()
                    dve.sem_inc(lru_y.sem, 1)

                def lru_low(j):
                    dve.wait_ge(lru_hi.sem, lru_hi.at(where, j + 1))
                    lo_part(r_lo[:, 2 * j:2 * j + 2, :], lru_r, r_hi[:, 2 * j:2 * j + 2, :]).then_inc(r_ready.sem, 1)

                for j in range(4):
                    vv = V2_WIN + 3 * j
                    lru_taps(j)
                    next_lo(where, vv)
                    if j:
                        lru_scan(j - 1)
                    next_lo(where, vv + 1)
                    if j:
                        lru_low(j - 1)
                    next_lo(where, vv + 2)
                    lru_gains(j)
                for j in range(4):
                    next_lo(where, V2_WIN + 12 + j)
                    if j == 0:
                        lru_scan(3)
                        dve.wait_ge(f_done.sem, f_done.at(where, 1))
                        own.link(V.tensor_tensor(lgs[:, 6, :], bank[2][:, 0:16],
                                                 bf[:, bass.ds(l, 1), :].rearrange("p l h -> p (l h)"), ALU.add))
                        own.wait()
                        V.scalar_tensor_tensor(out=lgs[:, 0, :], in0=lgs[:, 6, :], scalar=-1.0, in1=lgs[:, 6, :],
                                               op0=ALU.mult, op1=ALU.min).then_inc(f_abs.sem, 1)
                        group_rstd(where, 0)
                    if j == 1:
                        lru_low(3)
                        group_apply(where, 0, 0, (C2_QN, C2_QN))
                        dve.wait_ge(f_exp.sem, f_exp.at(where, 1))
                        log_sigmoid_rest(lgs[:, 6, :], lf[:, :], None)
                        dve.sem_inc(f_ready.sem, 1)
                for j in range(4):
                    vv, o = V2_WIN + 16 + j, O2_WIN + 16 + j
                    unit_wait(where, vv)
                    if j == 0:
                        dve.wait_ge(side_loaded.sem, l * 80 + 80)
                        dve.wait_ge(evacuated.sem, evacuated.at(where, o))
                    add = bv.rearrange("p (j c) -> p j c", j=4)[:, j:j + 1, :]
                    for t in range(TB):
                        last = V.tensor_tensor(v[:, t, UW * j:UW * (j + 1)], bank[o % 2][:, t * UW:(t + 1) * UW],
                                               bv[:, UW * j:UW * (j + 1)], ALU.add)
                    last.then_inc(evacuated.sem, 1)
                    next_lo(where, vv)
                    if j == 1:
                        group_rstd(where, 1)
                    if j == 2:
                        group_apply(where, 4, 8, (C2_KN, C2_KN))
                after_skip(where)
                attention(where, 4, l)
                for j in range(8):
                    vv = V2_GATED + 2 * j
                    next_lo(where, vv)
                    unit_wait(where, vv + 1)
                    dve.wait_ge(sig_ready.sem, sig_ready.at(where, j + 1))
                    two = bank[1][:, :].rearrange("p (m s) -> p m s", m=2)
                    tiles = qk[:, 2 * (j % 4):2 * (j % 4) + 2, :]
                    if j < 4:
                        own.link(V.tensor_tensor(tiles, sig_s, two, ALU.mult))
                        own.wait()
                        dve.sem_inc(evacuated.sem, 1)
                        next_lo(where, vv + 1)
                    else:
                        if j > 4:
                            dve.wait_ge(m_ready.sem, m_ready.at(where, j - 4))
                        own.link(V.tensor_tensor(part_s, sig_s, two, ALU.mult))
                        own.wait()
                        dve.sem_inc(evacuated.sem, 1)
                        own.link(V.tensor_tensor(part_s, part_s, tiles, ALU.add))
                        own.wait()
                        dve.sem_inc(merged_ready.sem, 1)
                        next_lo(where, vv + 1)
                        dve.wait_ge(merged_hi.sem, merged_hi.at(where, j - 3))
                        rs = slice(2 * j - 8, 2 * j - 6)
                        lo_part(r_lo[:, rs, :], part_s, r_hi[:, rs, :]).then_inc(m_ready.sem, 1)
                for u in range(4):
                    vv = V2_WOUT + u
                    unit_wait(where, vv)
                    for m in range(2):
                        t = 2 * u + m
                        last = V.tensor_tensor(x[:, t, :], bank[u % 2][:, m * SEQ:(m + 1) * SEQ], x[:, t, :], ALU.add)
                    own.link(last)
                    own.wait()
                    dve.sem_inc(evacuated.sem, 1)
                    dve.sem_inc(x_ready.sem, 2)
                    next_lo(where, vv)
                norm(where, 2, C2_FFN2)
                own.restart()
                ffn(where, V2_FFN2, lambda vv, step, i, last: ffn2_step(where, vv, step, STEPS, i, last), l, 0.5)
                own.restart()

            for c in range(4):
                dve.wait_ge(fin_pe, c + 1)
                V.tensor_copy(x_tok[:, :, 256 * c:256 * (c + 1)], bank[c][:, :].rearrange("p (t c) -> p t c", t=TB)
                              ).then_inc(fin_sb, 1)


def PAR(step):
    return step % 2


PAR_ROWS = [109, 88, 109, 88, 106, 32, 106, 32]
PAR_DMAS = LAYERS * (7 + 2 + 10 + 1)


def param_loads(a, prow, l):
    def rows(vec):
        return vec.rearrange("(t p) -> t p", p=P)

    t = prow[:, 2 * l, :]
    out = [(t[C1_ATTN:C1_ATTN + 8, :], rows(a["ln_attn_g"][l])), (t[C1_FFN:C1_FFN + 8, :], rows(a["ln_ffn_g"][l])),
           (t[C1_SUB:C1_SUB + 1, :], a["diff_subln_g"][l:l + 1, :]),
           (t[C1_QK:C1_QK + 4, 0:64], a["qk_norm_g"][l]), (t[C1_QK:C1_QK + 4, 64:128], a["qk_norm_g"][l]),
           (t[21:65, :], rows(a["conv_b"][l])), (t[65:109, :], rows(a["conv_w"][l, 2]))]
    t = prow[:, 2 * l + 1, :]
    out += [(t[0:44, :], rows(a["conv_w"][l, 0])), (t[44:88, :], rows(a["conv_w"][l, 1]))]
    t = prow[:, 4 + 2 * l, :]
    b = a["b_in_2"][l]
    out += [(t[0:8, :], rows(a["ffn1_norm_2"][l])), (t[8:16, :], rows(a["mix_norm_2"][l])),
            (t[16:24, :], rows(a["ffn2_norm_2"][l])), (t[24:40, :], rows(b[0:2 * D])),
            (t[40:72, :], rows(b[REST2:REST2 + 4 * D])),
            (t[72:73, :], a["q_norm_2"][l:l + 1, :]), (t[73:74, :], a["k_norm_2"][l:l + 1, :]),
            (t[74:82, :], rows(a["conv_b_2"][l])), (t[82:90, :], rows(a["lru_b_a_2"][l])),
            (t[90:98, :], rows(a["lru_b_x_2"][l]))]
    out += [(t[98:106, :], rows(a["lru_lambda_2"][l]))]
    t = prow[:, 5 + 2 * l, :]
    out += [(t[0:32, :], a["conv_w_2"][l].rearrange("k (t p) -> (k t) p", p=P))]
    return out


PAR_DMAS = LAYERS * (7 + 2 + 10 + 1 + 1)

_INS = ['x', 'ln_attn_g', 'w_in', 'qk_norm_g', 'diff_lambda', 'diff_subln_g', 'w_out', 'ln_ffn_g', 'w_up', 'conv_w',
        'conv_b', 'w_down', 'rel_bias', 'ffn1_norm_2', 'ffn1_w_gate_2', 'ffn1_w_up_2', 'ffn1_w_down_2', 'mix_norm_2',
        'w_in_2', 'b_in_2', 'q_norm_2', 'k_norm_2', 'conv_w_2', 'conv_b_2', 'lru_w_a_2', 'lru_b_a_2', 'lru_w_x_2',
        'lru_b_x_2', 'lru_lambda_2', 'w_o_attn_2', 'w_o_rnn_2', 'w_out_2', 'ffn2_norm_2', 'ffn2_w_gate_2',
        'ffn2_w_up_2', 'ffn2_w_down_2']


def shape_constants():
    import numpy as np
    j, k = np.arange(P)[:, None], np.arange(P)[None, :]
    c = np.zeros((P, K_N), np.float32)
    c[:, K_ID:K_ID + P] = j == k
    c[:, K_TRI:K_TRI + P] = j <= k
    c[:, K_ONEU:K_ONEU + P] = 1.0
    c[:, K_ONEU + P:K_ONEU + 2 * P] = j > k
    c[:, K_MASK + P:K_MASK + 2 * P] = np.where(k <= j, 0.0, NEG)
    sp = np.zeros((16, KT, P), np.float32)
    for t in range(KT):
        c[:64, K_G64 + 16 * t + 2 * t] = 1.0 / 64
        c[64:, K_G64 + 16 * t + 2 * t + 1] = 1.0 / 64
        c[:, K_G128 + 16 * t + 2 * t:K_G128 + 16 * t + 2 * t + 2] = 1.0 / 128
        sp[2 * t, t, :64] = 1.0
        sp[2 * t + 1, t, 64:] = 1.0
    c[:, K_MEAN:K_MEAN + P] = 1.0 / D
    dist = np.arange(SEQ)
    exact = BUCKETS // 2
    far = np.maximum(dist, exact).astype(np.float32) / np.float32(exact)
    far = exact + (np.log(far) / np.float32(math.log(1024 / exact)) * np.float32(BUCKETS - exact)).astype(np.int32)
    bucket = np.where(dist < exact, dist, np.minimum(far, BUCKETS - 1))
    onehot = np.zeros((BUCKETS, 384), np.float32)
    onehot[bucket, SEQ - 1 - dist] = 1.0
    flip = np.ascontiguousarray(np.eye(P, dtype=np.float32)[::-1])
    return {"const_main": c, "const_spread": sp.reshape(16, KT * P), "const_onehot": onehot, "const_flip": flip}


def kernel(**inputs):
    import numpy as np
    import concourse.bacc as bacc
    from concourse.bass_utils import run_bass_kernel_spmd

    nc = bacc.Bacc("TRN2", target_bir_lowering=False, num_devices=1)
    arrays, aps = {}, {}
    for name, value in [(n, inputs[n]) for n in _INS] + list(shape_constants().items()):
        value = np.ascontiguousarray(value)
        arrays[f"in_{name}"] = value
        aps[name] = nc.dram_tensor(f"in_{name}", value.shape, mybir.dt.from_np(value.dtype), kind="ExternalInput").ap()
    out = nc.dram_tensor("out_0", (1, SEQ, D), F32, kind="ExternalOutput").ap()
    build_program(nc, aps, out)
    r = run_bass_kernel_spmd(nc, [arrays], core_ids=[0])
    return r.results[0]["out_0"]
```

```python
import math
from contextlib import ExitStack

import concourse.bass as bass
from concourse import mybir

F32 = mybir.dt.float32
F32R = mybir.dt.float32r
BF16 = mybir.dt.bfloat16
ALU = mybir.AluOpType
ACT = mybir.ActivationFunctionType
AX_X = mybir.AxisListType.X

P = 128
LAYERS = 2
SEQ = 256
TB = SEQ // P
D = 1024
KT = D // P
F = 2816
FT = F // P
UW = 256
UNIT = KT * UW
STEPS = F // UW
NS = 3
EPS = 1e-6
NEG = -1e30
BUCKETS = 32
BIAS_HEADS = 12
DIFF_HEADS = 4
HD1 = 64
HD2 = 128
H2 = 8
LRU_C = 8.0
QKV2 = 3 * D
REST2 = QKV2 + H2
LAM_INIT = [0.8 - 0.6 * math.exp(-0.3 * i) for i in range(LAYERS)]

SKIP = 2
V1_WIN, V1_WOUT, V1_FFN = 0, 14, 18
V1 = 51
V2_FFN1, V2_WIN, V2_GATED, V2_WOUT, V2_FFN2 = 0, 33, 55, 71, 75
V2 = 108
LAST_BEFORE_SKIP = {1: 11, 2: 52}
O1_WIN, O1_WOUT, O1_FFN, O1 = 0, 12, 16, 38
O2_FFN1, O2_WIN, O2_GATED, O2_WOUT, O2_FFN2, O2 = 0, 22, 42, 58, 62, 84

C1_ATTN, C1_FFN, C1_SUB, C1_QK, C1_CONV, C1 = 0, 8, 16, 17, 21, 197
C2_FFN1, C2_MIX, C2_FFN2, C2_BQK, C2_BREST, C2_QN, C2_KN = 0, 8, 16, 24, 40, 72, 73
C2_CB, C2_BA, C2_BX, C2_LAM, C2_CONV, C2_POS, C2 = 74, 82, 90, 98, 106, 138, 146

K_ID, K_TRI, K_ONEU, K_MASK, K_G64, K_G128, K_MEAN, K_N = 0, 128, 256, 512, 768, 896, 1024, 1152


class Signal:

    def __init__(self, sem, per1, per2, credit=0):
        self.sem, self.per, self.credit = sem, {1: per1, 2: per2}, credit

    def at(self, where, k):
        block, layer = where
        before = self.credit + (LAYERS * self.per[1] if block == 2 else 0)
        return layer * self.per[block] + (before + k)


class Chain:

    def __init__(self, eng, sem):
        self.eng, self.sem, self.n = eng, sem, 0

    def link(self, ins):
        self.n += 1
        ins.then_inc(self.sem, 1)
        return self.n

    def wait(self, n=None):
        self.eng.wait_ge(self.sem, self.n if n is None else n)

    def tick(self):
        self.eng.sem_inc(self.sem, 1)
        self.n += 1

    def restart(self):
        if self.n:
            self.wait()
            self.eng.sem_clear(self.sem)
            self.n = 0


def build_program(nc, a, out):
    with ExitStack() as ctx:
        def sb(name, shape, dt=F32):
            return ctx.enter_context(nc.sbuf_tensor(name, shape, dt))

        def sem(name):
            return ctx.enter_context(nc.semaphore(name))

        raw = sb("raw", [P, NS, UNIT])
        w_hi = sb("w_hi", [P, NS, UNIT], F32R)
        w_lo = sb("w_lo", [P, NS, UNIT], F32R)
        x = sb("x", [P, KT, SEQ])
        h_hi, h_lo = sb("h_hi", [P, KT, SEQ], F32R), sb("h_lo", [P, KT, SEQ], F32R)
        y_hi, y_lo = sb("y_hi", [P, KT, SEQ], F32R), sb("y_lo", [P, KT, SEQ], F32R)
        r_hi, r_lo = sb("r_hi", [P, KT, SEQ], F32R), sb("r_lo", [P, KT, SEQ], F32R)
        g_hi = sb("g_hi", [P, 2, 2, SEQ], F32R)
        g_lo = sb("g_lo", [P, 2, 2, SEQ], F32R)
        qk = sb("qk", [P, 16, SEQ])
        v = sb("v", [P, TB, D])
        t4 = sb("t4", [P, 4, SEQ])
        tmp = sb("tmp", [P, 3072])
        big = sb("big", [P, 3072])
        cst = sb("cst", [P, K_N])
        spread = sb("spread", [16, KT * P])
        par1 = sb("par1", [P, LAYERS, C1])
        par2 = sb("par2", [P, LAYERS, C2])
        cur = sb("cur", [P, C1])
        prm = sb("prm", [P, 2, 4, 2, 2])
        wf_raw = sb("wf_raw", [P, LAYERS, KT, H2])
        wf_hi = sb("wf_hi", [P, LAYERS, KT, H2], F32R)
        wf_lo = sb("wf_lo", [P, LAYERS, KT, H2], F32R)
        bf = sb("bf", [P, LAYERS, TB * H2])
        zeros = sb("zeros", [1, 512], BF16)
        eps = sb("eps", [P, 1])
        neglam = sb("neglam", [P, LAYERS])
        std = sb("std", [P, SEQ])
        rstd = sb("rstd", [P, SEQ])
        warm = sb("warm", [1, 1])
        nmax = sb("nmax", [P, 2, 4])
        esum = sb("esum", [P, 2, 4])
        esc = sb("esc", [P, 2, 4])
        lgs = sb("lgs", [P, 8, 16])
        lf = sb("lf", [P, TB * H2])

        ident, tri = cst[:, K_ID:K_ID + P], cst[:, K_TRI:K_TRI + P]
        one_u = cst[:, K_ONEU:K_ONEU + 256]
        mask = cst[:, K_MASK:K_MASK + 256]
        g64, g128 = cst[:, K_G64:K_G64 + P], cst[:, K_G128:K_G128 + P]
        mean = cst[:, K_MEAN:K_MEAN + P]
        bias = big[:, :].rearrange("p (h k) -> p h k", h=BIAS_HEADS)
        bv = big[:, 0:D]
        lin_a = big[:, D:D + KT * P].rearrange("p (t c) -> p t c", t=KT)
        lin_x = big[:, 2 * D:2 * D + KT * P].rearrange("p (t c) -> p t c", t=KT)

        def pair512(at):
            return tmp[:, at:at + 512].rearrange("p (m s) -> p m s", m=2)

        gate_s, up_s, prod_s = pair512(0), pair512(512), pair512(1024)
        lru_x, lru_c, lru_g, lru_r, lru_i, lru_a = (pair512(512 * n) for n in range(6))
        sig_s = bv[:, 0:512].rearrange("p (m s) -> p m s", m=2)
        part_s = bv[:, 512:1024].rearrange("p (m s) -> p m s", m=2)
        probs = tmp[:, 0:1536].rearrange("p (e m k) -> p e m k", e=2, m=2)
        probs_t = tmp[:, 1536:2304].rearrange("p (m k) -> p m k", m=2)
        t4_flat = t4[:, :, :].rearrange("p t s -> p (t s)")
        decay = [tmp[:, 2304:3072].rearrange("p (m k) -> p m k", m=2),
                 t4_flat[:, 0:768].rearrange("p (m k) -> p m k", m=2)]
        x_tok = v
        prow = tmp[:, 0:1024].rearrange("p (n l c) -> p n l c", n=4, l=LAYERS)
        dlam = tmp[:, 1024:1536]
        dprod = tmp[:, 1536:1792].rearrange("p (n d) -> p n d", n=4)
        qk_flat = qk[:, :, :].rearrange("p t s -> p (t s)")
        onehot, relb = qk_flat[0:BUCKETS, 3072:3456], qk_flat[0:BUCKETS, 3456:3468]
        tsb = qk_flat[0:BIAS_HEADS, 3468:3852]
        by_dist = nc.dram_tensor("by_dist", (BIAS_HEADS, 384), F32, kind="Internal").ap()

        bank = [ctx.enter_context(nc.psum_tensor(f"bank{i}", [P, 512], F32)) for i in range(8)]

        def acc(m):
            return bank[4 + m // 2][:, (m % 2) * SEQ:(m % 2 + 1) * SEQ]

        raw_full = [sem(f"raw_full{s}") for s in range(NS)]
        hi_ready = Signal(sem("hi_ready"), V1, V2)
        lo_ready = Signal(sem("lo_ready"), V1, V2, credit=NS)
        unit_done = Signal(sem("unit_done"), V1, V2, credit=NS)
        evacuated = Signal(sem("evacuated"), O1, O2, credit=2)
        x_ready = Signal(sem("x_ready"), 2 * KT, 3 * KT)
        sq_ready = Signal(sem("sq_ready"), 2 * KT, 3 * KT)
        sq_used = Signal(sem("sq_used"), 2 * KT, 3 * KT)
        std_ready = Signal(sem("std_ready"), 2, 3)
        hf_ready = Signal(sem("hf_ready"), 2 * KT, 3 * KT)
        hh_ready = Signal(sem("hh_ready"), 2 * KT, 3 * KT)
        h_ready = Signal(sem("h_ready"), 2 * KT, 3 * KT)
        gsq_ready = Signal(sem("gsq_ready"), 8, 8)
        gsq_used = Signal(sem("gsq_used"), 8, 8, credit=2)
        gstd_ready = Signal(sem("gstd_ready"), 3, 2)
        grstd_ready = Signal(sem("grstd_ready"), 3, 2)
        bc_done = Signal(sem("bc_done"), 10, 8)
        bc_used = Signal(sem("bc_used"), 10, 8, credit=2)
        scored = Signal(sem("scored"), 8, 4)
        logits_ready = Signal(sem("logits_ready"), 8, 4, credit=1)
        exp_ready = Signal(sem("exp_ready"), 8, 4)
        probs_ready = Signal(sem("probs_ready"), 8, 4)
        turned = Signal(sem("turned"), 8, 4, credit=2)
        pt_ready = Signal(sem("pt_ready"), 8, 4, credit=1)
        pv_done = Signal(sem("pv_done"), 8, 4, credit=1)
        att_hi = Signal(sem("att_hi"), 4, 4, credit=1)
        att_out = Signal(sem("att_out"), 8, 4, credit=1)
        dsq_ready = Signal(sem("dsq_ready"), 1, 0)
        dsq_used = Signal(sem("dsq_used"), 1, 0)
        dn_ready = Signal(sem("dn_ready"), 4, 0)
        dn_hi = Signal(sem("dn_hi"), 4, 0)
        y_ready = Signal(sem("y_ready"), 1, 1)
        prm_ready = Signal(sem("prm_ready"), STEPS, 0)
        conv_main = Signal(sem("conv_main"), 2 * STEPS, 0)
        silu_ready = Signal(sem("silu_ready"), STEPS, 2 * STEPS)
        prod_ready = Signal(sem("prod_ready"), STEPS, 2 * STEPS)
        prod_hi = Signal(sem("prod_hi"), STEPS, 2 * STEPS)
        g_ready = Signal(sem("g_ready"), STEPS, 2 * STEPS)
        acc_done = Signal(sem("acc_done"), 3, 6)
        cur_ready = Signal(sem("cur_ready"), 1, 1)
        lru_conv = Signal(sem("lru_conv"), 0, 4)
        lru_lin = Signal(sem("lru_lin"), 0, 4)
        lru_gates = Signal(sem("lru_gates"), 0, 4)
        lru_m = Signal(sem("lru_m"), 0, 4)
        lru_sqrt = Signal(sem("lru_sqrt"), 0, 4)
        lru_y = Signal(sem("lru_y"), 0, 4)
        lru_hi = Signal(sem("lru_hi"), 0, 4)
        r_ready = Signal(sem("r_ready"), 0, 4)
        f_done = Signal(sem("f_done"), 0, 1)
        f_abs = Signal(sem("f_abs"), 0, 1)
        f_exp = Signal(sem("f_exp"), 0, 1)
        f_ready = Signal(sem("f_ready"), 0, 1)
        decay_ready = Signal(sem("decay_ready"), 0, 4)
        sig_ready = Signal(sem("sig_ready"), 0, 8)
        merged_ready = Signal(sem("merged_ready"), 0, 4)
        merged_hi = Signal(sem("merged_hi"), 0, 4)
        m_ready = Signal(sem("m_ready"), 0, 4)
        side_loaded = Signal(sem("side_loaded"), 0, 1)
        lin_cleared = sem("lin_cleared")
        ld_x, ld_cst, ld_rel, ld_wf = (sem(n) for n in ("ld_x", "ld_cst", "ld_rel", "ld_wf"))
        ld_par = [sem(f"ld_par{k}") for k in range(4)]
        ld_bias, st_by_dist, st_out = sem("ld_bias"), sem("st_by_dist"), sem("st_out")
        pro_pe, pro_dve, pro_act = sem("pro_pe"), sem("pro_dve"), sem("pro_act")
        fin_pe, fin_sb = sem("fin_pe"), sem("fin_sb")
        dve_own, act_own, pool_own = sem("dve_own"), sem("act_own"), sem("pool_own")
        loads_issued = sem("loads_issued")

        def full_at(where, vv, i):
            block, layer = where
            per = {1: V1, 2: V2}[block]
            if vv >= per:
                return full_at((block, layer + 1), vv - per, i)
            s = vv % NS
            skipped = [u % NS for u in range(LAST_BEFORE_SKIP[block] + 1, LAST_BEFORE_SKIP[block] + 1 + SKIP)]
            behind = vv > LAST_BEFORE_SKIP[block]
            uses = vv // NS - (behind and s in skipped)
            each = per // NS - (s in skipped)
            skipped1 = [u % NS for u in range(LAST_BEFORE_SKIP[1] + 1, LAST_BEFORE_SKIP[1] + 1 + SKIP)]
            before = LAYERS * (V1 // NS - (s in skipped1)) if block == 2 else 0
            return layer * (16 * each) + i * (16 * 6 // NS) + 16 * (before + uses + 1)

        def raises(block, vv):
            return 1 + SKIP if vv == LAST_BEFORE_SKIP[block] else 1

        block_ = ctx.enter_context(nc.Block())

        @block_.sync
        def _(sp):
            sp.dma_start(x_tok[:, :, :], a["x"].rearrange("a (b p) d -> (a p) b d", p=P)).then_inc(ld_x, 16)
            sp.dma_start(cst[:, :], a["const_main"]).then_inc(ld_cst, 16)
            sp.dma_start(spread[:, :], a["const_spread"]).then_inc(ld_cst, 16)

            def slot(where, vv, i, src, rows):
                s = vv % NS
                sp.wait_ge(lo_ready.sem, lo_ready.at(where, vv + 1 - NS) + i * 6)
                sp.sem_inc(loads_issued, 1)
                dst = raw[:, s, :].rearrange("p (k m) -> p k m", k=rows)
                sp.dma_start(dst, src).then_inc(raw_full[s], 16)

            def cols(where, vv, w, col, i=0, step=0):
                wv = w.rearrange("l (k p) m -> l p k m", p=P)
                at = i * step + col
                src = wv[bass.ds(where[1], 1), :, :, bass.ds(at, UW)].rearrange("l p k m -> (l p) k m")
                slot(where, vv, i, src, KT)

            def rows(where, vv, w, tile, i=0, step=0):
                wv = w.rearrange("l (t p) m -> l p t m", p=P)
                at = i * step + tile
                src = wv[bass.ds(where[1], 1), :, bass.ds(at, 2), :].rearrange("l p t m -> (l p) t m")
                slot(where, vv, i, src, 2)

            def ffn(where, vv, gate, up, up_col, down):
                cols(where, vv, gate, 0)
                cols(where, vv + 1, up, up_col)
                with sp.Fori(0, STEPS // 2) as i:
                    for e in range(2):
                        cols(where, vv + 2 + 3 * e, gate, UW * (e + 1), i, 2 * UW)
                        cols(where, vv + 3 + 3 * e, up, up_col + UW * (e + 1), i, 2 * UW)
                        rows(where, vv + 4 + 3 * e, down, 2 * e, i, 4)
                rows(where, vv + 3 * STEPS - 1, down, 2 * (STEPS - 1))

            with sp.Fori(0, LAYERS) as l:
                where = (1, l)
                for u in range(12):
                    cols(where, V1_WIN + u, a["w_in"], UW * u)
                for u in range(4):
                    cols(where, V1_WOUT + u, a["w_out"], UW * u)
                ffn(where, V1_FFN, a["w_up"], a["w_up"], F, a["w_down"])
            with sp.Fori(0, LAYERS) as l:
                where = (2, l)
                ffn(where, V2_FFN1, a["ffn1_w_gate_2"], a["ffn1_w_up_2"], 0, a["ffn1_w_down_2"])
                w = a["w_in_2"]
                for j in range(4):
                    cols(where, V2_WIN + 3 * j, w, REST2 + UW * j)
                    cols(where, V2_WIN + 3 * j + 1, w, REST2 + D + UW * j)
                    cols(where, V2_WIN + 3 * j + 2, w, UW * j)
                for j in range(8):
                    cols(where, V2_WIN + 12 + j, w, D + UW * j)
                for n, o in ((3, "w_o_rnn_2"), (2, "w_o_attn_2")):
                    for j in range(4):
                        at = V2_GATED + 8 * (3 - n) + 2 * j
                        cols(where, at, w, REST2 + n * D + UW * j)
                        cols(where, at + 1, a[o], UW * j)
                for u in range(4):
                    cols(where, V2_WOUT + u, a["w_out_2"], UW * u)
                ffn(where, V2_FFN2, a["ffn2_w_gate_2"], a["ffn2_w_up_2"], 0, a["ffn2_w_down_2"])
            sp.wait_ge(fin_sb, 4)
            sp.dma_start(out.rearrange("a (b p) d -> (a p) b d", p=P), x_tok[:, :, :]).then_inc(st_out, 16)
            sp.wait_ge(st_out, 16)

        @block_.gpsimd
        def _(pool):
            nc.gpsimd.memset(zeros[:, :], 0.0).then_inc(ld_cst, 1)
            nc.gpsimd.memset(eps[:, :], EPS).then_inc(ld_cst, 1)
            pool.dma_start(onehot, a["const_onehot"]).then_inc(ld_rel, 16)
            pool.dma_start(relb, a["rel_bias"]).then_inc(ld_rel, 16)
            pool.wait_ge(pro_dve, 9)
            pool.dma_start(by_dist, tsb).then_inc(st_by_dist, 16)
            pool.wait_ge(st_by_dist, 16)
            pool.dma_start(bias, bass.AP(by_dist.tensor, by_dist.offset, [[1, P], [384, BIAS_HEADS], [1, 256]])
                           ).then_inc(ld_bias, 16)
            with pool.Fori(0, LAYERS) as l:
                where = (2, l)
                pool.wait_ge(cur_ready.sem, cur_ready.at(where, 1))
                pool.wait_ge(lin_cleared, 2)
                bsrc = a["b_in_2"][bass.ds(l, 1), 2 * D:3 * D].rearrange("l d -> (l d)").partition_broadcast(P)
                pool.dma_start(bv, bsrc).then_inc(side_loaded.sem, 16)
                for dst, name in ((lin_a, "lru_w_a_2"), (lin_x, "lru_w_x_2")):
                    wv = a[name].rearrange("l (t e) c d -> l e c t d", e=2)
                    for e in range(2):
                        src = wv[bass.ds(l, 1), e, :, :, :].rearrange("l c t d -> (l c) t d")
                        pool.dma_start(dst[64 * e:64 * e + 64, :, 64 * e:64 * e + 64], src
                                       ).then_inc(side_loaded.sem, 16)
                pool.wait_ge(f_ready.sem, f_ready.at(where, 1))
                pool.wait_ge(r_ready.sem, r_ready.at(where, 4))
                for p in range(4):
                    if p == 1:
                        pool.wait_ge(gsq_used.sem, gsq_used.at(where, 8))
                    if p >= 2:
                        pool.wait_ge(scored.sem, scored.at(where, p - 1))
                    pool.sem_inc(pool_own, 1)
                    for m in range(2):
                        h = 2 * p + m
                        dst = decay[p % 2]
                        nc.gpsimd.tensor_scalar(dst[:, m, 0:256], one_u, lf[:, H2 + h:H2 + h + 1], 1.0,
                                                ALU.mult, ALU.mult)
                        last = nc.gpsimd.tensor_scalar(dst[:, m, 256:384], one_u[:, 128:256], lf[:, h:h + 1], 1.0,
                                                       ALU.mult, ALU.mult)
                    last.then_inc(decay_ready.sem, 1)

        @block_.tensor
        def _(pe):
            def three(out_, lh, ll, rh, rl, start, stop):
                pe.matmul(out_, lh, rh, start=start, stop=False, skip_group_check=True)
                pe.matmul(out_, lh, rl, start=False, stop=False, skip_group_check=True)
                return pe.matmul(out_, ll, rh, start=False, stop=stop, skip_group_check=True)

            def begin(where, vv, o, i=0, ostep=0, banks=2):
                pe.wait_ge(lo_ready.sem, lo_ready.at(where, vv + 1) + i * 6)
                if o is not None:
                    pe.wait_ge(evacuated.sem, evacuated.at(where, o + 1 - banks) + i * ostep)

            def unit(where, vv, o, b, oh, ol, i=0, ostep=0, banks=2):
                begin(where, vv, o, i, ostep, banks)
                s = vv % NS
                for m in range(2):
                    for k in range(KT):
                        c = k * UW + m * P
                        mm = three(bank[b][:, m * SEQ:(m + 1) * SEQ], w_hi[:, s, c:c + P], w_lo[:, s, c:c + P],
                                   oh[:, k, :], ol[:, k, :], k == 0, k == KT - 1)
                mm.then_inc(unit_done.sem, raises(where[0], vv))

            def unit_tok(where, vv, o, b):
                begin(where, vv, o)
                s = vv % NS
                for t in range(TB):
                    for k in range(KT):
                        mm = three(bank[b][:, t * UW:(t + 1) * UW], h_hi[:, k, t * P:(t + 1) * P],
                                   h_lo[:, k, t * P:(t + 1) * P], w_hi[:, s, k * UW:(k + 1) * UW],
                                   w_lo[:, s, k * UW:(k + 1) * UW], k == 0, k == KT - 1)
                mm.then_inc(unit_done.sem, raises(where[0], vv))

            def clear_acc():
                for b in range(4, 8):
                    pe.matmul(bank[b][:, :], zeros[:, 0:P], zeros[:, :], start=True, stop=False,
                              skip_group_check=True)

            def down(where, vv, par, step, i=0):
                begin(where, vv, None, i)
                pe.wait_ge(g_ready.sem, g_ready.at(where, step + 1) + i * 2)
                s = vv % NS
                for t in range(2):
                    for m in range(KT):
                        c = t * D + m * P
                        mm = three(acc(m), w_hi[:, s, c:c + P], w_lo[:, s, c:c + P],
                                   g_hi[:, par, t, :], g_lo[:, par, t, :], False, False)
                mm.then_inc(unit_done.sem, 1)

            def first_units(where, vv, o, norm):
                begin(where, vv, o)
                begin(where, vv + 1, o + 1)
                for k in range(KT):
                    pe.wait_ge(h_ready.sem, h_ready.at(where, norm * KT + k + 1))
                    for u in range(2):
                        s = (vv + u) % NS
                        for m in range(2):
                            c = k * UW + m * P
                            mm = three(bank[u][:, m * SEQ:(m + 1) * SEQ], w_hi[:, s, c:c + P],
                                       w_lo[:, s, c:c + P], h_hi[:, k, :], h_lo[:, k, :],
                                       k == 0 and m == 0, k == KT - 1)
                        if k == KT - 1:
                            mm.then_inc(unit_done.sem, 1)

            def last_down(where, vv, step, done, norm):
                begin(where, vv, None)
                pe.wait_ge(g_ready.sem, g_ready.at(where, step + 1))
                s = vv % NS
                for c in range(4):
                    for m in (2 * c, 2 * c + 1):
                        for t in range(2):
                            w = t * D + m * P
                            mm = three(acc(m), w_hi[:, s, w:w + P], w_lo[:, s, w:w + P],
                                       g_hi[:, 0, t, :], g_lo[:, 0, t, :], False, t == 1)
                    mm.then_inc(acc_done.sem if c < 3 else unit_done.sem, 1)
                    if c:
                        norm_sums(where, norm, 2 * c - 2)
                norm_sums(where, norm, 6)

            def ffn(where, vv, o, norm, steps0):
                clear_acc()
                first_units(where, vv, o, norm)
                with pe.Fori(0, STEPS // 2) as i:
                    for e in range(2):
                        b = 2 * ((e + 1) % 2)
                        unit(where, vv + 2 + 3 * e, o + 2 + 2 * e, b, h_hi, h_lo, i, 4, 4)
                        unit(where, vv + 3 + 3 * e, o + 3 + 2 * e, b + 1, h_hi, h_lo, i, 4, 4)
                        down(where, vv + 4 + 3 * e, e, steps0 + e, i)
                last_down(where, vv + 3 * STEPS - 1, steps0 + STEPS - 1, 0, norm + 1)

            def norm_sums(where, n, t0):
                for t in (t0, t0 + 1):
                    pe.wait_ge(sq_ready.sem, sq_ready.at(where, n * KT + t + 1))
                    pe.matmul(bank[2][:, 0:SEQ], mean, t4[:, t % 4, :], start=(t == 0), stop=(t == KT - 1),
                              skip_group_check=True).then_inc(sq_used.sem, 1)

            def out_units(where, vv, o, norm, oh, ol):
                for u in range(4):
                    unit(where, vv + u, o + u, u % 2, oh, ol)
                    if u:
                        norm_sums(where, norm, 2 * u - 2)
                norm_sums(where, norm, 6)

            def group_sums(where, n, sel):
                if n % 4 == 0 and n:
                    pe.wait_ge(gstd_ready.sem, gstd_ready.at(where, n // 4))
                pe.wait_ge(gsq_ready.sem, gsq_ready.at(where, n + 1))
                for m in range(2):
                    t = 2 * (n % 4) + m
                    mm = pe.matmul(bank[3][0:16, 0:SEQ], sel[:, 16 * t:16 * t + 16], t4[:, 2 * (n % 2) + m, :],
                                   start=(t == 0), stop=(t == KT - 1))
                mm.then_inc(gsq_used.sem, 1)

            def group_spread(where, n, q0, groups, banks):
                pe.wait_ge(grstd_ready.sem, grstd_ready.at(where, n + 1))
                for q, c in enumerate(groups, q0):
                    pe.wait_ge(bc_used.sem, bc_used.at(where, q - 1))
                    for m in range(2):
                        t = 2 * c + m
                        mm = pe.matmul(bank[banks[q % 2]][:, m * SEQ:(m + 1) * SEQ], spread[:, t * P:(t + 1) * P],
                                       rstd[0:16, :], start=True, stop=True)
                    mm.then_inc(bc_done.sem, 1)

            def scores(where, p):
                b, _ = where
                pe.wait_ge(logits_ready.sem, logits_ready.at(where, p))
                for m in range(2):
                    s = bank[4 + m]
                    if b == 1:
                        qt, kt = (p, 4 + p) if p < 4 else (8 + p - 4, 12 + p - 4)
                        r = slice(64 * m, 64 * m + 64)
                    else:
                        qt, kt = 2 * p + m, 8 + 2 * p + m
                        r = slice(0, P)
                    mm = pe.matmul(s[:, 0:256], qk[r, qt, 128:256], qk[r, kt, 0:256], start=True,
                                   stop=(b == 1), skip_group_check=True)
                    if b == 2:
                        if m == 0:
                            pe.wait_ge(decay_ready.sem, decay_ready.at(where, p + 1))
                        dc = decay[p % 2]
                        pe.matmul(s[:, 0:256], tri, dc[:, m, 0:256], start=False, stop=False,
                                  skip_group_check=True)
                        pe.matmul(s[:, 0:128], one_u[:, 0:128], dc[:, m, 256:384], start=False, stop=True,
                                  skip_group_check=True)
                    mm = pe.matmul(s[:, 256:384], qk[r, qt, 0:128], qk[r, kt, 0:128], start=True,
                                   stop=(b == 1), skip_group_check=True)
                    if b == 2:
                        mm = pe.matmul(s[:, 256:384], tri, dc[:, m, 256:384], start=False, stop=True,
                                       skip_group_check=True)
                mm.then_inc(scored.sem, 1)

            def turn(where, p):
                pe.wait_ge(probs_ready.sem, probs_ready.at(where, p + 1))
                pe.wait_ge(pt_ready.sem, pt_ready.at(where, p))
                maps = 1 if where[0] == 1 and p < 4 else 2
                for m in range(maps):
                    e = probs[:, p % 2, m, :]
                    for c, at in ((0, 256), (1, 0), (2, 128)):
                        mm = pe.transpose(bank[6 + m][:, 128 * c:128 * c + 128], e[:, at:at + 128], ident)
                mm.then_inc(turned.sem, 1)

            def weigh(where, p):
                pe.wait_ge(pt_ready.sem, pt_ready.at(where, p + 1))
                pe.wait_ge(att_out.sem, att_out.at(where, p))
                for m in range(2):
                    if where[0] == 1 and p < 4:
                        if m:
                            break
                        o, c0, n = bank[2][:, :], p * P, P
                    elif where[0] == 1:
                        o, c0, n = bank[2][64 * m:64 * m + 64, :], 512 + (2 * (p - 4) + m) * 64, 64
                    else:
                        o, c0, n = bank[2 + m][:, :], (2 * p + m) * P, P
                    pe.matmul(o[:, 0:256], v[:, 0, c0:c0 + n], probs_t[:, m, 0:256], start=True, stop=False,
                              skip_group_check=True)
                    mm = pe.matmul(o[:, 128:256], v[:, 1, c0:c0 + n], probs_t[:, m, 256:384], start=False,
                                   stop=True, skip_group_check=True)
                mm.then_inc(pv_done.sem, 1)

            def rest_of_attention(where, p0, pairs):
                for p in range(p0, pairs):
                    turn(where, p)
                    if p + 2 < pairs:
                        scores(where, p + 2)
                    weigh(where, p)
                    if p == 4:
                        pe.wait_ge(dsq_ready.sem, dsq_ready.at(where, 1))
                        for t in range(4):
                            mm = pe.matmul(bank[3][0:16, 0:SEQ], g128[:, 16 * t:16 * t + 16], t4[:, t, :],
                                           start=(t == 0), stop=(t == 3))
                        mm.then_inc(dsq_used.sem, 1)
                    if p == 6:
                        group_spread(where, 2, 8, (0, 1), (0, 1))

            pe.wait_ge(ld_cst, 34)
            pe.wait_ge(ld_x, 16)
            for c in range(4):
                for m in range(2):
                    for t in range(TB):
                        mm = pe.transpose(bank[c][:, m * SEQ + t * P:m * SEQ + (t + 1) * P],
                                          x_tok[:, t, (2 * c + m) * P:(2 * c + m + 1) * P], ident)
                mm.then_inc(pro_pe, 1)
            mm = pe.matmul(bank[7][:, :], zeros[:, 0:P], zeros[:, :], start=True, stop=True)
            mm.then_inc(unit_done.sem, NS)
            for k in range(4):
                pe.wait_ge(ld_par[k], 16 * PAR_DMAS[k])
                for l in range(LAYERS):
                    nr = PAR_ROWS[k]
                    mm = pe.transpose(bank[4 + k][:, 128 * l:128 * l + nr], prow[0:nr, k, l, :], ident[0:nr, 0:nr])
                mm.then_inc(pro_pe, 1)
                if k == 1:
                    pe.wait_ge(pro_dve, 4)
                    for t0 in (0, 2, 4, 6):
                        norm_sums((1, 0), 0, t0)
            pe.wait_ge(ld_rel, 32)
            pe.matmul(bank[3][0:BIAS_HEADS, 0:384], relb, onehot, start=True, stop=True).then_inc(pro_pe, 1)

            with pe.Fori(0, LAYERS) as l:
                where = (1, l)
                first_units(where, V1_WIN, O1_WIN, 0)
                for u in range(2, 12):
                    vv, o, b = V1_WIN + u, O1_WIN + u, u % 2
                    if u == 6:
                        unit(where, vv, o, b, h_hi, h_lo)
                        group_spread(where, 0, 0, (0, 2), (6, 7))
                        continue
                    if u % 6 < 4:
                        unit(where, vv, o, b, h_hi, h_lo)
                    else:
                        unit_tok(where, vv, o, b)
                    if u == 2:
                        group_sums(where, 0, g64)
                    if 1 <= u % 6 <= 4:
                        group_sums(where, 4 * (u // 6) + u % 6 - 1, g64)
                    if u == 7:
                        group_spread(where, 0, 2, (1, 3), (6, 7))
                        pe.wait_ge(bc_used.sem, bc_used.at(where, 2))
                        pe.wait_ge(evacuated.sem, evacuated.at(where, 6))
                        scores(where, 0)
                    if u == 8:
                        pe.wait_ge(bc_used.sem, bc_used.at(where, 4))
                        turn(where, 0)
                        scores(where, 1)
                    if u == 11:
                        group_spread(where, 1, 4, (0, 2), (3, 7))
                    if 9 <= u:
                        weigh(where, u - 9)
                        turn(where, u - 8)
                    if 9 <= u <= 10:
                        scores(where, u - 7)
                group_spread(where, 1, 6, (1, 3), (3, 7))
                pe.wait_ge(bc_used.sem, bc_used.at(where, 6))
                pe.wait_ge(evacuated.sem, evacuated.at(where, 12))
                scores(where, 4)
                weigh(where, 3)
                scores(where, 5)
                pe.wait_ge(bc_used.sem, bc_used.at(where, 8))
                rest_of_attention(where, 4, 8)
                pe.wait_ge(y_ready.sem, y_ready.at(where, 1))
                out_units(where, V1_WOUT, O1_WOUT, 1, y_hi, y_lo)
                ffn(where, V1_FFN, O1_FFN, 1, 0)

            with pe.Fori(0, LAYERS) as l:
                where = (2, l)
                ffn(where, V2_FFN1, O2_FFN1, 0, 0)

                def lru_linear(j):
                    if j == 0:
                        pe.wait_ge(side_loaded.sem, l * 80 + 80)
                    pe.wait_ge(lru_conv.sem, lru_conv.at(where, j + 1))
                    for b, lin in ((4, lin_a), (5, lin_x)):
                        for m in range(2):
                            mm = pe.matmul(bank[b][:, m * SEQ:(m + 1) * SEQ], lin[:, 2 * j + m, :],
                                           lru_c[:, m, :], start=True, stop=True)
                    mm.then_inc(lru_lin.sem, 1)

                def forget_logits():
                    for t in range(TB):
                        for k in range(KT):
                            wh = wf_hi[:, bass.ds(l, 1), k, :].rearrange("p l h -> p (l h)")
                            wl = wf_lo[:, bass.ds(l, 1), k, :].rearrange("p l h -> p (l h)")
                            mm = three(bank[2][:, t * H2:(t + 1) * H2], h_hi[:, k, t * P:(t + 1) * P],
                                       h_lo[:, k, t * P:(t + 1) * P], wh, wl, k == 0, k == KT - 1)
                    mm.then_inc(f_done.sem, 1)

                for j in range(4):
                    vv, o = V2_WIN + 3 * j, O2_WIN + 3 * j
                    if j == 0:
                        first_units(where, vv, o, 1)
                    else:
                        unit(where, vv, o, o % 2, h_hi, h_lo)
                        group_sums(where, j - 1, g128)
                        unit(where, vv + 1, o + 1, (o + 1) % 2, h_hi, h_lo)
                    unit(where, vv + 2, o + 2, (o + 2) % 2, h_hi, h_lo)
                    lru_linear(j)
                for j in range(4):
                    o = O2_WIN + 12 + j
                    unit(where, V2_WIN + 12 + j, o, o % 2, h_hi, h_lo)
                    group_sums(where, 3 + j, g128)
                    if j == 0:
                        forget_logits()
                    if j >= 2:
                        group_spread(where, 0, 2 * j - 4, (2 * j - 4, 2 * j - 3), (6, 7))
                for j in range(4):
                    o = O2_WIN + 16 + j
                    unit_tok(where, V2_WIN + 16 + j, o, o % 2)
                    if j == 0:
                        group_sums(where, 7, g128)
                    if 1 <= j <= 2:
                        group_spread(where, 1, 2 + 2 * j, (2 * j - 2, 2 * j - 1), (6, 7))
                    if j == 2:
                        pe.wait_ge(bc_used.sem, bc_used.at(where, 5))
                        scores(where, 0)
                    if j == 3:
                        pe.wait_ge(bc_used.sem, bc_used.at(where, 8))
                        turn(where, 0)
                        scores(where, 1)
                for j in range(8):
                    vv, o = V2_GATED + 2 * j, O2_GATED + 2 * j
                    unit(where, vv, o, 0, h_hi, h_lo)
                    if j == 0:
                        pe.wait_ge(evacuated.sem, evacuated.at(where, O2_GATED))
                        weigh(where, 0)
                        turn(where, 1)
                        scores(where, 2)
                        pe.wait_ge(r_ready.sem, r_ready.at(where, 4))
                    if j == 1:
                        weigh(where, 2)
                        turn(where, 3)
                    if j == 4:
                        pe.wait_ge(y_ready.sem, y_ready.at(where, 1))
                    oh, ol = (r_hi, r_lo) if j < 4 else (y_hi, y_lo)
                    unit(where, vv + 1, o + 1, 1, oh, ol)
                    if j == 0:
                        weigh(where, 1)
                        turn(where, 2)
                        scores(where, 3)
                    if j == 1:
                        weigh(where, 3)
                pe.wait_ge(m_ready.sem, m_ready.at(where, 4))
                out_units(where, V2_WOUT, O2_WOUT, 2, r_hi, r_lo)
                ffn(where, V2_FFN2, O2_FFN2, 2, STEPS)

            for c in range(4):
                pe.wait_ge(x_ready.sem, x_ready.at((2, LAYERS), 2 * c + 2))
                for m in range(2):
                    for t in range(TB):
                        mm = pe.transpose(bank[c][:, t * 256 + m * P:t * 256 + (m + 1) * P],
                                          x[:, 2 * c + m, t * P:(t + 1) * P], ident)
                mm.then_inc(fin_pe, 1)

        @block_.scalar
        def _(act):
            own = Chain(act, act_own)
            A = nc.scalar.activation

            def split_hi(where, vv, i=0):
                s = vv % NS
                act.wait_ge(raw_full[s], full_at(where, vv, i))
                act.wait_ge(unit_done.sem, unit_done.at(where, vv + 1 - NS) + i * 6)
                per = {1: V1, 2: V2}[where[0]]
                A(w_hi[:, s, :], raw[:, s, :], ACT.Copy).then_inc(hi_ready.sem, raises(where[0], vv % per))

            def next_hi(where, vv, i=0):
                skip = LAST_BEFORE_SKIP[where[0]]
                if not skip < vv + NS <= skip + SKIP:
                    split_hi(where, vv + NS, i)

            def guarded_hi(where, vv, i, last):
                if last is None:
                    next_hi(where, vv, i)
                else:
                    with act.If(last < LAYERS * (STEPS // 2) - 1):
                        next_hi(where, vv, i)

            def after_skip(where):
                for n in range(SKIP):
                    split_hi(where, LAST_BEFORE_SKIP[where[0]] + 1 + n + NS)

            def unit_wait(where, vv, i=0):
                act.wait_ge(unit_done.sem, unit_done.at(where, vv + 1) + i * 6)

            def squares(where, n, t0, count):
                if t0 == 0:
                    A(warm[:, :], eps[0:1, :], ACT.Sqrt)
                for t in range(t0, t0 + count):
                    act.wait_ge(x_ready.sem, x_ready.at(where, n * KT + t + 1))
                    if t >= 4:
                        act.wait_ge(sq_used.sem, sq_used.at(where, n * KT + t - 3))
                    A(t4[:, t % 4, :], x[:, t, :], ACT.Square).then_inc(sq_ready.sem, 1)

            def norm(where, n, vv):
                act.wait_ge(sq_used.sem, sq_used.at(where, n * KT + KT))
                A(std[:, :], bank[2][:, 0:SEQ], ACT.Sqrt, bias=eps[:, :]).then_inc(std_ready.sem, 1)
                for t in range(KT):
                    act.wait_ge(hf_ready.sem, hf_ready.at(where, n * KT + t + 1))
                    A(h_hi[:, t, :], t4[:, t % 4, :], ACT.Copy).then_inc(hh_ready.sem, 1)
                split_hi(where, vv + 2)

            def ffn1_step(where, vv, step, i=0):
                for half, dst in ((0, gate_s), (1, up_s)):
                    if half == 0:
                        act.wait_ge(prm_ready.sem, prm_ready.at(where, step + 1) + i * 2)
                    unit_wait(where, vv + half, i)
                    for m in range(2):
                        b = 2 * PAR(step) + half
                        last = A(dst[:, m, :], bank[b][:, m * SEQ:(m + 1) * SEQ], ACT.Identity,
                                 bias=prm[:, PAR(step), 0, half, m:m + 1], scale=prm[:, PAR(step), 1, half, m:m + 1])
                    last.then_inc(conv_main.sem, 1)
                    next_hi(where, vv + half, i)
                act.wait_ge(evacuated.sem, evacuated.at(where, O1_FFN + 2 * step + 1) + i * 4)
                A(gate_s, gate_s, ACT.Silu).then_inc(silu_ready.sem, 1)
                act.wait_ge(prod_ready.sem, prod_ready.at(where, step + 1) + i * 2)
                A(g_hi[:, PAR(step), :, :], prod_s, ACT.Copy).then_inc(prod_hi.sem, 1)

            def ffn2_step(where, vv, step, n, i=0, last=None):
                unit_wait(where, vv, i)
                b = 2 * PAR(step)
                A(gate_s, bank[b][:, :].rearrange("p (m s) -> p m s", m=2), ACT.Silu).then_inc(silu_ready.sem, 1)
                next_hi(where, vv, i)
                guarded_hi(where, vv + 1, i, last)
                act.wait_ge(prod_ready.sem, prod_ready.at(where, n + step + 1) + i * 2)
                A(g_hi[:, PAR(step), :, :], prod_s, ACT.Copy).then_inc(prod_hi.sem, 1)

            def ffn(where, vv, one_step, norm, last_layer=None):
                one_step(vv, 0, 0, None)
                own.restart()
                with act.Fori(0, STEPS // 2) as i:
                    for e in range(2):
                        last = None if last_layer is None or e == 0 else last_layer * (STEPS // 2) + i
                        one_step(vv + 2 + 3 * e, 1 + e, i, last)
                        guarded_hi(where, vv + 4 + 3 * e, i, last)
                    own.restart()
                squares(where, norm + 1, 0, KT)

            def group_std(where, n):
                act.wait_ge(gsq_used.sem, gsq_used.at(where, 4 * n + 4))
                if n:
                    act.wait_ge(grstd_ready.sem, grstd_ready.at(where, n))
                A(std[0:16, :], bank[3][0:16, 0:SEQ], ACT.Sqrt, bias=eps[0:16, :]).then_inc(gstd_ready.sem, 1)

            def exps(where, p):
                act.wait_ge(logits_ready.sem, logits_ready.at(where, p + 1))
                e = p % 2
                for m in range(2):
                    for c, cs in ((0, slice(0, 256)), (1, slice(256, 384))):
                        n = 2 * m + c
                        last = A(probs[:, e, m, cs], probs[:, e, m, cs], ACT.Exp, bias=nmax[:, e, n:n + 1],
                                 scale=-1.0, accum_out=esum[:, e, n:n + 1])
                last.then_inc(exp_ready.sem, 1)

            def copy_turned(where, p):
                act.wait_ge(turned.sem, turned.at(where, p + 1))
                act.wait_ge(pv_done.sem, pv_done.at(where, p))
                for m in range(1 if where[0] == 1 and p < 4 else 2):
                    last = A(probs_t[:, m, :], bank[6 + m][:, 0:384], ACT.Copy)
                last.then_inc(pt_ready.sem, 1)

            def att_high(where, p):
                act.wait_ge(pv_done.sem, pv_done.at(where, p + 1))
                if where[0] == 1 and p < 4:
                    A(qk[:, p, :], bank[2][:, 0:SEQ], ACT.Copy).then_inc(att_out.sem, 1)
                elif where[0] == 1:
                    A(y_hi[:, p, :], bank[2][:, 0:SEQ], ACT.Copy).then_inc(att_hi.sem, 1)
                else:
                    for m in range(2):
                        last = A(y_hi[:, 2 * p + m, :], bank[2 + m][:, 0:SEQ], ACT.Copy)
                    last.then_inc(att_hi.sem, 1)

            def rest_of_attention(where):
                act.wait_ge(att_out.sem, att_out.at(where, 4))
                A(t4[:, :, :], qk[:, 0:4, :], ACT.Square).then_inc(dsq_ready.sem, 1)
                exps(where, 4)
                exps(where, 5)
                for p in range(4, 8):
                    copy_turned(where, p)
                    if p + 2 < 8:
                        exps(where, p + 2)
                    if p == 7:
                        for t in range(4):
                            act.wait_ge(dn_ready.sem, dn_ready.at(where, t + 1))
                            A(y_hi[:, t, :], t4[:, t, :], ACT.Copy).then_inc(dn_hi.sem, 1)
                    att_high(where, p)
                    if p == 5:
                        act.wait_ge(dsq_used.sem, dsq_used.at(where, 1))
                        act.wait_ge(grstd_ready.sem, grstd_ready.at(where, 2))
                        A(std[0:16, :], bank[3][0:16, 0:SEQ], ACT.Sqrt, bias=eps[0:16, :]
                          ).then_inc(gstd_ready.sem, 1)

            def out_phase(where, vv, n):
                for u in range(4):
                    if u < 3:
                        next_hi(where, vv + u)
                    squares(where, n, 2 * u, 2)

            for kind, dst, src in param_loads(a, prow):
                act.dma_start(dst, src).then_inc(ld_par[kind], 16)
            act.dma_start(dlam, a["diff_lambda"].rearrange("l n d -> (l n d)").partition_broadcast(P)
                          ).then_inc(ld_wf, 16)
            for l in range(LAYERS):
                for t in range(TB):
                    act.dma_start(bf[:, l, t * H2:(t + 1) * H2], a["b_in_2"][l, QKV2:REST2].partition_broadcast(P)
                                  ).then_inc(ld_wf, 16)
                act.dma_start(wf_raw[:, l, :, :], a["w_in_2"][l].rearrange("(k p) m -> p k m", p=P)[:, :, QKV2:REST2]
                              ).then_inc(ld_wf, 16)
            act.wait_ge(ld_cst, 34)
            squares((1, 0), 0, 0, KT)
            for vv in range(2):
                act.wait_ge(raw_full[vv], 16)
                A(w_hi[:, vv, :], raw[:, vv, :], ACT.Copy).then_inc(hi_ready.sem, 1)
            act.wait_ge(ld_wf, 16 * (1 + LAYERS * (TB + 1)))
            A(wf_hi[:, :, :, :].rearrange("p l k h -> p (l k h)"), wf_raw[:, :, :, :].rearrange("p l k h -> p (l k h)"),
              ACT.Copy).then_inc(pro_act, 1)
            act.wait_ge(pro_dve, 10)
            A(lgs[:, 7, 4:8], lgs[:, 7, 0:4], ACT.Exp).then_inc(pro_act, 1)
            act.wait_ge(pro_dve, 11)
            own.link(A(lgs[:, 1, :], lgs[:, 0, :], ACT.Exp))
            own.wait()
            A(lgs[:, 2, :], lgs[:, 1, :], ACT.Ln, bias=1.0).then_inc(pro_act, 1)
            own.restart()

            with act.Fori(0, LAYERS) as l:
                where = (1, l)
                norm(where, 0, V1_WIN)
                for u in range(12):
                    vv, b = V1_WIN + u, u % 2
                    unit_wait(where, vv)
                    if u % 6 < 4:
                        n = 4 * (u // 6) + u % 6
                        t = 8 * (u // 6) + 2 * (u % 6)
                        two = bank[b][:, :].rearrange("p (m s) -> p m s", m=2)
                        A(qk[:, t:t + 2, :], two, ACT.Copy)
                        act.wait_ge(gsq_used.sem, gsq_used.at(where, n - 1))
                        last = A(t4[:, 2 * (n % 2):2 * (n % 2) + 2, :], two, ACT.Square)
                        own.link(last)
                        own.wait()
                        act.sem_inc(gsq_ready.sem, 1)
                        act.sem_inc(evacuated.sem, 1)
                    else:
                        c = 512 * (u // 6) + UW * (u % 6 - 4)
                        A(v[:, :, c:c + UW], bank[b][:, :].rearrange("p (t c) -> p t c", t=TB), ACT.Copy
                          ).then_inc(evacuated.sem, 1)
                    next_hi(where, vv)
                    if u == 4:
                        group_std(where, 0)
                    if u == 10:
                        group_std(where, 1)
                    if 9 <= u:
                        att_high(where, u - 9)
                    if 8 <= u:
                        copy_turned(where, u - 8)
                    if 7 <= u <= 10:
                        exps(where, u - 7)
                att_high(where, 3)
                rest_of_attention(where)
                after_skip(where)
                out_phase(where, V1_WOUT, 1)
                norm(where, 1, V1_FFN)
                act.wait_ge(cur_ready.sem, cur_ready.at(where, 1))
                ffn(where, V1_FFN, lambda vv, step, i, last: ffn1_step(where, vv, step, i), 1)
                own.restart()

            with act.Fori(0, LAYERS) as l:
                where = (2, l)
                norm(where, 0, V2_FFN1)
                ffn(where, V2_FFN1, lambda vv, step, i, last: ffn2_step(where, vv, step, 0, i), 0)
                norm(where, 1, V2_WIN)
                act.wait_ge(cur_ready.sem, cur_ready.at(where, 1))

                def lru_gates_(j):
                    act.wait_ge(lru_lin.sem, lru_lin.at(where, j + 1))
                    if j:
                        act.wait_ge(r_ready.sem, r_ready.at(where, j))
                    for b, dst, cb in ((4, lru_r, C2_BA), (5, lru_i, C2_BX)):
                        for m in range(2):
                            t = 2 * j + m
                            k = own.link(A(dst[:, m, :], bank[b][:, m * SEQ:(m + 1) * SEQ], ACT.Sigmoid,
                                           bias=cur[:, cb + t:cb + t + 1]))
                            if b == 4:
                                kr = k
                    own.wait(kr)
                    for m in range(2):
                        t = 2 * j + m
                        own.link(A(lru_x[:, m, :], lru_r[:, m, :], ACT.Tanh, scale=cur[:, C2_POS + t:C2_POS + t + 1]))
                    for m in range(2):
                        t = 2 * j + m
                        own.link(A(lru_a[:, m, :], lru_r[:, m, :], ACT.Exp, scale=cur[:, C2_LAM + t:C2_LAM + t + 1]))
                    own.wait()
                    A(lru_r, lru_a, ACT.Square).then_inc(lru_gates.sem, 1)

                def lru_root(j):
                    act.wait_ge(lru_m.sem, lru_m.at(where, j + 1))
                    A(lru_r, lru_r, ACT.Sqrt).then_inc(lru_sqrt.sem, 1)

                def lru_high(j):
                    act.wait_ge(lru_y.sem, lru_y.at(where, j + 1))
                    A(r_hi[:, 2 * j:2 * j + 2, :], lru_r, ACT.Copy).then_inc(lru_hi.sem, 1)

                def qk_unit(n, vv, b):
                    next_hi(where, vv)
                    act.wait_ge(gsq_used.sem, gsq_used.at(where, n - 1))
                    for m in range(2):
                        t = 2 * n + m
                        src = bank[b][:, m * SEQ:(m + 1) * SEQ]
                        cb = cur[:, C2_BQK + t:C2_BQK + t + 1]
                        own.link(A(qk[:, t, :], src, ACT.Identity, bias=cb))
                        own.link(A(t4[:, 2 * (n % 2) + m, :], src, ACT.Square, bias=cb))
                    own.wait()
                    act.sem_inc(gsq_ready.sem, 1)
                    act.sem_inc(evacuated.sem, 1)

                for j in range(4):
                    vv, o = V2_WIN + 3 * j, O2_WIN + 3 * j
                    next_hi(where, vv)
                    if j:
                        lru_root(j - 1)
                    next_hi(where, vv + 1)
                    if j:
                        lru_high(j - 1)
                    act.wait_ge(evacuated.sem, evacuated.at(where, o + 1))
                    for m in range(2):
                        t = 2 * j + m
                        last = A(lru_g[:, m, :], bank[(o + 1) % 2][:, m * SEQ:(m + 1) * SEQ], ACT.Gelu_apprx_tanh,
                                 bias=cur[:, C2_BREST + KT + t:C2_BREST + KT + t + 1])
                    last.then_inc(evacuated.sem, 1)
                    qk_unit(j, vv + 2, (o + 2) % 2)
                    lru_gates_(j)
                for j in range(4):
                    qk_unit(4 + j, V2_WIN + 12 + j, (O2_WIN + 12 + j) % 2)
                    if j == 0:
                        lru_root(3)
                        group_std(where, 0)
                    if j == 1:
                        lru_high(3)
                        act.wait_ge(f_abs.sem, f_abs.at(where, 1))
                        own.link(A(lgs[:, 1, :], lgs[:, 0, :], ACT.Exp))
                        own.wait()
                        A(lgs[:, 2, :], lgs[:, 1, :], ACT.Ln, bias=1.0).then_inc(f_exp.sem, 1)
                skipped = LAST_BEFORE_SKIP[2] + 1 + NS
                for j in range(4):
                    next_hi(where, V2_WIN + 16 + j)
                    if j == 0:
                        group_std(where, 1)
                    if j == 2:
                        exps(where, 0)
                    if j == 3:
                        copy_turned(where, 0)
                        exps(where, 1)
                        split_hi(where, skipped)
                for j in range(8):
                    vv = V2_GATED + 2 * j
                    unit_wait(where, vv)
                    act.wait_ge(evacuated.sem, evacuated.at(where, O2_GATED + 2 * j))
                    for m in range(2):
                        cb = C2_BREST + (24 if j < 4 else 16) + 2 * (j % 4) + m
                        own.link(A(sig_s[:, m, :], bank[0][:, m * SEQ:(m + 1) * SEQ], ACT.Sigmoid,
                                   bias=cur[:, cb:cb + 1]))
                    own.wait()
                    act.sem_inc(sig_ready.sem, 1)
                    act.sem_inc(evacuated.sem, 1)
                    if j == 0:
                        split_hi(where, skipped + 1)
                    if j < 2:
                        att_high(where, 2 * j)
                        copy_turned(where, 2 * j + 1)
                    if j == 0:
                        exps(where, 2)
                    next_hi(where, vv)
                    next_hi(where, vv + 1)
                    if j < 2:
                        att_high(where, 2 * j + 1)
                    if j == 0:
                        copy_turned(where, 2)
                        exps(where, 3)
                    if j >= 4:
                        act.wait_ge(merged_ready.sem, merged_ready.at(where, j - 3))
                        A(r_hi[:, 2 * j - 8:2 * j - 6, :], part_s, ACT.Copy).then_inc(merged_hi.sem, 1)
                out_phase(where, V2_WOUT, 2)
                norm(where, 2, V2_FFN2)
                own.restart()
                ffn(where, V2_FFN2, lambda vv, step, i, last: ffn2_step(where, vv, step, STEPS, i, last), 2, l)
                own.restart()

        @block_.vector
        def _(dve):
            own = Chain(dve, dve_own)
            V = nc.vector

            def lo_part(dst, src, hi):
                return V.tensor_tensor(dst, src, hi.bitcast(F32), ALU.subtract)

            def split_lo(where, vv, i=0):
                s = vv % NS
                dve.wait_ge(hi_ready.sem, hi_ready.at(where, vv + 1) + i * 6)
                per = {1: V1, 2: V2}[where[0]]
                lo_part(w_lo[:, s, :], raw[:, s, :], w_hi[:, s, :]).then_inc(
                    lo_ready.sem, raises(where[0], vv % per))

            def next_lo(where, vv, i=0):
                skip = LAST_BEFORE_SKIP[where[0]]
                if not skip < vv + NS <= skip + SKIP:
                    split_lo(where, vv + NS, i)

            def guarded_lo(where, vv, i, last):
                if last is None:
                    next_lo(where, vv, i)
                else:
                    with dve.If(last < LAYERS * (STEPS // 2) - 1):
                        next_lo(where, vv, i)

            def after_skip(where):
                for n in range(SKIP):
                    split_lo(where, LAST_BEFORE_SKIP[where[0]] + 1 + n + NS)

            def unit_wait(where, vv, i=0):
                dve.wait_ge(unit_done.sem, unit_done.at(where, vv + 1) + i * 6)

            def norm(where, n, col, vv):
                dve.wait_ge(std_ready.sem, std_ready.at(where, n + 1))
                own.link(V.reciprocal(rstd[:, :], std[:, :]))
                own.wait()
                for t in range(KT + 1):
                    if t < KT:
                        V.scalar_tensor_tensor(out=t4[:, t % 4, :], in0=x[:, t, :], scalar=cur[:, col + t:col + t + 1],
                                               in1=rstd[:, :], op0=ALU.mult, op1=ALU.mult).then_inc(hf_ready.sem, 1)
                    if t:
                        dve.wait_ge(hh_ready.sem, hh_ready.at(where, n * KT + t))
                        lo_part(h_lo[:, t - 1, :], t4[:, (t - 1) % 4, :], h_hi[:, t - 1, :]).then_inc(h_ready.sem, 1)
                split_lo(where, vv + 2)

            def add_down(where, vv, nth, scale):
                for t in range(KT):
                    if t % 2 == 0 and t < 6:
                        dve.wait_ge(acc_done.sem, acc_done.at(where, 3 * nth + t // 2 + 1))
                    if t == 6:
                        unit_wait(where, vv)
                    V.scalar_tensor_tensor(out=x[:, t, :], in0=acc(t), scalar=scale, in1=x[:, t, :],
                                           op0=ALU.mult, op1=ALU.add).then_inc(x_ready.sem, 1)

            def out_phase(where, vv, n):
                for u in range(4):
                    unit_wait(where, vv + u)
                    for m in range(2):
                        t = 2 * u + m
                        V.tensor_tensor(x[:, t, :], bank[u % 2][:, m * SEQ:(m + 1) * SEQ], x[:, t, :], ALU.add
                                        ).then_inc(x_ready.sem, 1)
                    dve.wait_ge(x_ready.sem, x_ready.at(where, n * KT + 2 * u + 2))
                    dve.sem_inc(evacuated.sem, 1)
                    if u < 3:
                        next_lo(where, vv + u)

            def product(where, step, n, i, gate, up):
                dve.wait_ge(silu_ready.sem, silu_ready.at(where, n + step + 1) + i * 2)
                if where[0] == 2:
                    dve.wait_ge(g_ready.sem, g_ready.at(where, n + step) + i * 2)
                own.link(V.tensor_tensor(prod_s, gate, up, ALU.mult))
                own.wait()
                dve.sem_inc(prod_ready.sem, 1)

            def product_lo(where, step, n, i):
                dve.wait_ge(prod_hi.sem, prod_hi.at(where, n + step + 1) + i * 2)
                lo_part(g_lo[:, PAR(step), :, :], prod_s, g_hi[:, PAR(step), :, :]).then_inc(g_ready.sem, 1)

            def step_params(where, step, i):
                kinds = cur[:, C1_CONV:C1_CONV + 8 * FT].rearrange("p (k f t) -> p k f t", k=4, f=2)
                at = i * 4 + 2 * step
                for half in range(2):
                    src = kinds[:, :, half, bass.ds(at, 2)]
                    last = V.tensor_copy(prm[:, PAR(step), :, half, :], src)
                own.link(last)
                own.wait()
                dve.sem_inc(prm_ready.sem, 1)

            def ffn1_step(where, vv, step, i=0):
                step_params(where, step, i)
                par = PAR(step)
                for half, dst in ((0, gate_s), (1, up_s)):
                    dve.wait_ge(conv_main.sem, conv_main.at(where, 2 * step + half + 1) + i * 4)
                    ks = []
                    for tap, kind in ((1, 3), (2, 2)):
                        for m in range(2):
                            if tap == 2:
                                own.wait(ks[m])
                            b = 2 * par + half
                            ks.append(own.link(V.scalar_tensor_tensor(
                                out=dst[:, m, tap:SEQ], in0=bank[b][:, m * SEQ:(m + 1) * SEQ - tap],
                                scalar=prm[:, par, kind, half, m:m + 1], in1=dst[:, m, tap:SEQ],
                                op0=ALU.mult, op1=ALU.add)))
                    own.wait()
                    dve.sem_inc(evacuated.sem, 1)
                    next_lo(where, vv + half, i)
                product(where, step, 0, i, gate_s, up_s)
                product_lo(where, step, 0, i)

            def ffn2_step(where, vv, step, n, i=0, last=None):
                next_lo(where, vv, i)
                unit_wait(where, vv + 1, i)
                up = bank[2 * PAR(step) + 1][:, :].rearrange("p (m s) -> p m s", m=2)
                product(where, step, n, i, gate_s, up)
                dve.sem_inc(evacuated.sem, 2)
                guarded_lo(where, vv + 1, i, last)
                product_lo(where, step, n, i)

            def ffn(where, vv, one_step, nth, scale, last_layer=None):
                one_step(vv, 0, 0, None)
                own.restart()
                with dve.Fori(0, STEPS // 2) as i:
                    for e in range(2):
                        last = None if last_layer is None or e == 0 else last_layer * (STEPS // 2) + i
                        one_step(vv + 2 + 3 * e, 1 + e, i, last)
                        guarded_lo(where, vv + 4 + 3 * e, i, last)
                    own.restart()
                add_down(where, vv + 3 * STEPS - 1, nth, scale)

            def group_rstd(where, n):
                dve.wait_ge(gstd_ready.sem, gstd_ready.at(where, n + 1))
                V.reciprocal(rstd[0:16, :], std[0:16, :]).then_inc(grstd_ready.sem, 1)

            def group_apply(where, q0, groups, tile0, gains, banks):
                for q, c in enumerate(groups, q0):
                    dve.wait_ge(bc_done.sem, bc_done.at(where, q + 1))
                    for m in range(2):
                        t = tile0 + 2 * c + m
                        g = gains[(2 * c + m) // 4]
                        own.link(V.scalar_tensor_tensor(
                            out=qk[:, t, :], in0=qk[:, t, :], scalar=cur[:, g:g + 1],
                            in1=bank[banks[q % 2]][:, m * SEQ:(m + 1) * SEQ], op0=ALU.mult, op1=ALU.mult))
                    own.wait()
                    dve.sem_inc(bc_used.sem, 1)

            def logits(where, p):
                dve.wait_ge(scored.sem, scored.at(where, p + 1))
                dve.wait_ge(turned.sem, turned.at(where, p - 1))
                own.tick()
                e = p % 2
                for m in range(2):
                    if where[0] == 1:
                        h = p if p < 4 else 4 + 2 * (p - 4) + m
                        add = bias[:, h, ::-1]
                    else:
                        add = mask
                    for c, ps, ad in ((0, slice(0, 256), add), (1, slice(256, 384), add[:, 128:256])):
                        n = 2 * m + c
                        last = V.tensor_tensor_reduce(out=probs[:, e, m, ps], in0=bank[4 + m][:, ps], in1=ad,
                                                      scale=-1.0, scalar=3e38, op0=ALU.add, op1=ALU.min,
                                                      accum_out=nmax[:, e, n:n + 1])
                last.then_inc(logits_ready.sem, 1)

            def normalise(where, p, l):
                dve.wait_ge(exp_ready.sem, exp_ready.at(where, p + 1))
                e = p % 2
                own.link(V.reciprocal(esc[:, e, :], esum[:, e, :]))
                own.wait()
                if where[0] == 1 and p < 4:
                    own.link(V.tensor_scalar(esc[:, e, 2:4], esc[:, e, 2:4], neglam[:, bass.ds(l, 1)], None, ALU.mult))
                    for c, cs in ((0, slice(0, 256)), (1, slice(256, 384))):
                        own.link(V.tensor_scalar(probs[:, e, 0, cs], probs[:, e, 0, cs], esc[:, e, c:c + 1], None,
                                                 ALU.mult))
                    own.wait()
                    for c, cs in ((0, slice(0, 256)), (1, slice(256, 384))):
                        last = V.scalar_tensor_tensor(out=probs[:, e, 0, cs], in0=probs[:, e, 1, cs],
                                                      scalar=esc[:, e, 2 + c:3 + c], in1=probs[:, e, 0, cs],
                                                      op0=ALU.mult, op1=ALU.add)
                else:
                    for m in range(2):
                        for c, cs in ((0, slice(0, 256)), (1, slice(256, 384))):
                            n = 2 * m + c
                            last = V.tensor_scalar(probs[:, e, m, cs], probs[:, e, m, cs], esc[:, e, n:n + 1], None,
                                                   ALU.mult)
                last.then_inc(probs_ready.sem, 1)

            def att_low(where, p):
                if where[0] == 1 and p < 4:
                    return
                dve.wait_ge(att_hi.sem, att_hi.at(where, p - 3 if where[0] == 1 else p + 1))
                if where[0] == 1:
                    last = lo_part(y_lo[:, p, :], bank[2][:, 0:SEQ], y_hi[:, p, :])
                else:
                    for m in range(2):
                        last = lo_part(y_lo[:, 2 * p + m, :], bank[2 + m][:, 0:SEQ], y_hi[:, 2 * p + m, :])
                last.then_inc(att_out.sem, 1)

            def rest_of_attention(where, l):
                logits(where, 4)
                logits(where, 5)
                normalise(where, 4, l)
                for p in range(4, 8):
                    if p + 1 < 8:
                        normalise(where, p + 1, l)
                    if p + 2 < 8:
                        logits(where, p + 2)
                    if p == 7:
                        for t in range(3):
                            dve.wait_ge(dn_hi.sem, dn_hi.at(where, t + 1))
                            lo_part(y_lo[:, t, :], t4[:, t, :], y_hi[:, t, :])
                    att_low(where, p)
                    if p == 5:
                        group_rstd(where, 2)
                    if p == 6:
                        for c in range(2):
                            dve.wait_ge(bc_done.sem, bc_done.at(where, 8 + c + 1))
                            for m in range(2):
                                t = 2 * c + m
                                own.link(V.scalar_tensor_tensor(
                                    out=t4[:, t, :], in0=qk[:, t, :], scalar=cur[:, C1_SUB:C1_SUB + 1],
                                    in1=bank[c][:, m * SEQ:(m + 1) * SEQ], op0=ALU.mult, op1=ALU.mult))
                            own.wait()
                            dve.sem_inc(bc_used.sem, 1)
                            dve.sem_inc(dn_ready.sem, 2)
                dve.wait_ge(dn_hi.sem, dn_hi.at(where, 4))
                lo_part(y_lo[:, 3, :], t4[:, 3, :], y_hi[:, 3, :]).then_inc(y_ready.sem, 1)

            def log_sigmoid_rest(f, dst, mul):
                e, ln, d, k = lgs[:, 1, :], lgs[:, 2, :], lgs[:, 3, :], lgs[:, 4, :]
                own.link(V.tensor_scalar(d, e, 1.0, -1.0, ALU.add, ALU.add))
                own.wait()
                own.link(V.tensor_scalar(k, d, 0.0, None, ALU.is_equal))
                own.wait()
                own.link(V.tensor_tensor(d, d, k, ALU.add))
                own.wait()
                own.link(V.reciprocal(d, d))
                own.wait()
                own.link(V.tensor_tensor(d, d, ln, ALU.mult))
                own.wait()
                own.link(V.tensor_tensor(d, d, k, ALU.add))
                own.wait()
                own.link(V.tensor_tensor(d, d, e, ALU.mult))
                own.wait()
                own.link(V.scalar_tensor_tensor(out=dst, in0=f, scalar=0.0, in1=d, op0=ALU.min, op1=ALU.subtract))
                own.wait()
                if mul is not None:
                    own.link(V.tensor_scalar(dst, dst, mul, None, ALU.mult))
                    own.wait()

            V.memset(lgs[:, 7, :], 0.0).then_inc(lo_ready.sem, NS)
            for c, (s, k) in enumerate(((evacuated, 2), (gsq_used, 2), (bc_used, 2), (logits_ready, 1), (turned, 2),
                                        (pt_ready, 1), (pv_done, 1), (att_hi, 1), (att_out, 1))):
                dve.sem_inc(s.sem, k)
            for c in range(4):
                dve.wait_ge(pro_pe, c + 1)
                own.link(V.tensor_copy(x[:, 2 * c:2 * c + 2, :], bank[c][:, :].rearrange("p (m s) -> p m s", m=2)))
                own.wait()
                dve.sem_inc(x_ready.sem, 2)
                dve.sem_inc(pro_dve, 1)
            for k, dst in enumerate((par1[:, :, 0:109], par1[:, :, 109:197], par2[:, :, 0:106], par2[:, :, 106:138])):
                dve.wait_ge(pro_pe, 5 + k)
                src = bank[4 + k][:, 0:2 * P].rearrange("p (l c) -> p l c", l=LAYERS)
                V.tensor_copy(dst, src[:, :, 0:PAR_ROWS[k]]).then_inc(pro_dve, 1)
            dve.wait_ge(pro_dve, 8)
            own.link(V.memset(tsb[:, 0:P - 1], NEG))
            own.link(V.tensor_copy(lgs[:, 7, 8:9], lgs[:, 7, 8:9]))
            own.wait()
            dve.wait_ge(pro_pe, 9)
            V.tensor_copy(tsb[:, P - 1:384], bank[3][0:BIAS_HEADS, P - 1:384]).then_inc(pro_dve, 1)
            for vv in range(2):
                dve.wait_ge(hi_ready.sem, vv + 1)
                lo_part(w_lo[:, vv, :], raw[:, vv, :], w_hi[:, vv, :]).then_inc(lo_ready.sem, 1)
            for l in range(LAYERS):
                for col, by in ((C1_QK, HD1 ** -0.5), (C1_QK + 2, HD1 ** -0.5), (C1_SUB, 1.0 - LAM_INIT[l])):
                    own.link(V.tensor_scalar(par1[:, l, col:col + 1], par1[:, l, col:col + 1], by, None, ALU.mult))
                own.link(V.tensor_scalar(par2[:, l, C2_QN:C2_QN + 1], par2[:, l, C2_QN:C2_QN + 1], HD2 ** -0.5, None,
                                         ALU.mult))
            dve.wait_ge(ld_wf, 16 * (1 + LAYERS * (TB + 1)))
            dve.wait_ge(pro_act, 1)
            lo_part(wf_lo[:, :, :, :].rearrange("p l k h -> p (l k h)"),
                    wf_raw[:, :, :, :].rearrange("p l k h -> p (l k h)"),
                    wf_hi[:, :, :, :].rearrange("p l k h -> p (l k h)"))
            pairs = dlam.rearrange("p (n e d) -> p n e d", n=4, e=2)
            own.link(V.tensor_tensor(dprod, pairs[:, :, 0, :], pairs[:, :, 1, :], ALU.mult))
            own.wait()
            V.tensor_reduce(lgs[:, 7, 0:4], dprod, AX_X, ALU.add).then_inc(pro_dve, 1)
            lam2 = lgs[:, 6, :].rearrange("p (l t) -> p l t", l=LAYERS)
            own.link(V.tensor_copy(lam2, par2[:, :, C2_LAM:C2_LAM + KT]))
            own.wait()
            V.scalar_tensor_tensor(out=lgs[:, 0, :], in0=lgs[:, 6, :], scalar=-1.0, in1=lgs[:, 6, :], op0=ALU.mult,
                                   op1=ALU.min).then_inc(pro_dve, 1)
            dve.wait_ge(pro_act, 2)
            e4 = lgs[:, 7, 4:8].rearrange("p (l e) -> p l e", l=LAYERS)
            own.link(V.tensor_tensor(neglam[:, :], e4[:, :, 1], e4[:, :, 0], ALU.subtract))
            own.wait()
            for l in range(LAYERS):
                own.link(V.tensor_scalar(neglam[:, l:l + 1], neglam[:, l:l + 1], -LAM_INIT[l], None, ALU.add))
            dve.wait_ge(pro_act, 3)
            log_sigmoid_rest(lgs[:, 6, :], lgs[:, 5, :], LRU_C)
            c5 = lgs[:, 5, :].rearrange("p (l t) -> p l t", l=LAYERS)
            own.link(V.tensor_copy(par2[:, :, C2_LAM:C2_LAM + KT], c5))
            own.link(V.tensor_scalar(par2[:, :, C2_POS:C2_POS + KT], c5, -1.0, None, ALU.mult))
            own.restart()

            with dve.Fori(0, LAYERS) as l:
                where = (1, l)
                own.link(V.tensor_copy(cur[:, :], par1[:, bass.ds(l, 1), :].rearrange("p l c -> p (l c)")))
                own.wait()
                dve.sem_inc(cur_ready.sem, 1)
                norm(where, 0, C1_ATTN, V1_WIN)
                for u in range(12):
                    next_lo(where, V1_WIN + u)
                    if u == 5:
                        group_rstd(where, 0)
                    if 6 <= u <= 7:
                        group_apply(where, 2 * u - 12, (u - 6, u - 4), 0, (C1_QK, C1_QK + 1), (6, 7))
                    if u == 10:
                        group_rstd(where, 1)
                    if u == 7:
                        dve.wait_ge(ld_bias, 16)
                    if 7 <= u <= 10:
                        logits(where, u - 7)
                        normalise(where, u - 7, l)
                group_apply(where, 4, (0, 2, 1, 3), 8, (C1_QK + 2, C1_QK + 3), (3, 7))
                rest_of_attention(where, l)
                after_skip(where)
                out_phase(where, V1_WOUT, 1)
                norm(where, 1, C1_FFN, V1_FFN)
                ffn(where, V1_FFN, lambda vv, step, i, last: ffn1_step(where, vv, step, i), 0, 1.0)
                own.restart()

            V.memset(lin_a, 0.0).then_inc(lin_cleared, 1)
            V.memset(lin_x, 0.0).then_inc(lin_cleared, 1)
            with dve.Fori(0, LAYERS) as l:
                where = (2, l)
                own.link(V.tensor_copy(cur[:, 0:C2], par2[:, bass.ds(l, 1), :].rearrange("p l c -> p (l c)")))
                own.wait()
                dve.sem_inc(cur_ready.sem, 1)
                norm(where, 0, C2_FFN1, V2_FFN1)
                ffn(where, V2_FFN1, lambda vv, step, i, last: ffn2_step(where, vv, step, 0, i), 0, 0.5)
                norm(where, 1, C2_MIX, V2_WIN)

                def lru_taps(j):
                    o = O2_WIN + 3 * j
                    dve.wait_ge(evacuated.sem, evacuated.at(where, o))
                    for m in range(2):
                        t = 2 * j + m
                        own.link(V.tensor_scalar(lru_x[:, m, :], bank[o % 2][:, m * SEQ:(m + 1) * SEQ],
                                                 cur[:, C2_BREST + t:C2_BREST + t + 1], None, ALU.add))
                    own.wait()
                    dve.sem_inc(evacuated.sem, 1)
                    ks = []
                    for m in range(2):
                        t = 2 * j + m
                        ks.append(own.link(V.tensor_scalar(
                            lru_c[:, m, :], lru_x[:, m, :], cur[:, C2_CONV + 24 + t:C2_CONV + 25 + t],
                            cur[:, C2_CB + t:C2_CB + t + 1], ALU.mult, ALU.add)))
                    for tap in (1, 2, 3):
                        for m in range(2):
                            own.wait(ks[-2])
                            cc = C2_CONV + (3 - tap) * KT + 2 * j + m
                            ks.append(own.link(V.scalar_tensor_tensor(
                                out=lru_c[:, m, tap:SEQ], in0=lru_x[:, m, 0:SEQ - tap], scalar=cur[:, cc:cc + 1],
                                in1=lru_c[:, m, tap:SEQ], op0=ALU.mult, op1=ALU.add)))
                    own.wait()
                    dve.sem_inc(lru_conv.sem, 1)

                def lru_gains(j):
                    dve.wait_ge(lru_gates.sem, lru_gates.at(where, j + 1))
                    own.link(V.tensor_tensor(lru_i, lru_i, lru_c, ALU.mult))
                    own.link(V.scalar_tensor_tensor(out=lru_r, in0=lru_r, scalar=1.0, in1=lru_x, op0=ALU.add,
                                                    op1=ALU.mult))
                    own.wait()
                    dve.sem_inc(lru_m.sem, 1)

                def lru_scan(j):
                    dve.wait_ge(lru_sqrt.sem, lru_sqrt.at(where, j + 1))
                    own.link(V.tensor_tensor(lru_i, lru_i, lru_r, ALU.mult))
                    own.wait()
                    for m in range(2):
                        own.link(V.tensor_tensor_scan(lru_r[:, m, :], lru_a[:, m, :], lru_i[:, m, :], 0.0, ALU.mult,
                                                      ALU.add))
                    own.wait()
                    own.link(V.tensor_tensor(lru_r, lru_r, lru_g, ALU.mult))
                    own.wait()
                    dve.sem_inc(lru_y.sem, 1)

                def lru_low(j):
                    dve.wait_ge(lru_hi.sem, lru_hi.at(where, j + 1))
                    lo_part(r_lo[:, 2 * j:2 * j + 2, :], lru_r, r_hi[:, 2 * j:2 * j + 2, :]).then_inc(r_ready.sem, 1)

                for j in range(4):
                    vv = V2_WIN + 3 * j
                    next_lo(where, vv)
                    if j:
                        lru_scan(j - 1)
                    lru_taps(j)
                    next_lo(where, vv + 1)
                    if j:
                        lru_low(j - 1)
                    next_lo(where, vv + 2)
                    lru_gains(j)
                for j in range(4):
                    next_lo(where, V2_WIN + 12 + j)
                    if j == 0:
                        lru_scan(3)
                        dve.wait_ge(f_done.sem, f_done.at(where, 1))
                        own.link(V.tensor_tensor(lgs[:, 6, :], bank[2][:, 0:16],
                                                 bf[:, bass.ds(l, 1), :].rearrange("p l h -> p (l h)"), ALU.add))
                        own.wait()
                        V.scalar_tensor_tensor(out=lgs[:, 0, :], in0=lgs[:, 6, :], scalar=-1.0, in1=lgs[:, 6, :],
                                               op0=ALU.mult, op1=ALU.min).then_inc(f_abs.sem, 1)
                        group_rstd(where, 0)
                    if j == 1:
                        lru_low(3)
                        dve.wait_ge(f_exp.sem, f_exp.at(where, 1))
                        log_sigmoid_rest(lgs[:, 6, :], lf[:, :], None)
                        dve.sem_inc(f_ready.sem, 1)
                    if j >= 2:
                        group_apply(where, 2 * j - 4, (2 * j - 4, 2 * j - 3), 0, (C2_QN, C2_QN), (6, 7))
                for j in range(4):
                    vv, o = V2_WIN + 16 + j, O2_WIN + 16 + j
                    unit_wait(where, vv)
                    if j == 0:
                        dve.wait_ge(side_loaded.sem, l * 80 + 80)
                        dve.wait_ge(evacuated.sem, evacuated.at(where, o))
                    for t in range(TB):
                        last = V.tensor_tensor(v[:, t, UW * j:UW * (j + 1)], bank[o % 2][:, t * UW:(t + 1) * UW],
                                               bv[:, UW * j:UW * (j + 1)], ALU.add)
                    last.then_inc(evacuated.sem, 1)
                    next_lo(where, vv)
                    if j == 0:
                        group_rstd(where, 1)
                    if 1 <= j <= 2:
                        group_apply(where, 2 + 2 * j, (2 * j - 2, 2 * j - 1), 8, (C2_KN, C2_KN), (6, 7))
                    if j >= 2:
                        logits(where, j - 2)
                        normalise(where, j - 2, l)
                skipped = LAST_BEFORE_SKIP[2] + 1 + NS
                split_lo(where, skipped)
                for j in range(8):
                    vv = V2_GATED + 2 * j
                    if j == 0:
                        split_lo(where, skipped + 1)
                    if j < 2:
                        att_low(where, 2 * j)
                    if j == 0:
                        logits(where, 2)
                        normalise(where, 2, l)
                    next_lo(where, vv)
                    unit_wait(where, vv + 1)
                    dve.wait_ge(sig_ready.sem, sig_ready.at(where, j + 1))
                    two = bank[1][:, :].rearrange("p (m s) -> p m s", m=2)
                    tiles = qk[:, 2 * (j % 4):2 * (j % 4) + 2, :]
                    if j < 4:
                        own.link(V.tensor_tensor(tiles, sig_s, two, ALU.mult))
                        own.wait()
                        dve.sem_inc(evacuated.sem, 1)
                        next_lo(where, vv + 1)
                        if j < 2:
                            att_low(where, 2 * j + 1)
                        if j == 0:
                            logits(where, 3)
                            normalise(where, 3, l)
                        if j == 1:
                            dve.wait_ge(att_out.sem, att_out.at(where, 4))
                            dve.sem_inc(y_ready.sem, 1)
                    else:
                        if j > 4:
                            dve.wait_ge(m_ready.sem, m_ready.at(where, j - 4))
                        own.link(V.tensor_tensor(part_s, sig_s, two, ALU.mult))
                        own.wait()
                        dve.sem_inc(evacuated.sem, 1)
                        own.link(V.tensor_tensor(part_s, part_s, tiles, ALU.add))
                        own.wait()
                        dve.sem_inc(merged_ready.sem, 1)
                        next_lo(where, vv + 1)
                        dve.wait_ge(merged_hi.sem, merged_hi.at(where, j - 3))
                        rs = slice(2 * j - 8, 2 * j - 6)
                        lo_part(r_lo[:, rs, :], part_s, r_hi[:, rs, :]).then_inc(m_ready.sem, 1)
                out_phase(where, V2_WOUT, 2)
                norm(where, 2, C2_FFN2, V2_FFN2)
                own.restart()
                ffn(where, V2_FFN2, lambda vv, step, i, last: ffn2_step(where, vv, step, STEPS, i, last), 1, 0.5, l)
                own.restart()

            for c in range(4):
                dve.wait_ge(fin_pe, c + 1)
                V.tensor_copy(x_tok[:, :, 256 * c:256 * (c + 1)], bank[c][:, :].rearrange("p (t c) -> p t c", t=TB)
                              ).then_inc(fin_sb, 1)


def PAR(step):
    return step % 2


PAR_ROWS = [109, 88, 106, 32]
PAR_DMAS = [7, 1, 11, 1]


def param_loads(a, prow):
    def rows(vec):
        return vec.rearrange("l (t p) -> t l p", p=P)

    def one(vec):
        return vec.rearrange("(o l) p -> o l p", o=1)

    def to(kind, r0, n):
        return kind, prow[r0:r0 + n, kind, :, :]

    b, qk_g = a["b_in_2"], a["qk_norm_g"].rearrange("l n d -> n l d")
    kinds = [
        (*to(0, C1_ATTN, 8), rows(a["ln_attn_g"])), (*to(0, C1_FFN, 8), rows(a["ln_ffn_g"])),
        (*to(0, C1_SUB, 1), one(a["diff_subln_g"])),
        (0, prow[C1_QK:C1_QK + 4, 0, :, 0:64], qk_g), (0, prow[C1_QK:C1_QK + 4, 0, :, 64:128], qk_g),
        (*to(0, 21, FT * 2), rows(a["conv_b"])), (*to(0, 65, FT * 2), rows(a["conv_w"][:, 2])),
        (*to(1, 0, FT * 4), a["conv_w"][:, 0:2].rearrange("l k (t p) -> (k t) l p", p=P)),
        (*to(2, 0, 8), rows(a["ffn1_norm_2"])), (*to(2, 8, 8), rows(a["mix_norm_2"])),
        (*to(2, 16, 8), rows(a["ffn2_norm_2"])), (*to(2, 24, 16), rows(b[:, 0:2 * D])),
        (*to(2, 40, 32), rows(b[:, REST2:REST2 + 4 * D])),
        (*to(2, 72, 1), one(a["q_norm_2"])), (*to(2, 73, 1), one(a["k_norm_2"])),
        (*to(2, 74, 8), rows(a["conv_b_2"])), (*to(2, 82, 8), rows(a["lru_b_a_2"])),
        (*to(2, 90, 8), rows(a["lru_b_x_2"])), (*to(2, 98, 8), rows(a["lru_lambda_2"])),
        (*to(3, 0, 32), a["conv_w_2"].rearrange("l k (t p) -> (k t) l p", p=P))]
    assert [sum(k == kind for k, _, _ in kinds) for kind in range(4)] == PAR_DMAS
    return kinds


_INS = ['x', 'ln_attn_g', 'w_in', 'qk_norm_g', 'diff_lambda', 'diff_subln_g', 'w_out', 'ln_ffn_g', 'w_up', 'conv_w',
        'conv_b', 'w_down', 'rel_bias', 'ffn1_norm_2', 'ffn1_w_gate_2', 'ffn1_w_up_2', 'ffn1_w_down_2', 'mix_norm_2',
        'w_in_2', 'b_in_2', 'q_norm_2', 'k_norm_2', 'conv_w_2', 'conv_b_2', 'lru_w_a_2', 'lru_b_a_2', 'lru_w_x_2',
        'lru_b_x_2', 'lru_lambda_2', 'w_o_attn_2', 'w_o_rnn_2', 'w_out_2', 'ffn2_norm_2', 'ffn2_w_gate_2',
        'ffn2_w_up_2', 'ffn2_w_down_2']


def shape_constants():
    import numpy as np
    j, k = np.arange(P)[:, None], np.arange(P)[None, :]
    c = np.zeros((P, K_N), np.float32)
    c[:, K_ID:K_ID + P] = j == k
    c[:, K_TRI:K_TRI + P] = j <= k
    c[:, K_ONEU:K_ONEU + P] = 1.0
    c[:, K_ONEU + P:K_ONEU + 2 * P] = j > k
    c[:, K_MASK + P:K_MASK + 2 * P] = np.where(k <= j, 0.0, NEG)
    sp = np.zeros((16, KT, P), np.float32)
    for t in range(KT):
        c[:64, K_G64 + 16 * t + 2 * t] = 1.0 / 64
        c[64:, K_G64 + 16 * t + 2 * t + 1] = 1.0 / 64
        c[:, K_G128 + 16 * t + 2 * t:K_G128 + 16 * t + 2 * t + 2] = 1.0 / 128
        sp[2 * t, t, :64] = 1.0
        sp[2 * t + 1, t, 64:] = 1.0
    c[:, K_MEAN:K_MEAN + P] = 1.0 / D
    dist = np.arange(SEQ)
    exact = BUCKETS // 2
    far = np.maximum(dist, exact).astype(np.float32) / np.float32(exact)
    far = exact + (np.log(far) / np.float32(math.log(1024 / exact)) * np.float32(BUCKETS - exact)).astype(np.int32)
    bucket = np.where(dist < exact, dist, np.minimum(far, BUCKETS - 1))
    onehot = np.zeros((BUCKETS, 384), np.float32)
    onehot[bucket, P - 1 + dist] = 1.0
    return {"const_main": c, "const_spread": sp.reshape(16, KT * P), "const_onehot": onehot}


def kernel(**inputs):
    import numpy as np
    import concourse.bacc as bacc
    from concourse.bass_utils import run_bass_kernel_spmd

    nc = bacc.Bacc("TRN2", target_bir_lowering=False, num_devices=1)
    arrays, aps = {}, {}
    for name, value in [(n, inputs[n]) for n in _INS] + list(shape_constants().items()):
        value = np.ascontiguousarray(value)
        arrays[f"in_{name}"] = value
        aps[name] = nc.dram_tensor(f"in_{name}", value.shape, mybir.dt.from_np(value.dtype), kind="ExternalInput").ap()
    out = nc.dram_tensor("out_0", (1, SEQ, D), F32, kind="ExternalOutput").ap()
    build_program(nc, aps, out)
    r = run_bass_kernel_spmd(nc, [arrays], core_ids=[0])
    return r.results[0]["out_0"]
```

```python
import math
from contextlib import ExitStack

import concourse.bass as bass
from concourse import mybir

F32 = mybir.dt.float32
F32R = mybir.dt.float32r
BF16 = mybir.dt.bfloat16
ALU = mybir.AluOpType
ACT = mybir.ActivationFunctionType
AX_X = mybir.AxisListType.X

P = 128
LAYERS = 2
SEQ = 256
TB = SEQ // P
D = 1024
KT = D // P
F = 2816
FT = F // P
UW = 256
UNIT = KT * UW
STEPS = F // UW
NS = 3
EPS = 1e-6
NEG = -1e30
BUCKETS = 32
BIAS_HEADS = 12
DIFF_HEADS = 4
HD1 = 64
HD2 = 128
H2 = 8
LRU_C = 8.0
QKV2 = 3 * D
REST2 = QKV2 + H2
LAM_INIT = [0.8 - 0.6 * math.exp(-0.3 * i) for i in range(LAYERS)]

SKIP = 2
V1_WIN, V1_WOUT, V1_FFN = 0, 14, 18
V1 = 51
V2_FFN1, V2_WIN, V2_GATED, V2_WOUT, V2_FFN2 = 0, 33, 55, 71, 75
V2 = 108
LAST_BEFORE_SKIP = {1: 11, 2: 52}
O1_WIN, O1_WOUT, O1_FFN, O1 = 0, 12, 16, 38
O2_FFN1, O2_WIN, O2_GATED, O2_WOUT, O2_FFN2, O2 = 0, 22, 42, 58, 62, 84

C1_ATTN, C1_FFN, C1_SUB, C1_QK, C1_CONV, C1 = 0, 8, 16, 17, 21, 197
C2_FFN1, C2_MIX, C2_FFN2, C2_BQK, C2_BREST, C2_QN, C2_KN = 0, 8, 16, 24, 40, 72, 73
C2_CB, C2_BA, C2_BX, C2_LAM, C2_CONV, C2_POS, C2 = 74, 82, 90, 98, 106, 138, 146

K_ID, K_TRI, K_ONEU, K_MASK, K_G64, K_G128, K_MEAN, K_N = 0, 128, 256, 512, 768, 896, 1024, 1152


class Signal:

    def __init__(self, sem, per1, per2, credit=0):
        self.sem, self.per, self.credit = sem, {1: per1, 2: per2}, credit

    def at(self, where, k):
        block, layer = where
        before = self.credit + (LAYERS * self.per[1] if block == 2 else 0)
        return layer * self.per[block] + (before + k)


class Chain:

    def __init__(self, eng, sem):
        self.eng, self.sem, self.n = eng, sem, 0

    def link(self, ins):
        self.n += 1
        ins.then_inc(self.sem, 1)
        return self.n

    def wait(self, n=None):
        self.eng.wait_ge(self.sem, self.n if n is None else n)

    def tick(self):
        self.eng.sem_inc(self.sem, 1)
        self.n += 1

    def restart(self):
        if self.n:
            self.wait()
            self.eng.sem_clear(self.sem)
            self.n = 0


def build_program(nc, a, out):
    with ExitStack() as ctx:
        def sb(name, shape, dt=F32):
            return ctx.enter_context(nc.sbuf_tensor(name, shape, dt))

        def sem(name):
            return ctx.enter_context(nc.semaphore(name))

        raw = sb("raw", [P, NS, UNIT])
        w_hi = sb("w_hi", [P, NS, UNIT], F32R)
        w_lo = sb("w_lo", [P, NS, UNIT], F32R)
        x = sb("x", [P, KT, SEQ])
        h_hi, h_lo = sb("h_hi", [P, KT, SEQ], F32R), sb("h_lo", [P, KT, SEQ], F32R)
        y_hi, y_lo = sb("y_hi", [P, KT, SEQ], F32R), sb("y_lo", [P, KT, SEQ], F32R)
        r_hi, r_lo = sb("r_hi", [P, KT, SEQ], F32R), sb("r_lo", [P, KT, SEQ], F32R)
        g_hi = sb("g_hi", [P, 2, 2, SEQ], F32R)
        g_lo = sb("g_lo", [P, 2, 2, SEQ], F32R)
        qk = sb("qk", [P, 16, SEQ])
        v = sb("v", [P, TB, D])
        t4 = sb("t4", [P, 4, SEQ])
        tmp = sb("tmp", [P, 3072])
        big = sb("big", [P, 3072])
        cst = sb("cst", [P, K_N])
        spread = sb("spread", [16, KT * P])
        par1 = sb("par1", [P, LAYERS, C1])
        par2 = sb("par2", [P, LAYERS, C2])
        cur = sb("cur", [P, C1])
        prm = sb("prm", [P, 2, 4, 2, 2])
        wf_raw = sb("wf_raw", [P, LAYERS, KT, H2])
        wf_hi = sb("wf_hi", [P, LAYERS, KT, H2], F32R)
        wf_lo = sb("wf_lo", [P, LAYERS, KT, H2], F32R)
        bf = sb("bf", [P, LAYERS, TB * H2])
        zeros = sb("zeros", [1, 512], BF16)
        eps = sb("eps", [P, 1])
        neglam = sb("neglam", [P, LAYERS])
        std = sb("std", [P, SEQ])
        rstd = sb("rstd", [P, SEQ])
        warm = sb("warm", [1, 4])
        first_gain = sb("first_gain", [P, 2 * LAYERS + 1, KT])
        nmax = sb("nmax", [P, 2, 4])
        esum = sb("esum", [P, 2, 4])
        esc = sb("esc", [P, 2, 4])
        lgs = sb("lgs", [P, 8, 16])
        lf = sb("lf", [P, TB * H2])

        ident, tri = cst[:, K_ID:K_ID + P], cst[:, K_TRI:K_TRI + P]
        one_u = cst[:, K_ONEU:K_ONEU + 256]
        mask = cst[:, K_MASK:K_MASK + 256]
        g64, g128 = cst[:, K_G64:K_G64 + P], cst[:, K_G128:K_G128 + P]
        mean = cst[:, K_MEAN:K_MEAN + P]
        bias = big[:, :].rearrange("p (h k) -> p h k", h=BIAS_HEADS)
        bv = big[:, 0:D]
        lin_a = big[:, D:D + KT * P].rearrange("p (t c) -> p t c", t=KT)
        lin_x = big[:, 2 * D:2 * D + KT * P].rearrange("p (t c) -> p t c", t=KT)

        def pair512(at):
            return tmp[:, at:at + 512].rearrange("p (m s) -> p m s", m=2)

        gate_s, up_s, prod_s = pair512(0), pair512(512), pair512(1024)
        lru_x, lru_c, lru_g, lru_r, lru_i, lru_a = (pair512(512 * n) for n in range(6))
        gate_n, up_n = pair512(1536), pair512(2048)
        lru_t = v[:, 0, 0:512].rearrange("p (m s) -> p m s", m=2)
        sig_s = bv[:, 0:512].rearrange("p (m s) -> p m s", m=2)
        part_s = bv[:, 512:1024].rearrange("p (m s) -> p m s", m=2)
        probs = tmp[:, 0:1536].rearrange("p (e m k) -> p e m k", e=2, m=2)
        probs_t = tmp[:, 1536:2304].rearrange("p (m k) -> p m k", m=2)
        t4_flat = t4[:, :, :].rearrange("p t s -> p (t s)")
        decay = [tmp[:, 2304:3072].rearrange("p (m k) -> p m k", m=2),
                 t4_flat[:, 0:768].rearrange("p (m k) -> p m k", m=2)]
        x_tok = v
        prow = tmp[:, 0:1024].rearrange("p (n l c) -> p n l c", n=4, l=LAYERS)
        dlam = tmp[:, 1024:1536]
        dprod = tmp[:, 1536:1792].rearrange("p (n d) -> p n d", n=4)
        qk_flat = qk[:, :, :].rearrange("p t s -> p (t s)")
        onehot, relb = qk_flat[0:BUCKETS, 3072:3456], qk_flat[0:BUCKETS, 3456:3468]
        tsb = qk_flat[0:BIAS_HEADS, 3468:3852]
        by_dist = nc.dram_tensor("by_dist", (BIAS_HEADS, 384), F32, kind="Internal").ap()

        bank = [ctx.enter_context(nc.psum_tensor(f"bank{i}", [P, 512], F32)) for i in range(8)]

        def gain_of(index, t):
            return first_gain[:, bass.ds(index, 1), t:t + 1].rearrange("p l t -> p (l t)")

        def raw_h(where, n):
            return (y_hi, y_lo) if where[0] == 2 and n == 2 else (r_hi, r_lo)

        def acc(m):
            return bank[4 + m // 2][:, (m % 2) * SEQ:(m % 2 + 1) * SEQ]

        raw_full = [sem(f"raw_full{s}") for s in range(NS)]
        hi_ready = Signal(sem("hi_ready"), V1, V2)
        lo_ready = Signal(sem("lo_ready"), V1, V2, credit=NS)
        unit_done = Signal(sem("unit_done"), V1, V2, credit=NS)
        evacuated = Signal(sem("evacuated"), O1, O2, credit=2)
        x_ready = Signal(sem("x_ready"), 2 * KT, 3 * KT)
        sq_ready = Signal(sem("sq_ready"), 2 * KT, 3 * KT)
        sq_used = Signal(sem("sq_used"), 2 * KT, 3 * KT)
        std_ready = Signal(sem("std_ready"), 2, 3)
        hf_ready = Signal(sem("hf_ready"), 2 * KT, 3 * KT)
        hh_ready = Signal(sem("hh_ready"), 2 * KT, 3 * KT)
        rh_hi = Signal(sem("rh_hi"), 2 * KT, 3 * KT)
        rh_ready = Signal(sem("rh_ready"), 2 * KT, 3 * KT)
        scaled = Signal(sem("scaled"), 4, 6)
        h_ready = Signal(sem("h_ready"), 2 * KT, 3 * KT)
        gsq_ready = Signal(sem("gsq_ready"), 8, 8)
        gsq_used = Signal(sem("gsq_used"), 8, 8, credit=2)
        gstd_ready = Signal(sem("gstd_ready"), 3, 2)
        grstd_ready = Signal(sem("grstd_ready"), 3, 2)
        bc_done = Signal(sem("bc_done"), 10, 8)
        bc_used = Signal(sem("bc_used"), 10, 8, credit=2)
        scored = Signal(sem("scored"), 8, 4)
        logits_ready = Signal(sem("logits_ready"), 8, 4, credit=1)
        exp_ready = Signal(sem("exp_ready"), 8, 4)
        probs_ready = Signal(sem("probs_ready"), 8, 4)
        turned = Signal(sem("turned"), 8, 4, credit=2)
        pt_ready = Signal(sem("pt_ready"), 8, 4, credit=1)
        pv_done = Signal(sem("pv_done"), 8, 4, credit=1)
        att_hi = Signal(sem("att_hi"), 4, 4, credit=1)
        att_out = Signal(sem("att_out"), 8, 4, credit=1)
        dsq_ready = Signal(sem("dsq_ready"), 1, 0)
        dsq_used = Signal(sem("dsq_used"), 1, 0)
        dn_ready = Signal(sem("dn_ready"), 4, 0)
        dn_hi = Signal(sem("dn_hi"), 4, 0)
        y_ready = Signal(sem("y_ready"), 1, 1)
        prm_ready = Signal(sem("prm_ready"), STEPS, 0)
        conv_main = Signal(sem("conv_main"), 2 * STEPS, 0)
        silu_ready = Signal(sem("silu_ready"), STEPS, 2 * STEPS)
        prod_ready = Signal(sem("prod_ready"), STEPS, 2 * STEPS)
        prod_hi = Signal(sem("prod_hi"), STEPS, 2 * STEPS)
        g_ready = Signal(sem("g_ready"), STEPS, 2 * STEPS)
        acc_done = Signal(sem("acc_done"), 3, 6)
        cur_ready = Signal(sem("cur_ready"), 1, 1)
        lru_conv = Signal(sem("lru_conv"), 0, 4)
        lru_lin = Signal(sem("lru_lin"), 0, 4)
        lru_gates = Signal(sem("lru_gates"), 0, 4)
        lru_m = Signal(sem("lru_m"), 0, 4)
        lru_sqrt = Signal(sem("lru_sqrt"), 0, 4)
        lru_y = Signal(sem("lru_y"), 0, 4)
        lru_hi = Signal(sem("lru_hi"), 0, 4)
        r_ready = Signal(sem("r_ready"), 0, 4)
        f_done = Signal(sem("f_done"), 0, 1)
        f_abs = Signal(sem("f_abs"), 0, 1)
        f_exp = Signal(sem("f_exp"), 0, 1)
        f_ready = Signal(sem("f_ready"), 0, 1)
        decay_ready = Signal(sem("decay_ready"), 0, 4)
        sig_ready = Signal(sem("sig_ready"), 0, 8)
        merged_ready = Signal(sem("merged_ready"), 0, 4)
        merged_hi = Signal(sem("merged_hi"), 0, 4)
        m_ready = Signal(sem("m_ready"), 0, 4)
        side_loaded = Signal(sem("side_loaded"), 0, 1)
        lin_cleared = sem("lin_cleared")
        ld_x, ld_cst, ld_rel, ld_wf = (sem(n) for n in ("ld_x", "ld_cst", "ld_rel", "ld_wf"))
        ld_par = [sem(f"ld_par{k}") for k in range(4)]
        ld_bias, st_by_dist, st_out = sem("ld_bias"), sem("st_by_dist"), sem("st_out")
        pro_pe, pro_dve, pro_act = sem("pro_pe"), sem("pro_dve"), sem("pro_act")
        fin_pe, fin_sb = sem("fin_pe"), sem("fin_sb")
        dve_own, act_own, pool_own = sem("dve_own"), sem("act_own"), sem("pool_own")
        loads_issued = sem("loads_issued")

        def full_at(where, vv, i):
            block, layer = where
            per = {1: V1, 2: V2}[block]
            if vv >= per:
                return full_at((block, layer + 1), vv - per, i)
            s = vv % NS
            skipped = [u % NS for u in range(LAST_BEFORE_SKIP[block] + 1, LAST_BEFORE_SKIP[block] + 1 + SKIP)]
            behind = vv > LAST_BEFORE_SKIP[block]
            uses = vv // NS - (behind and s in skipped)
            each = per // NS - (s in skipped)
            skipped1 = [u % NS for u in range(LAST_BEFORE_SKIP[1] + 1, LAST_BEFORE_SKIP[1] + 1 + SKIP)]
            before = LAYERS * (V1 // NS - (s in skipped1)) if block == 2 else 0
            return layer * (16 * each) + i * (16 * 6 // NS) + 16 * (before + uses + 1)

        def raises(block, vv):
            return 1 + SKIP if vv == LAST_BEFORE_SKIP[block] else 1

        block_ = ctx.enter_context(nc.Block())

        @block_.sync
        def _(sp):
            sp.dma_start(x_tok[:, :, :], a["x"].rearrange("a (b p) d -> (a p) b d", p=P)).then_inc(ld_x, 16)
            sp.dma_start(cst[:, :], a["const_main"]).then_inc(ld_cst, 16)
            sp.dma_start(spread[:, :], a["const_spread"]).then_inc(ld_cst, 16)

            def slot(where, vv, i, src, rows):
                s = vv % NS
                sp.wait_ge(lo_ready.sem, lo_ready.at(where, vv + 1 - NS) + i * 6)
                sp.sem_inc(loads_issued, 1)
                dst = raw[:, s, :].rearrange("p (k m) -> p k m", k=rows)
                sp.dma_start(dst, src).then_inc(raw_full[s], 16)

            def cols(where, vv, w, col, i=0, step=0):
                wv = w.rearrange("l (k p) m -> l p k m", p=P)
                at = i * step + col
                src = wv[bass.ds(where[1], 1), :, :, bass.ds(at, UW)].rearrange("l p k m -> (l p) k m")
                slot(where, vv, i, src, KT)

            def rows(where, vv, w, tile, i=0, step=0):
                wv = w.rearrange("l (t p) m -> l p t m", p=P)
                at = i * step + tile
                src = wv[bass.ds(where[1], 1), :, bass.ds(at, 2), :].rearrange("l p t m -> (l p) t m")
                slot(where, vv, i, src, 2)

            def ffn(where, vv, gate, up, up_col, down):
                cols(where, vv, gate, 0)
                cols(where, vv + 1, up, up_col)
                with sp.Fori(0, STEPS // 2) as i:
                    for e in range(2):
                        cols(where, vv + 2 + 3 * e, gate, UW * (e + 1), i, 2 * UW)
                        cols(where, vv + 3 + 3 * e, up, up_col + UW * (e + 1), i, 2 * UW)
                        rows(where, vv + 4 + 3 * e, down, 2 * e, i, 4)
                rows(where, vv + 3 * STEPS - 1, down, 2 * (STEPS - 1))

            with sp.Fori(0, LAYERS) as l:
                where = (1, l)
                for u in range(12):
                    cols(where, V1_WIN + u, a["w_in"], UW * u)
                for u in range(4):
                    cols(where, V1_WOUT + u, a["w_out"], UW * u)
                ffn(where, V1_FFN, a["w_up"], a["w_up"], F, a["w_down"])
            with sp.Fori(0, LAYERS) as l:
                where = (2, l)
                ffn(where, V2_FFN1, a["ffn1_w_gate_2"], a["ffn1_w_up_2"], 0, a["ffn1_w_down_2"])
                w = a["w_in_2"]
                for j in range(4):
                    cols(where, V2_WIN + 3 * j, w, REST2 + UW * j)
                    cols(where, V2_WIN + 3 * j + 1, w, REST2 + D + UW * j)
                    cols(where, V2_WIN + 3 * j + 2, w, UW * j)
                for j in range(8):
                    cols(where, V2_WIN + 12 + j, w, D + UW * j)
                for n, o in ((3, "w_o_rnn_2"), (2, "w_o_attn_2")):
                    for j in range(4):
                        at = V2_GATED + 8 * (3 - n) + 2 * j
                        cols(where, at, w, REST2 + n * D + UW * j)
                        cols(where, at + 1, a[o], UW * j)
                for u in range(4):
                    cols(where, V2_WOUT + u, a["w_out_2"], UW * u)
                ffn(where, V2_FFN2, a["ffn2_w_gate_2"], a["ffn2_w_up_2"], 0, a["ffn2_w_down_2"])
            for c in range(4):
                sp.wait_ge(fin_sb, c + 1)
                cs = slice(256 * c, 256 * (c + 1))
                sp.dma_start(out.rearrange("a (b p) d -> (a p) b d", p=P)[:, :, cs], x_tok[:, :, cs]
                             ).then_inc(st_out, 16)
            sp.wait_ge(st_out, 64)

        @block_.gpsimd
        def _(pool):
            nc.gpsimd.memset(zeros[:, :], 0.0).then_inc(ld_cst, 1)
            nc.gpsimd.memset(eps[:, :], EPS).then_inc(ld_cst, 1)
            pool.dma_start(onehot, a["const_onehot"]).then_inc(ld_rel, 16)
            pool.dma_start(relb, a["rel_bias"]).then_inc(ld_rel, 16)
            for kind, dst, src in param_loads(a, prow):
                if kind >= 2:
                    pool.dma_start(dst, src).then_inc(ld_par[kind], 16)
            pool.dma_start(dlam, a["diff_lambda"].rearrange("l n d -> (l n d)").partition_broadcast(P)
                          ).then_inc(ld_wf, 16)
            for l in range(LAYERS):
                for t in range(TB):
                    pool.dma_start(bf[:, l, t * H2:(t + 1) * H2], a["b_in_2"][l, QKV2:REST2].partition_broadcast(P)
                                  ).then_inc(ld_wf, 16)
                pool.dma_start(wf_raw[:, l, :, :], a["w_in_2"][l].rearrange("(k p) m -> p k m", p=P)[:, :, QKV2:REST2]
                              ).then_inc(ld_wf, 16)
            pool.wait_ge(pro_dve, 9)
            pool.dma_start(by_dist, tsb).then_inc(st_by_dist, 16)
            pool.wait_ge(st_by_dist, 16)
            pool.dma_start(bias, bass.AP(by_dist.tensor, by_dist.offset, [[1, P], [384, BIAS_HEADS], [1, 256]])
                           ).then_inc(ld_bias, 16)
            with pool.Fori(0, LAYERS) as l:
                where = (2, l)
                pool.wait_ge(cur_ready.sem, cur_ready.at(where, 1))
                pool.wait_ge(lin_cleared, 2)
                bsrc = a["b_in_2"][bass.ds(l, 1), 2 * D:3 * D].rearrange("l d -> (l d)").partition_broadcast(P)
                pool.dma_start(bv, bsrc).then_inc(side_loaded.sem, 16)
                for dst, name in ((lin_a, "lru_w_a_2"), (lin_x, "lru_w_x_2")):
                    wv = a[name].rearrange("l (t e) c d -> l e c t d", e=2)
                    for e in range(2):
                        src = wv[bass.ds(l, 1), e, :, :, :].rearrange("l c t d -> (l c) t d")
                        pool.dma_start(dst[64 * e:64 * e + 64, :, 64 * e:64 * e + 64], src
                                       ).then_inc(side_loaded.sem, 16)
                pool.wait_ge(f_ready.sem, f_ready.at(where, 1))
                pool.wait_ge(r_ready.sem, r_ready.at(where, 4))
                for p in range(4):
                    if p == 1:
                        pool.wait_ge(gsq_used.sem, gsq_used.at(where, 8))
                    if p >= 2:
                        pool.wait_ge(scored.sem, scored.at(where, p - 1))
                    pool.sem_inc(pool_own, 1)
                    for m in range(2):
                        h = 2 * p + m
                        dst = decay[p % 2]
                        nc.gpsimd.tensor_scalar(dst[:, m, 0:256], one_u, lf[:, H2 + h:H2 + h + 1], 1.0,
                                                ALU.mult, ALU.mult)
                        last = nc.gpsimd.tensor_scalar(dst[:, m, 256:384], one_u[:, 128:256], lf[:, h:h + 1], 1.0,
                                                       ALU.mult, ALU.mult)
                    last.then_inc(decay_ready.sem, 1)

        @block_.tensor
        def _(pe):
            def three(out_, lh, ll, rh, rl, start, stop):
                pe.matmul(out_, lh, rh, start=start, stop=False, skip_group_check=True)
                pe.matmul(out_, lh, rl, start=False, stop=False, skip_group_check=True)
                return pe.matmul(out_, ll, rh, start=False, stop=stop, skip_group_check=True)

            def begin(where, vv, o, i=0, ostep=0, banks=2):
                pe.wait_ge(lo_ready.sem, lo_ready.at(where, vv + 1) + i * 6)
                if o is not None:
                    pe.wait_ge(evacuated.sem, evacuated.at(where, o + 1 - banks) + i * ostep)

            def unit(where, vv, o, b, oh, ol, i=0, ostep=0, banks=2, norm=None):
                begin(where, vv, o, i, ostep, banks)
                s = vv % NS
                for m in range(2):
                    for k in range(KT):
                        if norm is not None and m == 0:
                            pe.wait_ge(h_ready.sem, h_ready.at(where, norm * KT + k + 1))
                        c = k * UW + m * P
                        mm = three(bank[b][:, m * SEQ:(m + 1) * SEQ], w_hi[:, s, c:c + P], w_lo[:, s, c:c + P],
                                   oh[:, k, :], ol[:, k, :], k == 0, k == KT - 1)
                mm.then_inc(unit_done.sem, raises(where[0], vv))

            def unit_tok(where, vv, o, b):
                begin(where, vv, o)
                s = vv % NS
                for t in range(TB):
                    for k in range(KT):
                        mm = three(bank[b][:, t * UW:(t + 1) * UW], h_hi[:, k, t * P:(t + 1) * P],
                                   h_lo[:, k, t * P:(t + 1) * P], w_hi[:, s, k * UW:(k + 1) * UW],
                                   w_lo[:, s, k * UW:(k + 1) * UW], k == 0, k == KT - 1)
                mm.then_inc(unit_done.sem, raises(where[0], vv))

            def clear_acc():
                for b in range(4, 8):
                    pe.matmul(bank[b][:, :], zeros[:, 0:P], zeros[:, :], start=True, stop=False,
                              skip_group_check=True)

            def down(where, vv, par, step, i=0):
                begin(where, vv, None, i)
                pe.wait_ge(g_ready.sem, g_ready.at(where, step + 1) + i * 2)
                s = vv % NS
                for t in range(2):
                    for m in range(KT):
                        c = t * D + m * P
                        mm = three(acc(m), w_hi[:, s, c:c + P], w_lo[:, s, c:c + P],
                                   g_hi[:, par, t, :], g_lo[:, par, t, :], False, False)
                mm.then_inc(unit_done.sem, 1)

            def first_units(where, vv, o, norm, sums):
                begin(where, vv, o)
                begin(where, vv + 1, o + 1)
                oh, ol = raw_h(where, norm)

                def tile(u, k):
                    pe.wait_ge(rh_ready.sem, rh_ready.at(where, norm * KT + k + 1))
                    s = (vv + u) % NS
                    for m in range(2):
                        c = k * UW + m * P
                        mm = three(bank[u][:, m * SEQ:(m + 1) * SEQ], w_hi[:, s, c:c + P], w_lo[:, s, c:c + P],
                                   oh[:, k, :], ol[:, k, :], k == 0 and m == 0, k == KT - 1)
                    return mm

                for k in range(KT // 2):
                    for u in range(2):
                        tile(u, k)
                    for t0 in sums[k]:
                        norm_sums(where, norm, t0)
                for u in range(2):
                    for k in range(KT // 2, KT):
                        mm = tile(u, k)
                    mm.then_inc(unit_done.sem, 1)

            def last_down(where, vv, step):
                begin(where, vv, None)
                pe.wait_ge(g_ready.sem, g_ready.at(where, step + 1))
                s = vv % NS
                for c in range(4):
                    for m in (2 * c, 2 * c + 1):
                        for t in range(2):
                            w = t * D + m * P
                            mm = three(acc(m), w_hi[:, s, w:w + P], w_lo[:, s, w:w + P],
                                       g_hi[:, 0, t, :], g_lo[:, 0, t, :], False, t == 1)
                    mm.then_inc(acc_done.sem if c < 3 else unit_done.sem, 1)

            def ffn(where, vv, o, norm, steps0, sums):
                first_units(where, vv, o, norm, sums)
                clear_acc()
                with pe.Fori(0, STEPS // 2) as i:
                    for e in range(2):
                        b = 2 * ((e + 1) % 2)
                        unit(where, vv + 2 + 3 * e, o + 2 + 2 * e, b, h_hi, h_lo, i, 4, 4, norm if e == 0 else None)
                        unit(where, vv + 3 + 3 * e, o + 3 + 2 * e, b + 1, h_hi, h_lo, i, 4, 4)
                        down(where, vv + 4 + 3 * e, e, steps0 + e, i)
                last_down(where, vv + 3 * STEPS - 1, steps0 + STEPS - 1)

            def norm_sums(where, n, t0):
                for t in (t0, t0 + 1):
                    pe.wait_ge(sq_ready.sem, sq_ready.at(where, n * KT + t + 1))
                    pe.matmul(bank[2][:, 0:SEQ], mean, t4[:, t % 4, :], start=(t == 0), stop=(t == KT - 1),
                              skip_group_check=True).then_inc(sq_used.sem, 1)

            def tiles(where, vv, b, oh, ol, ks, first, last):
                s = vv % NS
                for k in ks:
                    for m in range(2):
                        c = k * UW + m * P
                        mm = three(bank[b][:, m * SEQ:(m + 1) * SEQ], w_hi[:, s, c:c + P], w_lo[:, s, c:c + P],
                                   oh[:, k, :], ol[:, k, :], k == first and m == 0, k == last)
                return mm

            def out_units(where, vv, o, norm, oh, ol, u0):
                for u in range(u0, 4):
                    unit(where, vv + u, o + u, u % 2, oh, ol)
                    if u >= 2:
                        norm_sums(where, norm, 2 * u - 4)

            def group_sums(where, n, sel):
                if n % 4 == 0 and n:
                    pe.wait_ge(gstd_ready.sem, gstd_ready.at(where, n // 4))
                pe.wait_ge(gsq_ready.sem, gsq_ready.at(where, n + 1))
                for m in range(2):
                    t = 2 * (n % 4) + m
                    mm = pe.matmul(bank[3][0:16, 0:SEQ], sel[:, 16 * t:16 * t + 16], t4[:, 2 * (n % 2) + m, :],
                                   start=(t == 0), stop=(t == KT - 1))
                mm.then_inc(gsq_used.sem, 1)

            def group_spread(where, n, q0, groups, banks):
                pe.wait_ge(grstd_ready.sem, grstd_ready.at(where, n + 1))
                for q, c in enumerate(groups, q0):
                    pe.wait_ge(bc_used.sem, bc_used.at(where, q - 1))
                    for m in range(2):
                        t = 2 * c + m
                        mm = pe.matmul(bank[banks[q % 2]][:, m * SEQ:(m + 1) * SEQ], spread[:, t * P:(t + 1) * P],
                                       rstd[0:16, :], start=True, stop=True)
                    mm.then_inc(bc_done.sem, 1)

            def scores(where, p):
                b, _ = where
                pe.wait_ge(logits_ready.sem, logits_ready.at(where, p))
                for m in range(2):
                    s = bank[4 + m]
                    if b == 1:
                        qt, kt = (p, 4 + p) if p < 4 else (8 + p - 4, 12 + p - 4)
                        r = slice(64 * m, 64 * m + 64)
                    else:
                        qt, kt = 2 * p + m, 8 + 2 * p + m
                        r = slice(0, P)
                    mm = pe.matmul(s[:, 0:256], qk[r, qt, 128:256], qk[r, kt, 0:256], start=True,
                                   stop=(b == 1), skip_group_check=True)
                    if b == 2:
                        if m == 0:
                            pe.wait_ge(decay_ready.sem, decay_ready.at(where, p + 1))
                        dc = decay[p % 2]
                        pe.matmul(s[:, 0:256], tri, dc[:, m, 0:256], start=False, stop=False,
                                  skip_group_check=True)
                        pe.matmul(s[:, 0:128], one_u[:, 0:128], dc[:, m, 256:384], start=False, stop=True,
                                  skip_group_check=True)
                    mm = pe.matmul(s[:, 256:384], qk[r, qt, 0:128], qk[r, kt, 0:128], start=True,
                                   stop=(b == 1), skip_group_check=True)
                    if b == 2:
                        mm = pe.matmul(s[:, 256:384], tri, dc[:, m, 256:384], start=False, stop=True,
                                       skip_group_check=True)
                mm.then_inc(scored.sem, 1)

            def turn(where, p):
                pe.wait_ge(probs_ready.sem, probs_ready.at(where, p + 1))
                pe.wait_ge(pt_ready.sem, pt_ready.at(where, p))
                maps = 1 if where[0] == 1 and p < 4 else 2
                for m in range(maps):
                    e = probs[:, p % 2, m, :]
                    for c, at in ((0, 256), (1, 0), (2, 128)):
                        mm = pe.transpose(bank[6 + m][:, 128 * c:128 * c + 128], e[:, at:at + 128], ident)
                mm.then_inc(turned.sem, 1)

            def weigh(where, p):
                pe.wait_ge(pt_ready.sem, pt_ready.at(where, p + 1))
                pe.wait_ge(att_out.sem, att_out.at(where, p))
                for m in range(2):
                    if where[0] == 1 and p < 4:
                        if m:
                            break
                        o, c0, n = bank[2][:, :], p * P, P
                    elif where[0] == 1:
                        o, c0, n = bank[2][64 * m:64 * m + 64, :], 512 + (2 * (p - 4) + m) * 64, 64
                    else:
                        o, c0, n = bank[2 + m][:, :], (2 * p + m) * P, P
                    pe.matmul(o[:, 0:256], v[:, 0, c0:c0 + n], probs_t[:, m, 0:256], start=True, stop=False,
                              skip_group_check=True)
                    mm = pe.matmul(o[:, 128:256], v[:, 1, c0:c0 + n], probs_t[:, m, 256:384], start=False,
                                   stop=True, skip_group_check=True)
                mm.then_inc(pv_done.sem, 1)

            def rest_of_attention(where):
                for p in range(4, 8):
                    turn(where, p)
                    if p + 2 < 8:
                        scores(where, p + 2)
                    if p == 6:
                        begin(where, V1_WOUT, O1_WOUT)
                    if p >= 6:
                        pe.wait_ge(att_out.sem, att_out.at(where, p - 1))
                        tiles(where, V1_WOUT, 0, y_hi, y_lo, (p - 2,), 4, None)
                    if p == 7:
                        pe.wait_ge(y_ready.sem, y_ready.at(where, 1))
                        tiles(where, V1_WOUT, 0, y_hi, y_lo, (0, 1, 2, 3), 4, None)
                    weigh(where, p)
                pe.wait_ge(att_out.sem, att_out.at(where, 7))
                tiles(where, V1_WOUT, 0, y_hi, y_lo, (6,), 4, None)
                pe.wait_ge(att_out.sem, att_out.at(where, 8))
                tiles(where, V1_WOUT, 0, y_hi, y_lo, (7,), 4, 7).then_inc(unit_done.sem, 1)

            pe.wait_ge(ld_cst, 34)
            pe.wait_ge(ld_x, 16)
            for c in range(4):
                for m in range(2):
                    for t in range(TB):
                        mm = pe.transpose(bank[c][:, m * SEQ + t * P:m * SEQ + (t + 1) * P],
                                          x_tok[:, t, (2 * c + m) * P:(2 * c + m + 1) * P], ident)
                mm.then_inc(pro_pe, 1)
            mm = pe.matmul(bank[7][:, :], zeros[:, 0:P], zeros[:, :], start=True, stop=True)
            mm.then_inc(unit_done.sem, NS)
            for k in range(4):
                pe.wait_ge(ld_par[k], 16 * PAR_DMAS[k])
                for l in range(LAYERS):
                    nr = PAR_ROWS[k]
                    mm = pe.transpose(bank[4 + k][:, 128 * l:128 * l + nr], prow[0:nr, k, l, :], ident[0:nr, 0:nr])
                mm.then_inc(pro_pe, 1)
                if k == 1:
                    pe.wait_ge(pro_dve, 4)
            pe.wait_ge(ld_rel, 32)
            pe.matmul(bank[3][0:BIAS_HEADS, 0:384], relb, onehot, start=True, stop=True).then_inc(pro_pe, 1)

            with pe.Fori(0, LAYERS) as l:
                where = (1, l)
                first_units(where, V1_WIN, O1_WIN, 0, ((0, 2), (4, 6), (), ()))
                for u in range(2, 12):
                    vv, o, b = V1_WIN + u, O1_WIN + u, u % 2
                    if u == 6:
                        unit(where, vv, o, b, h_hi, h_lo)
                        group_spread(where, 0, 0, (0, 2), (6, 7))
                        continue
                    if u % 6 < 4:
                        unit(where, vv, o, b, h_hi, h_lo, norm=0 if u == 2 else None)
                    else:
                        unit_tok(where, vv, o, b)
                    if u == 2:
                        group_sums(where, 0, g64)
                    if 1 <= u % 6 <= 4:
                        group_sums(where, 4 * (u // 6) + u % 6 - 1, g64)
                    if u == 7:
                        group_spread(where, 0, 2, (1, 3), (6, 7))
                        pe.wait_ge(bc_used.sem, bc_used.at(where, 2))
                        pe.wait_ge(evacuated.sem, evacuated.at(where, 6))
                        scores(where, 0)
                    if u == 8:
                        pe.wait_ge(bc_used.sem, bc_used.at(where, 4))
                        turn(where, 0)
                        scores(where, 1)
                    if u == 11:
                        group_spread(where, 1, 4, (0, 2), (3, 7))
                    if 9 <= u:
                        weigh(where, u - 9)
                        turn(where, u - 8)
                    if 9 <= u <= 10:
                        scores(where, u - 7)
                weigh(where, 3)
                pe.wait_ge(evacuated.sem, evacuated.at(where, 12))
                pe.wait_ge(dsq_ready.sem, dsq_ready.at(where, 1))
                for t in range(4):
                    mm = pe.matmul(bank[1][0:16, 0:SEQ], g128[:, 16 * t:16 * t + 16], t4[:, t, :],
                                   start=(t == 0), stop=(t == 3))
                mm.then_inc(dsq_used.sem, 1)
                group_spread(where, 1, 6, (1, 3), (3, 7))
                pe.wait_ge(bc_used.sem, bc_used.at(where, 6))
                pe.wait_ge(evacuated.sem, evacuated.at(where, 12))
                scores(where, 4)
                scores(where, 5)
                pe.wait_ge(bc_used.sem, bc_used.at(where, 8))
                group_spread(where, 2, 8, (0, 1), (1, 3))
                rest_of_attention(where)
                out_units(where, V1_WOUT, O1_WOUT, 1, y_hi, y_lo, 1)
                ffn(where, V1_FFN, O1_FFN, 1, 0, ((4,), (6,), (), ()))

            with pe.Fori(0, LAYERS) as l:
                where = (2, l)
                ffn(where, V2_FFN1, O2_FFN1, 0, 0, ((0, 2), (4, 6), (), ()))

                def lru_linear(j):
                    if j == 0:
                        pe.wait_ge(side_loaded.sem, l * 80 + 80)
                    pe.wait_ge(lru_conv.sem, lru_conv.at(where, j + 1))
                    for b, lin in ((4, lin_a), (5, lin_x)):
                        for m in range(2):
                            mm = pe.matmul(bank[b][:, m * SEQ:(m + 1) * SEQ], lin[:, 2 * j + m, :],
                                           lru_c[:, m, :], start=True, stop=True)
                    mm.then_inc(lru_lin.sem, 1)

                def forget_logits():
                    for t in range(TB):
                        for k in range(KT):
                            wh = wf_hi[:, bass.ds(l, 1), k, :].rearrange("p l h -> p (l h)")
                            wl = wf_lo[:, bass.ds(l, 1), k, :].rearrange("p l h -> p (l h)")
                            mm = three(bank[2][:, t * H2:(t + 1) * H2], h_hi[:, k, t * P:(t + 1) * P],
                                       h_lo[:, k, t * P:(t + 1) * P], wh, wl, k == 0, k == KT - 1)
                    mm.then_inc(f_done.sem, 1)

                for j in range(4):
                    vv, o = V2_WIN + 3 * j, O2_WIN + 3 * j
                    if j == 0:
                        first_units(where, vv, o, 1, ((0, 2), (4, 6), (), ()))
                    else:
                        unit(where, vv, o, o % 2, h_hi, h_lo)
                        group_sums(where, j - 1, g128)
                        unit(where, vv + 1, o + 1, (o + 1) % 2, h_hi, h_lo)
                    unit(where, vv + 2, o + 2, (o + 2) % 2, h_hi, h_lo, norm=1 if j == 0 else None)
                    if j == 0:
                        forget_logits()
                    lru_linear(j)
                for j in range(4):
                    o = O2_WIN + 12 + j
                    unit(where, V2_WIN + 12 + j, o, o % 2, h_hi, h_lo)
                    group_sums(where, 3 + j, g128)
                    if j >= 2:
                        group_spread(where, 0, 2 * j - 4, (2 * j - 4, 2 * j - 3), (6, 7))
                for j in range(4):
                    o = O2_WIN + 16 + j
                    unit_tok(where, V2_WIN + 16 + j, o, o % 2)
                    if j == 0:
                        group_sums(where, 7, g128)
                    if 1 <= j <= 2:
                        group_spread(where, 1, 2 + 2 * j, (2 * j - 2, 2 * j - 1), (6, 7))
                    if j == 2:
                        pe.wait_ge(bc_used.sem, bc_used.at(where, 5))
                        scores(where, 0)
                    if j == 3:
                        pe.wait_ge(bc_used.sem, bc_used.at(where, 8))
                        turn(where, 0)
                        scores(where, 1)
                for j in range(8):
                    vv, o = V2_GATED + 2 * j, O2_GATED + 2 * j
                    unit(where, vv, o, 0, h_hi, h_lo)
                    if j == 0:
                        pe.wait_ge(evacuated.sem, evacuated.at(where, O2_GATED))
                        weigh(where, 0)
                        turn(where, 1)
                        scores(where, 2)
                        pe.wait_ge(r_ready.sem, r_ready.at(where, 4))
                    if j == 1:
                        weigh(where, 2)
                        turn(where, 3)
                    if j == 4:
                        pe.wait_ge(y_ready.sem, y_ready.at(where, 1))
                    oh, ol = (r_hi, r_lo) if j < 4 else (y_hi, y_lo)
                    unit(where, vv + 1, o + 1, 1, oh, ol)
                    if j == 0:
                        weigh(where, 1)
                        turn(where, 2)
                        scores(where, 3)
                    if j == 1:
                        weigh(where, 3)
                for u in range(2):
                    begin(where, V2_WOUT + u, O2_WOUT + u)
                for c in range(3):
                    pe.wait_ge(m_ready.sem, m_ready.at(where, c + 1))
                    for u in range(2):
                        tiles(where, V2_WOUT + u, u, r_hi, r_lo, (2 * c, 2 * c + 1), 0, None)
                pe.wait_ge(m_ready.sem, m_ready.at(where, 4))
                for u in range(2):
                    tiles(where, V2_WOUT + u, u, r_hi, r_lo, (6, 7), 0, 7).then_inc(unit_done.sem, 1)
                out_units(where, V2_WOUT, O2_WOUT, 2, r_hi, r_lo, 2)
                ffn(where, V2_FFN2, O2_FFN2, 2, STEPS, ((4,), (6,), (), ()))

            for t0 in (0, 2, 4, 6):
                norm_sums((2, LAYERS), 0, t0)
            for c in range(4):
                pe.wait_ge(x_ready.sem, x_ready.at((2, LAYERS), 2 * c + 2))
                for m in range(2):
                    for t in range(TB):
                        mm = pe.transpose(bank[4 + c][:, t * 256 + m * P:t * 256 + (m + 1) * P],
                                          x[:, 2 * c + m, t * P:(t + 1) * P], ident)
                mm.then_inc(fin_pe, 1)

        @block_.scalar
        def _(act):
            own = Chain(act, act_own)
            A = nc.scalar.activation

            def split_hi(where, vv, i=0):
                s = vv % NS
                act.wait_ge(raw_full[s], full_at(where, vv, i))
                act.wait_ge(unit_done.sem, unit_done.at(where, vv + 1 - NS) + i * 6)
                per = {1: V1, 2: V2}[where[0]]
                A(w_hi[:, s, :], raw[:, s, :], ACT.Copy).then_inc(hi_ready.sem, raises(where[0], vv % per))

            def next_hi(where, vv, i=0):
                skip = LAST_BEFORE_SKIP[where[0]]
                if not skip < vv + NS <= skip + SKIP:
                    split_hi(where, vv + NS, i)

            def guarded_hi(where, vv, i, last):
                if last is None:
                    next_hi(where, vv, i)
                else:
                    with act.If(last < LAYERS * (STEPS // 2) - 1):
                        next_hi(where, vv, i)

            def unit_wait(where, vv, i=0):
                act.wait_ge(unit_done.sem, unit_done.at(where, vv + 1) + i * 6)

            def tiles_of_norm(where, n, t0, count, gain):
                if t0 == 0:
                    A(warm[:, 0:1], eps[0:1, :], ACT.Sqrt)
                oh, _ = raw_h(where, n)
                for c in range(t0, t0 + count, 2):
                    for t in (c, c + 1):
                        act.wait_ge(x_ready.sem, x_ready.at(where, n * KT + t + 1))
                        if t >= 4:
                            act.wait_ge(sq_used.sem, sq_used.at(where, n * KT + t - 3))
                        A(t4[:, t % 4, :], x[:, t, :], ACT.Square).then_inc(sq_ready.sem, 1)
                    for t in (c, c + 1):
                        A(oh[:, t, :], x[:, t, :], ACT.Identity, scale=gain(t)).then_inc(rh_hi.sem, 1)

            def deviation(where, n):
                act.wait_ge(sq_used.sem, sq_used.at(where, n * KT + KT))
                A(std[:, :], bank[2][:, 0:SEQ], ACT.Sqrt, bias=eps[:, :]).then_inc(std_ready.sem, 1)

            def norm(where, n):
                for t in range(KT):
                    act.wait_ge(hf_ready.sem, hf_ready.at(where, n * KT + t + 1))
                    A(h_hi[:, t, :], t4[:, t % 4, :], ACT.Copy).then_inc(hh_ready.sem, 1)

            def ffn1_step(where, vv, step, i=0):
                for half, dst in ((0, gate_s), (1, up_s)):
                    if half == 0:
                        act.wait_ge(prm_ready.sem, prm_ready.at(where, step + 1) + i * 2)
                    if step == 0:
                        if half == 0:
                            next_hi(where, vv)
                        act.wait_ge(scaled.sem, scaled.at(where, 2 + half + 1))
                        src = (gate_n, up_n)[half]
                    else:
                        unit_wait(where, vv + half, i)
                        src = bank[2 * PAR(step) + half][:, :].rearrange("p (m s) -> p m s", m=2)
                    for m in range(2):
                        last = A(dst[:, m, :], src[:, m, :], ACT.Identity,
                                 bias=prm[:, PAR(step), 0, half, m:m + 1], scale=prm[:, PAR(step), 1, half, m:m + 1])
                    last.then_inc(conv_main.sem, 1)
                    if half == 0:
                        if step:
                            next_hi(where, vv, i)
                        else:
                            next_hi(where, vv + 1)
                        act.wait_ge(evacuated.sem, evacuated.at(where, O1_FFN + 2 * step + 1) + i * 4)
                        A(gate_s, gate_s, ACT.Silu).then_inc(silu_ready.sem, 1)
                act.wait_ge(prod_ready.sem, prod_ready.at(where, step + 1) + i * 2)
                A(g_hi[:, PAR(step), :, :], prod_s, ACT.Copy).then_inc(prod_hi.sem, 1)
                if step:
                    next_hi(where, vv + 1, i)

            def ffn2_step(where, vv, step, n, i=0, last=None):
                if step == 0:
                    next_hi(where, vv)
                    act.wait_ge(scaled.sem, scaled.at(where, (4 if n else 0) + 1))
                    A(gate_s, gate_n, ACT.Silu).then_inc(silu_ready.sem, 1)
                else:
                    unit_wait(where, vv, i)
                    gate = bank[2 * PAR(step)][:, :].rearrange("p (m s) -> p m s", m=2)
                    A(gate_s, gate, ACT.Silu).then_inc(silu_ready.sem, 1)
                    next_hi(where, vv, i)
                act.wait_ge(prod_ready.sem, prod_ready.at(where, n + step + 1) + i * 2)
                A(g_hi[:, PAR(step), :, :], prod_s, ACT.Copy).then_inc(prod_hi.sem, 1)
                guarded_hi(where, vv + 1, i, last)

            def ffn(where, vv, one_step, norm, gain, last_layer=None):
                one_step(vv, 0, 0, None)
                own.restart()
                with act.Fori(0, STEPS // 2) as i:
                    for e in range(2):
                        last = None if last_layer is None or e == 0 else last_layer * (STEPS // 2) + i
                        one_step(vv + 2 + 3 * e, 1 + e, i, last)
                        guarded_hi(where, vv + 4 + 3 * e, i, last)
                    own.restart()
                tiles_of_norm(where, norm + 1, 0, KT, gain)
                if last_layer is None:
                    split_hi(where, vv + 3 * STEPS + 2)
                else:
                    with act.If(last_layer < LAYERS - 1):
                        split_hi(where, vv + 3 * STEPS + 2)
                    A(warm[:, 1:2], eps[0:1, :], ACT.Sqrt)
                deviation(where, norm + 1)

            def group_std(where, n):
                act.wait_ge(gsq_used.sem, gsq_used.at(where, 4 * n + 4))
                if n:
                    act.wait_ge(grstd_ready.sem, grstd_ready.at(where, n))
                A(std[0:16, :], bank[3][0:16, 0:SEQ], ACT.Sqrt, bias=eps[0:16, :]).then_inc(gstd_ready.sem, 1)

            def exps(where, p):
                act.wait_ge(logits_ready.sem, logits_ready.at(where, p + 1))
                e = p % 2
                for m in range(2):
                    for c, cs in ((0, slice(0, 256)), (1, slice(256, 384))):
                        n = 2 * m + c
                        last = A(probs[:, e, m, cs], probs[:, e, m, cs], ACT.Exp, bias=nmax[:, e, n:n + 1],
                                 scale=-1.0, accum_out=esum[:, e, n:n + 1])
                last.then_inc(exp_ready.sem, 1)

            def copy_turned(where, p):
                act.wait_ge(turned.sem, turned.at(where, p + 1))
                act.wait_ge(pv_done.sem, pv_done.at(where, p))
                for m in range(1 if where[0] == 1 and p < 4 else 2):
                    last = A(probs_t[:, m, :], bank[6 + m][:, 0:384], ACT.Copy)
                last.then_inc(pt_ready.sem, 1)

            def att_high(where, p):
                act.wait_ge(pv_done.sem, pv_done.at(where, p + 1))
                if where[0] == 1 and p < 4:
                    A(qk[:, p, :], bank[2][:, 0:SEQ], ACT.Copy).then_inc(att_out.sem, 1)
                elif where[0] == 1:
                    A(y_hi[:, p, :], bank[2][:, 0:SEQ], ACT.Copy).then_inc(att_hi.sem, 1)
                else:
                    for m in range(2):
                        last = A(y_hi[:, 2 * p + m, :], bank[2 + m][:, 0:SEQ], ACT.Copy)
                    last.then_inc(att_hi.sem, 1)

            def rest_of_attention(where):
                skipped = LAST_BEFORE_SKIP[1] + 1 + NS
                act.wait_ge(att_out.sem, att_out.at(where, 4))
                A(t4[:, :, :], qk[:, 0:4, :], ACT.Square).then_inc(dsq_ready.sem, 1)
                act.wait_ge(dsq_used.sem, dsq_used.at(where, 1))
                act.wait_ge(grstd_ready.sem, grstd_ready.at(where, 2))
                A(std[0:16, :], bank[1][0:16, 0:SEQ], ACT.Sqrt, bias=eps[0:16, :]).then_inc(gstd_ready.sem, 1)
                exps(where, 4)
                exps(where, 5)
                for p in range(4, 8):
                    copy_turned(where, p)
                    if p == 4:
                        for t in range(4):
                            act.wait_ge(dn_ready.sem, dn_ready.at(where, t + 1))
                            A(y_hi[:, t, :], t4[:, t, :], ACT.Copy).then_inc(dn_hi.sem, 1)
                    if p + 2 < 8:
                        exps(where, p + 2)
                    att_high(where, p)
                    if p == 6:
                        split_hi(where, skipped)

            def out_phase(where, vv, n, col):
                for u in range(4):
                    if u < 3:
                        next_hi(where, vv + u)
                    tiles_of_norm(where, n, 2 * u, 2, lambda t: cur[:, col + t:col + t + 1])
                split_hi(where, vv + 6)
                deviation(where, n)

            for kind, dst, src in param_loads(a, prow):
                if kind < 2:
                    act.dma_start(dst, src).then_inc(ld_par[kind], 16)
            act.wait_ge(ld_cst, 34)
            act.wait_ge(raw_full[0], 16)
            A(w_hi[:, 0, :], raw[:, 0, :], ACT.Copy).then_inc(hi_ready.sem, 1)
            act.wait_ge(raw_full[1], 16)
            A(w_hi[:, 1, :], raw[:, 1, :], ACT.Copy).then_inc(hi_ready.sem, 1)
            act.wait_ge(pro_dve, 5)
            tiles_of_norm((1, 0), 0, 0, KT, lambda t: first_gain[:, 0, t:t + 1])
            act.wait_ge(raw_full[2], 16)
            A(w_hi[:, 2, :], raw[:, 2, :], ACT.Copy).then_inc(hi_ready.sem, 1)
            act.wait_ge(ld_wf, 16 * (1 + LAYERS * (TB + 1)))
            A(wf_hi[:, :, :, :].rearrange("p l k h -> p (l k h)"), wf_raw[:, :, :, :].rearrange("p l k h -> p (l k h)"),
              ACT.Copy).then_inc(pro_act, 1)
            act.wait_ge(pro_dve, 10)
            A(lgs[:, 7, 4:8], lgs[:, 7, 0:4], ACT.Exp).then_inc(pro_act, 1)
            act.wait_ge(pro_dve, 11)
            own.link(A(lgs[:, 1, :], lgs[:, 0, :], ACT.Exp))
            own.wait()
            A(lgs[:, 2, :], lgs[:, 1, :], ACT.Ln, bias=1.0).then_inc(pro_act, 1)
            deviation((1, 0), 0)
            own.restart()

            with act.Fori(0, LAYERS) as l:
                where = (1, l)
                A(warm[:, 2:3], eps[0:1, :], ACT.Copy)
                norm(where, 0)
                act.wait_ge(cur_ready.sem, cur_ready.at(where, 1))
                for u in range(12):
                    vv, b = V1_WIN + u, u % 2
                    if u < 2:
                        next_hi(where, vv)
                        if u == 0:
                            act.wait_ge(h_ready.sem, h_ready.at(where, KT))
                        act.wait_ge(scaled.sem, scaled.at(where, u + 1))
                        A(t4[:, 2 * u:2 * u + 2, :], qk[:, 2 * u:2 * u + 2, :], ACT.Square
                          ).then_inc(gsq_ready.sem, 1)
                        continue
                    unit_wait(where, vv)
                    if u % 6 < 4:
                        n = 4 * (u // 6) + u % 6
                        t = 8 * (u // 6) + 2 * (u % 6)
                        two = bank[b][:, :].rearrange("p (m s) -> p m s", m=2)
                        A(qk[:, t:t + 2, :], two, ACT.Copy)
                        act.wait_ge(gsq_used.sem, gsq_used.at(where, n - 1))
                        last = A(t4[:, 2 * (n % 2):2 * (n % 2) + 2, :], two, ACT.Square)
                        own.link(last)
                        own.wait()
                        act.sem_inc(gsq_ready.sem, 1)
                        act.sem_inc(evacuated.sem, 1)
                    else:
                        c = 512 * (u // 6) + UW * (u % 6 - 4)
                        A(v[:, :, c:c + UW], bank[b][:, :].rearrange("p (t c) -> p t c", t=TB), ACT.Copy
                          ).then_inc(evacuated.sem, 1)
                    next_hi(where, vv)
                    if u == 4:
                        group_std(where, 0)
                    if u == 10:
                        group_std(where, 1)
                    if 9 <= u:
                        att_high(where, u - 9)
                    if 8 <= u:
                        copy_turned(where, u - 8)
                    if 7 <= u <= 10:
                        exps(where, u - 7)
                att_high(where, 3)
                rest_of_attention(where)
                split_hi(where, LAST_BEFORE_SKIP[1] + 2 + NS)
                out_phase(where, V1_WOUT, 1, C1_FFN)
                norm(where, 1)
                ffn(where, V1_FFN, lambda vv, step, i, last: ffn1_step(where, vv, step, i), 1,
                    lambda t: gain_of(l + 1, t))
                own.restart()

            with act.Fori(0, LAYERS) as l:
                where = (2, l)
                A(warm[:, 3:4], eps[0:1, :], ACT.Copy)
                norm(where, 0)
                act.wait_ge(cur_ready.sem, cur_ready.at(where, 1))
                ffn(where, V2_FFN1, lambda vv, step, i, last: ffn2_step(where, vv, step, 0, i), 0,
                    lambda t: cur[:, C2_MIX + t:C2_MIX + t + 1])
                norm(where, 1)

                def lru_gates_(j):
                    act.wait_ge(lru_lin.sem, lru_lin.at(where, j + 1))
                    if j:
                        act.wait_ge(r_ready.sem, r_ready.at(where, j))
                    for b, dst, cb in ((4, lru_r, C2_BA), (5, lru_i, C2_BX)):
                        for m in range(2):
                            t = 2 * j + m
                            k = own.link(A(dst[:, m, :], bank[b][:, m * SEQ:(m + 1) * SEQ], ACT.Sigmoid,
                                           bias=cur[:, cb + t:cb + t + 1]))
                            if b == 4:
                                kr = k
                    own.wait(kr)
                    for m in range(2):
                        t = 2 * j + m
                        own.link(A(lru_t[:, m, :], lru_r[:, m, :], ACT.Tanh, scale=cur[:, C2_POS + t:C2_POS + t + 1]))
                    for m in range(2):
                        t = 2 * j + m
                        own.link(A(lru_a[:, m, :], lru_r[:, m, :], ACT.Exp, scale=cur[:, C2_LAM + t:C2_LAM + t + 1]))
                    own.wait()
                    A(lru_r, lru_a, ACT.Square).then_inc(lru_gates.sem, 1)

                def lru_root(j):
                    act.wait_ge(lru_m.sem, lru_m.at(where, j + 1))
                    A(lru_r, lru_r, ACT.Sqrt).then_inc(lru_sqrt.sem, 1)

                def lru_high(j):
                    act.wait_ge(lru_y.sem, lru_y.at(where, j + 1))
                    A(r_hi[:, 2 * j:2 * j + 2, :], lru_r, ACT.Copy).then_inc(lru_hi.sem, 1)

                def qk_unit(n, vv, b):
                    next_hi(where, vv)
                    act.wait_ge(gsq_used.sem, gsq_used.at(where, n - 1))
                    for m in range(2):
                        t = 2 * n + m
                        src = bank[b][:, m * SEQ:(m + 1) * SEQ]
                        cb = cur[:, C2_BQK + t:C2_BQK + t + 1]
                        own.link(A(qk[:, t, :], src, ACT.Identity, bias=cb))
                        own.link(A(t4[:, 2 * (n % 2) + m, :], src, ACT.Square, bias=cb))
                    own.wait()
                    act.sem_inc(gsq_ready.sem, 1)
                    act.sem_inc(evacuated.sem, 1)

                for j in range(4):
                    vv, o = V2_WIN + 3 * j, O2_WIN + 3 * j
                    next_hi(where, vv)
                    if j:
                        lru_root(j - 1)
                    next_hi(where, vv + 1)
                    if j:
                        lru_high(j - 1)
                    if j == 0:
                        act.wait_ge(scaled.sem, scaled.at(where, 4))
                        src = lru_g
                    else:
                        act.wait_ge(evacuated.sem, evacuated.at(where, o + 1))
                        src = bank[(o + 1) % 2][:, :].rearrange("p (m s) -> p m s", m=2)
                    for m in range(2):
                        t = 2 * j + m
                        last = A(lru_g[:, m, :], src[:, m, :], ACT.Gelu_apprx_tanh,
                                 bias=cur[:, C2_BREST + KT + t:C2_BREST + KT + t + 1])
                    if j:
                        last.then_inc(evacuated.sem, 1)
                    qk_unit(j, vv + 2, (o + 2) % 2)
                    lru_gates_(j)
                for j in range(4):
                    qk_unit(4 + j, V2_WIN + 12 + j, (O2_WIN + 12 + j) % 2)
                    if j == 0:
                        lru_root(3)
                        group_std(where, 0)
                    if j == 1:
                        lru_high(3)
                        act.wait_ge(f_abs.sem, f_abs.at(where, 1))
                        own.link(A(lgs[:, 1, :], lgs[:, 0, :], ACT.Exp))
                        own.wait()
                        A(lgs[:, 2, :], lgs[:, 1, :], ACT.Ln, bias=1.0).then_inc(f_exp.sem, 1)
                skipped = LAST_BEFORE_SKIP[2] + 1 + NS
                for j in range(4):
                    next_hi(where, V2_WIN + 16 + j)
                    if j == 0:
                        group_std(where, 1)
                    if j == 2:
                        exps(where, 0)
                    if j == 3:
                        copy_turned(where, 0)
                        exps(where, 1)
                        split_hi(where, skipped)
                for j in range(8):
                    vv = V2_GATED + 2 * j
                    unit_wait(where, vv)
                    act.wait_ge(evacuated.sem, evacuated.at(where, O2_GATED + 2 * j))
                    for m in range(2):
                        cb = C2_BREST + (24 if j < 4 else 16) + 2 * (j % 4) + m
                        own.link(A(sig_s[:, m, :], bank[0][:, m * SEQ:(m + 1) * SEQ], ACT.Sigmoid,
                                   bias=cur[:, cb:cb + 1]))
                    own.wait()
                    act.sem_inc(sig_ready.sem, 1)
                    act.sem_inc(evacuated.sem, 1)
                    if j == 0:
                        split_hi(where, skipped + 1)
                    if j < 2:
                        att_high(where, 2 * j)
                        copy_turned(where, 2 * j + 1)
                    if j == 0:
                        exps(where, 2)
                    next_hi(where, vv)
                    next_hi(where, vv + 1)
                    if j < 2:
                        att_high(where, 2 * j + 1)
                    if j == 0:
                        copy_turned(where, 2)
                        exps(where, 3)
                    if j >= 4:
                        act.wait_ge(merged_ready.sem, merged_ready.at(where, j - 3))
                        A(r_hi[:, 2 * j - 8:2 * j - 6, :], part_s, ACT.Copy).then_inc(merged_hi.sem, 1)
                out_phase(where, V2_WOUT, 2, C2_FFN2)
                norm(where, 2)
                own.restart()
                ffn(where, V2_FFN2, lambda vv, step, i, last: ffn2_step(where, vv, step, STEPS, i, last), 2,
                    lambda t: gain_of(l + 3, t), l)
                own.restart()

            for c in range(4):
                act.wait_ge(fin_pe, c + 1)
                A(x_tok[:, :, 256 * c:256 * (c + 1)], bank[4 + c][:, :].rearrange("p (t c) -> p t c", t=TB), ACT.Copy
                  ).then_inc(fin_sb, 1)

        @block_.vector
        def _(dve):
            own = Chain(dve, dve_own)
            V = nc.vector

            def lo_part(dst, src, hi):
                return V.tensor_tensor(dst, src, hi.bitcast(F32), ALU.subtract)

            def split_lo(where, vv, i=0):
                s = vv % NS
                dve.wait_ge(hi_ready.sem, hi_ready.at(where, vv + 1) + i * 6)
                per = {1: V1, 2: V2}[where[0]]
                lo_part(w_lo[:, s, :], raw[:, s, :], w_hi[:, s, :]).then_inc(
                    lo_ready.sem, raises(where[0], vv % per))

            def next_lo(where, vv, i=0):
                skip = LAST_BEFORE_SKIP[where[0]]
                if not skip < vv + NS <= skip + SKIP:
                    split_lo(where, vv + NS, i)

            def guarded_lo(where, vv, i, last):
                if last is None:
                    next_lo(where, vv, i)
                else:
                    with dve.If(last < LAYERS * (STEPS // 2) - 1):
                        next_lo(where, vv, i)

            def unit_wait(where, vv, i=0):
                dve.wait_ge(unit_done.sem, unit_done.at(where, vv + 1) + i * 6)

            def reciprocal_deviation(where, n):
                dve.wait_ge(std_ready.sem, std_ready.at(where, n + 1))
                own.link(V.reciprocal(rstd[:, :], std[:, :]))

            def normed(where, n, u, vv, dst, gives_bank=True):
                unit_wait(where, vv + u)
                for m in range(2):
                    last = V.tensor_tensor(dst[:, m, :], bank[u][:, m * SEQ:(m + 1) * SEQ], rstd[:, :], ALU.mult)
                own.link(last)
                own.wait()
                if gives_bank:
                    dve.sem_inc(evacuated.sem, 1)
                dve.sem_inc(scaled.sem, 1)

            def norm(where, n, col, vv, dst, gives_bank=True):
                own.wait()
                for t in range(KT + 1):
                    if t < KT:
                        V.scalar_tensor_tensor(out=t4[:, t % 4, :], in0=x[:, t, :], scalar=cur[:, col + t:col + t + 1],
                                               in1=rstd[:, :], op0=ALU.mult, op1=ALU.mult).then_inc(hf_ready.sem, 1)
                    if t:
                        dve.wait_ge(hh_ready.sem, hh_ready.at(where, n * KT + t))
                        lo_part(h_lo[:, t - 1, :], t4[:, (t - 1) % 4, :], h_hi[:, t - 1, :]).then_inc(h_ready.sem, 1)
                    if t == KT // 2:
                        normed(where, n, 0, vv, dst, gives_bank)

            def raw_low(where, n, tiles, gain):
                oh, ol = raw_h(where, n)
                for t in tiles:
                    dve.wait_ge(rh_hi.sem, rh_hi.at(where, n * KT + t + 1))
                    V.scalar_tensor_tensor(out=ol[:, t, :], in0=x[:, t, :], scalar=gain(t),
                                           in1=oh[:, t, :].bitcast(F32), op0=ALU.mult, op1=ALU.subtract
                                           ).then_inc(rh_ready.sem, 1)

            def add_down(where, vv, nth, scale, n, gain, last_layer):
                for t in range(KT):
                    if t % 2 == 0 and t < 6:
                        dve.wait_ge(acc_done.sem, acc_done.at(where, 3 * nth + t // 2 + 1))
                    if t == 6:
                        unit_wait(where, vv)
                    V.scalar_tensor_tensor(out=x[:, t, :], in0=acc(t), scalar=scale, in1=x[:, t, :],
                                           op0=ALU.mult, op1=ALU.add).then_inc(x_ready.sem, 1)
                    if t % 2 and t > 1:
                        raw_low(where, n, (t - 3, t - 2), gain)
                raw_low(where, n, (6, 7), gain)
                if last_layer is None:
                    split_lo(where, vv + 3)
                else:
                    with dve.If(last_layer < LAYERS - 1):
                        split_lo(where, vv + 3)
                reciprocal_deviation(where, n)

            def out_phase(where, vv, n, col):
                for u in range(4):
                    unit_wait(where, vv + u)
                    for m in range(2):
                        t = 2 * u + m
                        V.tensor_tensor(x[:, t, :], bank[u % 2][:, m * SEQ:(m + 1) * SEQ], x[:, t, :], ALU.add
                                        ).then_inc(x_ready.sem, 1)
                    dve.wait_ge(x_ready.sem, x_ready.at(where, n * KT + 2 * u + 2))
                    dve.sem_inc(evacuated.sem, 1)
                    if u < 3:
                        next_lo(where, vv + u)
                    raw_low(where, n, (2 * u, 2 * u + 1), lambda t: cur[:, col + t:col + t + 1])
                split_lo(where, vv + 6)
                reciprocal_deviation(where, n)

            def product(where, step, n, i, gate, up):
                dve.wait_ge(silu_ready.sem, silu_ready.at(where, n + step + 1) + i * 2)
                if where[0] == 2:
                    dve.wait_ge(g_ready.sem, g_ready.at(where, n + step) + i * 2)
                own.link(V.tensor_tensor(prod_s, gate, up, ALU.mult))
                own.wait()
                dve.sem_inc(prod_ready.sem, 1)

            def product_lo(where, step, n, i):
                dve.wait_ge(prod_hi.sem, prod_hi.at(where, n + step + 1) + i * 2)
                lo_part(g_lo[:, PAR(step), :, :], prod_s, g_hi[:, PAR(step), :, :]).then_inc(g_ready.sem, 1)

            def step_params(where, step, i):
                kinds = cur[:, C1_CONV:C1_CONV + 8 * FT].rearrange("p (k f t) -> p k f t", k=4, f=2)
                at = i * 4 + 2 * step
                for half in range(2):
                    src = kinds[:, :, half, bass.ds(at, 2)]
                    last = V.tensor_copy(prm[:, PAR(step), :, half, :], src)
                own.link(last)
                own.wait()
                dve.sem_inc(prm_ready.sem, 1)

            def ffn1_step(where, vv, step, i=0):
                step_params(where, step, i)
                par = PAR(step)
                for half, dst in ((0, gate_s), (1, up_s)):
                    src = bank[2 * par + half][:, :].rearrange("p (m s) -> p m s", m=2)
                    if step == 0:
                        next_lo(where, vv + half)
                        if half == 0:
                            normed(where, 1, 1, vv, up_n, False)
                        src = (gate_n, up_n)[half]
                    dve.wait_ge(conv_main.sem, conv_main.at(where, 2 * step + half + 1) + i * 4)
                    ks = []
                    for tap, kind in ((1, 3), (2, 2)):
                        for m in range(2):
                            if tap == 2:
                                own.wait(ks[m])
                            ks.append(own.link(V.scalar_tensor_tensor(
                                out=dst[:, m, tap:SEQ], in0=src[:, m, 0:SEQ - tap],
                                scalar=prm[:, par, kind, half, m:m + 1], in1=dst[:, m, tap:SEQ],
                                op0=ALU.mult, op1=ALU.add)))
                    own.wait()
                    dve.sem_inc(evacuated.sem, 1)
                    if step and half == 0:
                        next_lo(where, vv, i)
                product(where, step, 0, i, gate_s, up_s)
                product_lo(where, step, 0, i)
                if step:
                    next_lo(where, vv + 1, i)

            def ffn2_step(where, vv, step, n, i=0, last=None):
                next_lo(where, vv, i)
                if step == 0:
                    normed(where, 2 if n else 0, 1, vv, up_n, False)
                    up = up_n
                else:
                    unit_wait(where, vv + 1, i)
                    up = bank[2 * PAR(step) + 1][:, :].rearrange("p (m s) -> p m s", m=2)
                product(where, step, n, i, gate_s, up)
                dve.sem_inc(evacuated.sem, 2)
                product_lo(where, step, n, i)
                guarded_lo(where, vv + 1, i, last)

            def ffn(where, vv, one_step, nth, scale, n, gain, last_layer=None):
                one_step(vv, 0, 0, None)
                own.restart()
                with dve.Fori(0, STEPS // 2) as i:
                    for e in range(2):
                        last = None if last_layer is None or e == 0 else last_layer * (STEPS // 2) + i
                        one_step(vv + 2 + 3 * e, 1 + e, i, last)
                        guarded_lo(where, vv + 4 + 3 * e, i, last)
                    own.restart()
                add_down(where, vv + 3 * STEPS - 1, nth, scale, n, gain, last_layer)

            def group_rstd(where, n):
                dve.wait_ge(gstd_ready.sem, gstd_ready.at(where, n + 1))
                V.reciprocal(rstd[0:16, :], std[0:16, :]).then_inc(grstd_ready.sem, 1)

            def group_apply(where, q0, groups, tile0, gains, banks):
                for q, c in enumerate(groups, q0):
                    dve.wait_ge(bc_done.sem, bc_done.at(where, q + 1))
                    for m in range(2):
                        t = tile0 + 2 * c + m
                        g = gains[(2 * c + m) // 4]
                        own.link(V.scalar_tensor_tensor(
                            out=qk[:, t, :], in0=qk[:, t, :], scalar=cur[:, g:g + 1],
                            in1=bank[banks[q % 2]][:, m * SEQ:(m + 1) * SEQ], op0=ALU.mult, op1=ALU.mult))
                    own.wait()
                    dve.sem_inc(bc_used.sem, 1)

            def logits(where, p):
                dve.wait_ge(scored.sem, scored.at(where, p + 1))
                dve.wait_ge(turned.sem, turned.at(where, p - 1))
                own.tick()
                e = p % 2
                for m in range(2):
                    if where[0] == 1:
                        h = p if p < 4 else 4 + 2 * (p - 4) + m
                        add = bias[:, h, ::-1]
                    else:
                        add = mask
                    for c, ps, ad in ((0, slice(0, 256), add), (1, slice(256, 384), add[:, 128:256])):
                        n = 2 * m + c
                        last = V.tensor_tensor_reduce(out=probs[:, e, m, ps], in0=bank[4 + m][:, ps], in1=ad,
                                                      scale=-1.0, scalar=3e38, op0=ALU.add, op1=ALU.min,
                                                      accum_out=nmax[:, e, n:n + 1])
                last.then_inc(logits_ready.sem, 1)

            def normalise(where, p, l):
                dve.wait_ge(exp_ready.sem, exp_ready.at(where, p + 1))
                e = p % 2
                own.link(V.reciprocal(esc[:, e, :], esum[:, e, :]))
                own.wait()
                if where[0] == 1 and p < 4:
                    own.link(V.tensor_scalar(esc[:, e, 2:4], esc[:, e, 2:4], neglam[:, bass.ds(l, 1)], None, ALU.mult))
                    for c, cs in ((0, slice(0, 256)), (1, slice(256, 384))):
                        own.link(V.tensor_scalar(probs[:, e, 0, cs], probs[:, e, 0, cs], esc[:, e, c:c + 1], None,
                                                 ALU.mult))
                    own.wait()
                    for c, cs in ((0, slice(0, 256)), (1, slice(256, 384))):
                        last = V.scalar_tensor_tensor(out=probs[:, e, 0, cs], in0=probs[:, e, 1, cs],
                                                      scalar=esc[:, e, 2 + c:3 + c], in1=probs[:, e, 0, cs],
                                                      op0=ALU.mult, op1=ALU.add)
                else:
                    for m in range(2):
                        for c, cs in ((0, slice(0, 256)), (1, slice(256, 384))):
                            n = 2 * m + c
                            last = V.tensor_scalar(probs[:, e, m, cs], probs[:, e, m, cs], esc[:, e, n:n + 1], None,
                                                   ALU.mult)
                last.then_inc(probs_ready.sem, 1)

            def att_low(where, p):
                if where[0] == 1 and p < 4:
                    return
                dve.wait_ge(att_hi.sem, att_hi.at(where, p - 3 if where[0] == 1 else p + 1))
                if where[0] == 1:
                    last = lo_part(y_lo[:, p, :], bank[2][:, 0:SEQ], y_hi[:, p, :])
                else:
                    for m in range(2):
                        last = lo_part(y_lo[:, 2 * p + m, :], bank[2 + m][:, 0:SEQ], y_hi[:, 2 * p + m, :])
                last.then_inc(att_out.sem, 1)

            def rest_of_attention(where, l):
                logits(where, 4)
                group_rstd(where, 2)
                logits(where, 5)
                normalise(where, 4, l)
                for c in range(2):
                    dve.wait_ge(bc_done.sem, bc_done.at(where, 8 + c + 1))
                    for m in range(2):
                        t = 2 * c + m
                        own.link(V.scalar_tensor_tensor(
                            out=t4[:, t, :], in0=qk[:, t, :], scalar=cur[:, C1_SUB:C1_SUB + 1],
                            in1=bank[(1, 3)[c]][:, m * SEQ:(m + 1) * SEQ], op0=ALU.mult, op1=ALU.mult))
                    own.wait()
                    dve.sem_inc(bc_used.sem, 1)
                    dve.sem_inc(dn_ready.sem, 2)
                for p in range(4, 8):
                    if p + 1 < 8:
                        normalise(where, p + 1, l)
                    if p + 2 < 8:
                        logits(where, p + 2)
                    if p == 4:
                        for t in range(4):
                            dve.wait_ge(dn_hi.sem, dn_hi.at(where, t + 1))
                            last = lo_part(y_lo[:, t, :], t4[:, t, :], y_hi[:, t, :])
                        last.then_inc(y_ready.sem, 1)
                    att_low(where, p)
                    if p == 6:
                        split_lo(where, LAST_BEFORE_SKIP[1] + 1 + NS)

            def log_sigmoid_rest(f, dst, mul):
                e, ln, d, k = lgs[:, 1, :], lgs[:, 2, :], lgs[:, 3, :], lgs[:, 4, :]
                own.link(V.tensor_scalar(d, e, 1.0, -1.0, ALU.add, ALU.add))
                own.wait()
                own.link(V.tensor_scalar(k, d, 0.0, None, ALU.is_equal))
                own.wait()
                own.link(V.tensor_tensor(d, d, k, ALU.add))
                own.wait()
                own.link(V.reciprocal(d, d))
                own.wait()
                own.link(V.tensor_tensor(d, d, ln, ALU.mult))
                own.wait()
                own.link(V.tensor_tensor(d, d, k, ALU.add))
                own.wait()
                own.link(V.tensor_tensor(d, d, e, ALU.mult))
                own.wait()
                own.link(V.scalar_tensor_tensor(out=dst, in0=f, scalar=0.0, in1=d, op0=ALU.min, op1=ALU.subtract))
                own.wait()
                if mul is not None:
                    own.link(V.tensor_scalar(dst, dst, mul, None, ALU.mult))
                    own.wait()

            V.memset(first_gain[:, 2 * LAYERS, :], 1.0)
            V.memset(lgs[:, 7, :], 0.0).then_inc(lo_ready.sem, NS)
            for c, (s, k) in enumerate(((evacuated, 2), (gsq_used, 2), (bc_used, 2), (logits_ready, 1), (turned, 2),
                                        (pt_ready, 1), (pv_done, 1), (att_hi, 1), (att_out, 1))):
                dve.sem_inc(s.sem, k)
            for c in range(4):
                dve.wait_ge(pro_pe, c + 1)
                own.link(V.tensor_copy(x[:, 2 * c:2 * c + 2, :], bank[c][:, :].rearrange("p (m s) -> p m s", m=2)))
                own.wait()
                dve.sem_inc(x_ready.sem, 2)
                dve.sem_inc(pro_dve, 1)
            for vv in range(2):
                dve.wait_ge(hi_ready.sem, vv + 1)
                lo_part(w_lo[:, vv, :], raw[:, vv, :], w_hi[:, vv, :]).then_inc(lo_ready.sem, 1)
            for k, dst in enumerate((par1[:, :, 0:109], par1[:, :, 109:197], par2[:, :, 0:106], par2[:, :, 106:138])):
                dve.wait_ge(pro_pe, 5 + k)
                src = bank[4 + k][:, 0:2 * P].rearrange("p (l c) -> p l c", l=LAYERS)
                if k % 2 == 0:
                    col = (C1_ATTN, C2_FFN1)[k // 2]
                    V.tensor_copy(first_gain[:, k:k + 2, :], src[:, :, col:col + KT])
                V.tensor_copy(dst, src[:, :, 0:PAR_ROWS[k]]).then_inc(pro_dve, 1)
                if k == 0:
                    dve.wait_ge(pro_dve, 5)
                    raw_low((1, 0), 0, range(KT), lambda t: first_gain[:, 0, t:t + 1])
            dve.wait_ge(hi_ready.sem, 3)
            lo_part(w_lo[:, 2, :], raw[:, 2, :], w_hi[:, 2, :]).then_inc(lo_ready.sem, 1)
            dve.wait_ge(pro_dve, 8)
            own.link(V.memset(tsb[:, 0:P - 1], NEG))
            dve.wait_ge(pro_pe, 9)
            V.tensor_copy(tsb[:, P - 1:384], bank[3][0:BIAS_HEADS, P - 1:384]).then_inc(pro_dve, 1)
            for l in range(LAYERS):
                for col, by in ((C1_QK, HD1 ** -0.5), (C1_QK + 2, HD1 ** -0.5), (C1_SUB, 1.0 - LAM_INIT[l])):
                    own.link(V.tensor_scalar(par1[:, l, col:col + 1], par1[:, l, col:col + 1], by, None, ALU.mult))
                own.link(V.tensor_scalar(par2[:, l, C2_QN:C2_QN + 1], par2[:, l, C2_QN:C2_QN + 1], HD2 ** -0.5, None,
                                         ALU.mult))
            dve.wait_ge(ld_wf, 16 * (1 + LAYERS * (TB + 1)))
            dve.wait_ge(pro_act, 1)
            lo_part(wf_lo[:, :, :, :].rearrange("p l k h -> p (l k h)"),
                    wf_raw[:, :, :, :].rearrange("p l k h -> p (l k h)"),
                    wf_hi[:, :, :, :].rearrange("p l k h -> p (l k h)"))
            pairs = dlam.rearrange("p (n e d) -> p n e d", n=4, e=2)
            own.link(V.tensor_tensor(dprod, pairs[:, :, 0, :], pairs[:, :, 1, :], ALU.mult))
            own.wait()
            V.tensor_reduce(lgs[:, 7, 0:4], dprod, AX_X, ALU.add).then_inc(pro_dve, 1)
            lam2 = lgs[:, 6, :].rearrange("p (l t) -> p l t", l=LAYERS)
            own.link(V.tensor_copy(lam2, par2[:, :, C2_LAM:C2_LAM + KT]))
            own.wait()
            V.scalar_tensor_tensor(out=lgs[:, 0, :], in0=lgs[:, 6, :], scalar=-1.0, in1=lgs[:, 6, :], op0=ALU.mult,
                                   op1=ALU.min).then_inc(pro_dve, 1)
            dve.wait_ge(pro_act, 2)
            e4 = lgs[:, 7, 4:8].rearrange("p (l e) -> p l e", l=LAYERS)
            own.link(V.tensor_tensor(neglam[:, :], e4[:, :, 1], e4[:, :, 0], ALU.subtract))
            own.wait()
            for l in range(LAYERS):
                own.link(V.tensor_scalar(neglam[:, l:l + 1], neglam[:, l:l + 1], -LAM_INIT[l], None, ALU.add))
            dve.wait_ge(pro_act, 3)
            log_sigmoid_rest(lgs[:, 6, :], lgs[:, 5, :], LRU_C)
            c5 = lgs[:, 5, :].rearrange("p (l t) -> p l t", l=LAYERS)
            own.link(V.tensor_copy(par2[:, :, C2_LAM:C2_LAM + KT], c5))
            own.link(V.tensor_scalar(par2[:, :, C2_POS:C2_POS + KT], c5, -1.0, None, ALU.mult))
            reciprocal_deviation((1, 0), 0)
            own.restart()

            with dve.Fori(0, LAYERS) as l:
                where = (1, l)
                own.link(V.tensor_copy(cur[:, :], par1[:, bass.ds(l, 1), :].rearrange("p l c -> p (l c)")))
                own.wait()
                dve.sem_inc(cur_ready.sem, 1)
                norm(where, 0, C1_ATTN, V1_WIN, qk[:, 0:2, :])
                for u in range(12):
                    if u == 1:
                        normed(where, 0, 1, V1_WIN, qk[:, 2:4, :])
                    if u != 7:
                        next_lo(where, V1_WIN + u)
                    if u == 5:
                        group_rstd(where, 0)
                    if 6 <= u <= 7:
                        group_apply(where, 2 * u - 12, (u - 6, u - 4), 0, (C1_QK, C1_QK + 1), (6, 7))
                    if u == 10:
                        group_rstd(where, 1)
                    if u == 7:
                        dve.wait_ge(ld_bias, 16)
                    if 7 <= u <= 10:
                        logits(where, u - 7)
                        normalise(where, u - 7, l)
                    if u == 7:
                        next_lo(where, V1_WIN + u)
                group_apply(where, 4, (0, 2, 1, 3), 8, (C1_QK + 2, C1_QK + 3), (3, 7))
                rest_of_attention(where, l)
                split_lo(where, LAST_BEFORE_SKIP[1] + 2 + NS)
                out_phase(where, V1_WOUT, 1, C1_FFN)
                norm(where, 1, C1_FFN, V1_FFN, gate_n, False)
                ffn(where, V1_FFN, lambda vv, step, i, last: ffn1_step(where, vv, step, i), 0, 1.0, 2,
                    lambda t: gain_of(l + 1, t))
                own.restart()

            V.memset(lin_a, 0.0).then_inc(lin_cleared, 1)
            V.memset(lin_x, 0.0).then_inc(lin_cleared, 1)
            with dve.Fori(0, LAYERS) as l:
                where = (2, l)
                own.link(V.tensor_copy(cur[:, 0:C2], par2[:, bass.ds(l, 1), :].rearrange("p l c -> p (l c)")))
                own.wait()
                dve.sem_inc(cur_ready.sem, 1)
                norm(where, 0, C2_FFN1, V2_FFN1, gate_n, False)
                ffn(where, V2_FFN1, lambda vv, step, i, last: ffn2_step(where, vv, step, 0, i), 0, 0.5, 1,
                    lambda t: cur[:, C2_MIX + t:C2_MIX + t + 1])
                norm(where, 1, C2_MIX, V2_WIN, lru_x)

                def lru_input(j):
                    o = O2_WIN + 3 * j
                    src = lru_x
                    if j:
                        src = bank[o % 2][:, :].rearrange("p (m s) -> p m s", m=2)
                        dve.wait_ge(evacuated.sem, evacuated.at(where, o))
                    for m in range(2):
                        t = 2 * j + m
                        own.link(V.tensor_scalar(lru_x[:, m, :], src[:, m, :],
                                                 cur[:, C2_BREST + t:C2_BREST + t + 1], None, ALU.add))
                    own.wait()
                    if j:
                        dve.sem_inc(evacuated.sem, 1)

                def lru_taps(j):
                    ks = []
                    for m in range(2):
                        t = 2 * j + m
                        ks.append(own.link(V.tensor_scalar(
                            lru_c[:, m, :], lru_x[:, m, :], cur[:, C2_CONV + 24 + t:C2_CONV + 25 + t],
                            cur[:, C2_CB + t:C2_CB + t + 1], ALU.mult, ALU.add)))
                    for tap in (1, 2, 3):
                        for m in range(2):
                            own.wait(ks[-2])
                            cc = C2_CONV + (3 - tap) * KT + 2 * j + m
                            ks.append(own.link(V.scalar_tensor_tensor(
                                out=lru_c[:, m, tap:SEQ], in0=lru_x[:, m, 0:SEQ - tap], scalar=cur[:, cc:cc + 1],
                                in1=lru_c[:, m, tap:SEQ], op0=ALU.mult, op1=ALU.add)))
                    own.wait()
                    dve.sem_inc(lru_conv.sem, 1)

                def lru_gains(j):
                    dve.wait_ge(lru_gates.sem, lru_gates.at(where, j + 1))
                    own.link(V.tensor_tensor(lru_i, lru_i, lru_c, ALU.mult))
                    own.link(V.scalar_tensor_tensor(out=lru_r, in0=lru_r, scalar=1.0, in1=lru_t, op0=ALU.add,
                                                    op1=ALU.mult))
                    own.wait()
                    dve.sem_inc(lru_m.sem, 1)

                def lru_scan(j):
                    dve.wait_ge(lru_sqrt.sem, lru_sqrt.at(where, j + 1))
                    own.link(V.tensor_tensor(lru_i, lru_i, lru_r, ALU.mult))
                    own.wait()
                    for m in range(2):
                        own.link(V.tensor_tensor_scan(lru_r[:, m, :], lru_a[:, m, :], lru_i[:, m, :], 0.0, ALU.mult,
                                                      ALU.add))
                    own.wait()
                    own.link(V.tensor_tensor(lru_r, lru_r, lru_g, ALU.mult))
                    own.wait()
                    dve.sem_inc(lru_y.sem, 1)

                def lru_low(j):
                    dve.wait_ge(lru_hi.sem, lru_hi.at(where, j + 1))
                    lo_part(r_lo[:, 2 * j:2 * j + 2, :], lru_r, r_hi[:, 2 * j:2 * j + 2, :]).then_inc(r_ready.sem, 1)

                for j in range(4):
                    vv = V2_WIN + 3 * j
                    if j:
                        unit_wait(where, vv)
                    lru_input(j)
                    if j:
                        lru_gains(j - 1)
                    next_lo(where, vv)
                    if j:
                        lru_scan(j - 1)
                    lru_taps(j)
                    if j == 0:
                        normed(where, 1, 1, vv, lru_g)
                    next_lo(where, vv + 1)
                    if j:
                        lru_low(j - 1)
                    next_lo(where, vv + 2)
                lru_gains(3)
                for j in range(4):
                    next_lo(where, V2_WIN + 12 + j)
                    if j == 0:
                        lru_scan(3)
                        dve.wait_ge(f_done.sem, f_done.at(where, 1))
                        own.link(V.tensor_tensor(lgs[:, 6, :], bank[2][:, 0:16],
                                                 bf[:, bass.ds(l, 1), :].rearrange("p l h -> p (l h)"), ALU.add))
                        own.wait()
                        V.scalar_tensor_tensor(out=lgs[:, 0, :], in0=lgs[:, 6, :], scalar=-1.0, in1=lgs[:, 6, :],
                                               op0=ALU.mult, op1=ALU.min).then_inc(f_abs.sem, 1)
                        group_rstd(where, 0)
                    if j == 1:
                        lru_low(3)
                        dve.wait_ge(f_exp.sem, f_exp.at(where, 1))
                        log_sigmoid_rest(lgs[:, 6, :], lf[:, :], None)
                        dve.sem_inc(f_ready.sem, 1)
                    if j >= 2:
                        group_apply(where, 2 * j - 4, (2 * j - 4, 2 * j - 3), 0, (C2_QN, C2_QN), (6, 7))
                for j in range(4):
                    vv, o = V2_WIN + 16 + j, O2_WIN + 16 + j
                    unit_wait(where, vv)
                    if j == 0:
                        dve.wait_ge(side_loaded.sem, l * 80 + 80)
                        dve.wait_ge(evacuated.sem, evacuated.at(where, o))
                    for t in range(TB):
                        last = V.tensor_tensor(v[:, t, UW * j:UW * (j + 1)], bank[o % 2][:, t * UW:(t + 1) * UW],
                                               bv[:, UW * j:UW * (j + 1)], ALU.add)
                    last.then_inc(evacuated.sem, 1)
                    next_lo(where, vv)
                    if j == 0:
                        group_rstd(where, 1)
                    if 1 <= j <= 2:
                        group_apply(where, 2 + 2 * j, (2 * j - 2, 2 * j - 1), 8, (C2_KN, C2_KN), (6, 7))
                    if j >= 2:
                        logits(where, j - 2)
                        normalise(where, j - 2, l)
                skipped = LAST_BEFORE_SKIP[2] + 1 + NS
                split_lo(where, skipped)
                for j in range(8):
                    vv = V2_GATED + 2 * j
                    if j == 0:
                        split_lo(where, skipped + 1)
                    if j < 2:
                        att_low(where, 2 * j)
                    if j == 0:
                        logits(where, 2)
                        normalise(where, 2, l)
                    next_lo(where, vv)
                    unit_wait(where, vv + 1)
                    dve.wait_ge(sig_ready.sem, sig_ready.at(where, j + 1))
                    two = bank[1][:, :].rearrange("p (m s) -> p m s", m=2)
                    tiles = qk[:, 2 * (j % 4):2 * (j % 4) + 2, :]
                    if j < 4:
                        own.link(V.tensor_tensor(tiles, sig_s, two, ALU.mult))
                        own.wait()
                        dve.sem_inc(evacuated.sem, 1)
                        next_lo(where, vv + 1)
                        if j < 2:
                            att_low(where, 2 * j + 1)
                        if j == 0:
                            logits(where, 3)
                            normalise(where, 3, l)
                        if j == 1:
                            dve.wait_ge(att_out.sem, att_out.at(where, 4))
                            dve.sem_inc(y_ready.sem, 1)
                    else:
                        if j > 4:
                            dve.wait_ge(m_ready.sem, m_ready.at(where, j - 4))
                        own.link(V.tensor_tensor(part_s, sig_s, two, ALU.mult))
                        own.wait()
                        dve.sem_inc(evacuated.sem, 1)
                        own.link(V.tensor_tensor(part_s, part_s, tiles, ALU.add))
                        own.wait()
                        dve.sem_inc(merged_ready.sem, 1)
                        next_lo(where, vv + 1)
                        dve.wait_ge(merged_hi.sem, merged_hi.at(where, j - 3))
                        rs = slice(2 * j - 8, 2 * j - 6)
                        lo_part(r_lo[:, rs, :], part_s, r_hi[:, rs, :]).then_inc(m_ready.sem, 1)
                out_phase(where, V2_WOUT, 2, C2_FFN2)
                norm(where, 2, C2_FFN2, V2_FFN2, gate_n, False)
                own.restart()
                ffn(where, V2_FFN2, lambda vv, step, i, last: ffn2_step(where, vv, step, STEPS, i, last), 1, 0.5, 3,
                    lambda t: gain_of(l + 3, t), l)
                own.restart()


def PAR(step):
    return step % 2


PAR_ROWS = [109, 88, 106, 32]
PAR_DMAS = [7, 1, 11, 1]


def param_loads(a, prow):
    def rows(vec):
        return vec.rearrange("l (t p) -> t l p", p=P)

    def one(vec):
        return vec.rearrange("(o l) p -> o l p", o=1)

    def to(kind, r0, n):
        return kind, prow[r0:r0 + n, kind, :, :]

    b, qk_g = a["b_in_2"], a["qk_norm_g"].rearrange("l n d -> n l d")
    kinds = [
        (*to(0, C1_ATTN, 8), rows(a["ln_attn_g"])), (*to(0, C1_FFN, 8), rows(a["ln_ffn_g"])),
        (*to(0, C1_SUB, 1), one(a["diff_subln_g"])),
        (0, prow[C1_QK:C1_QK + 4, 0, :, 0:64], qk_g), (0, prow[C1_QK:C1_QK + 4, 0, :, 64:128], qk_g),
        (*to(0, 21, FT * 2), rows(a["conv_b"])), (*to(0, 65, FT * 2), rows(a["conv_w"][:, 2])),
        (*to(1, 0, FT * 4), a["conv_w"][:, 0:2].rearrange("l k (t p) -> (k t) l p", p=P)),
        (*to(2, 0, 8), rows(a["ffn1_norm_2"])), (*to(2, 8, 8), rows(a["mix_norm_2"])),
        (*to(2, 16, 8), rows(a["ffn2_norm_2"])), (*to(2, 24, 16), rows(b[:, 0:2 * D])),
        (*to(2, 40, 32), rows(b[:, REST2:REST2 + 4 * D])),
        (*to(2, 72, 1), one(a["q_norm_2"])), (*to(2, 73, 1), one(a["k_norm_2"])),
        (*to(2, 74, 8), rows(a["conv_b_2"])), (*to(2, 82, 8), rows(a["lru_b_a_2"])),
        (*to(2, 90, 8), rows(a["lru_b_x_2"])), (*to(2, 98, 8), rows(a["lru_lambda_2"])),
        (*to(3, 0, 32), a["conv_w_2"].rearrange("l k (t p) -> (k t) l p", p=P))]
    assert [sum(k == kind for k, _, _ in kinds) for kind in range(4)] == PAR_DMAS
    return kinds


_INS = ['x', 'ln_attn_g', 'w_in', 'qk_norm_g', 'diff_lambda', 'diff_subln_g', 'w_out', 'ln_ffn_g', 'w_up', 'conv_w',
        'conv_b', 'w_down', 'rel_bias', 'ffn1_norm_2', 'ffn1_w_gate_2', 'ffn1_w_up_2', 'ffn1_w_down_2', 'mix_norm_2',
        'w_in_2', 'b_in_2', 'q_norm_2', 'k_norm_2', 'conv_w_2', 'conv_b_2', 'lru_w_a_2', 'lru_b_a_2', 'lru_w_x_2',
        'lru_b_x_2', 'lru_lambda_2', 'w_o_attn_2', 'w_o_rnn_2', 'w_out_2', 'ffn2_norm_2', 'ffn2_w_gate_2',
        'ffn2_w_up_2', 'ffn2_w_down_2']


def shape_constants():
    import numpy as np
    j, k = np.arange(P)[:, None], np.arange(P)[None, :]
    c = np.zeros((P, K_N), np.float32)
    c[:, K_ID:K_ID + P] = j == k
    c[:, K_TRI:K_TRI + P] = j <= k
    c[:, K_ONEU:K_ONEU + P] = 1.0
    c[:, K_ONEU + P:K_ONEU + 2 * P] = j > k
    c[:, K_MASK + P:K_MASK + 2 * P] = np.where(k <= j, 0.0, NEG)
    sp = np.zeros((16, KT, P), np.float32)
    for t in range(KT):
        c[:64, K_G64 + 16 * t + 2 * t] = 1.0 / 64
        c[64:, K_G64 + 16 * t + 2 * t + 1] = 1.0 / 64
        c[:, K_G128 + 16 * t + 2 * t:K_G128 + 16 * t + 2 * t + 2] = 1.0 / 128
        sp[2 * t, t, :64] = 1.0
        sp[2 * t + 1, t, 64:] = 1.0
    c[:, K_MEAN:K_MEAN + P] = 1.0 / D
    dist = np.arange(SEQ)
    exact = BUCKETS // 2
    far = np.maximum(dist, exact).astype(np.float32) / np.float32(exact)
    far = exact + (np.log(far) / np.float32(math.log(1024 / exact)) * np.float32(BUCKETS - exact)).astype(np.int32)
    bucket = np.where(dist < exact, dist, np.minimum(far, BUCKETS - 1))
    onehot = np.zeros((BUCKETS, 384), np.float32)
    onehot[bucket, P - 1 + dist] = 1.0
    return {"const_main": c, "const_spread": sp.reshape(16, KT * P), "const_onehot": onehot}


def kernel(**inputs):
    import numpy as np
    import concourse.bacc as bacc
    from concourse.bass_utils import run_bass_kernel_spmd

    nc = bacc.Bacc("TRN2", target_bir_lowering=False, num_devices=1)
    arrays, aps = {}, {}
    for name, value in [(n, inputs[n]) for n in _INS] + list(shape_constants().items()):
        value = np.ascontiguousarray(value)
        arrays[f"in_{name}"] = value
        aps[name] = nc.dram_tensor(f"in_{name}", value.shape, mybir.dt.from_np(value.dtype), kind="ExternalInput").ap()
    out = nc.dram_tensor("out_0", (1, SEQ, D), F32, kind="ExternalOutput").ap()
    build_program(nc, aps, out)
    r = run_bass_kernel_spmd(nc, [arrays], core_ids=[0])
    return r.results[0]["out_0"]
```
